# Optimizing a Trainium2 kernel written in Bass

```python
import math
import jax, jax.numpy as jnp
from jax import lax
import numpy as np
import jax
import jax.numpy as jnp

D_MODEL = 1024
BATCH = 1
SEQ = 256
DEPTH = 2

N_MIXERS = 2
N_RET = (DEPTH + 1) // 2
N_LRU = DEPTH // 2

RET_HEADS = D_MODEL // 256
RET_DK = 256
RET_DV = 2 * RET_DK
RET_QK_W = RET_HEADS * RET_DK
RET_V_W = RET_HEADS * RET_DV
RET_CHUNK = 128
ROPE_BASE = 10000.0

LRU_WIDTH = 1536
LRU_BLOCK = 256
LRU_BLOCKS = LRU_WIDTH // LRU_BLOCK
LRU_CONV = 4
LRU_C = 8.0

D_FF = ((8 * D_MODEL // 3 + 255) // 256) * 256

NORM_EPS = 1e-6


def rms_norm(x, g):
    xf = x.astype(jnp.float32)
    y = xf * lax.rsqrt(jnp.mean(xf * xf, axis=-1, keepdims=True) + NORM_EPS)
    return (y * g.astype(jnp.float32)).astype(x.dtype)

def rope(x, pos):
    half = x.shape[-1] // 2
    inv = 1.0 / (ROPE_BASE ** (jnp.arange(half, dtype=jnp.float32) / half))
    ang = pos.astype(jnp.float32)[:, None] * inv[None, :]
    cos = jnp.cos(ang)[None, :, None, :]
    sin = jnp.sin(ang)[None, :, None, :]
    x1, x2 = x[..., :half], x[..., half:]
    return jnp.concatenate([x1 * cos - x2 * sin, x1 * sin + x2 * cos], axis=-1)

def retention_mixer(x, w_in, w_out):
    B, S, _ = x.shape
    H, DK, DV, C = RET_HEADS, RET_DK, RET_DV, RET_CHUNK
    N = S // C
    proj = x @ w_in
    q, k, v, g = jnp.split(proj, [RET_QK_W, 2 * RET_QK_W, 2 * RET_QK_W + RET_V_W], axis=-1)
    pos = jnp.arange(S)
    q = rope(q.reshape(B, S, H, DK).astype(jnp.float32), pos)
    k = rope(k.reshape(B, S, H, DK).astype(jnp.float32), pos) * (DK ** -0.5)
    v = v.reshape(B, S, H, DV).astype(jnp.float32)

    log_gamma = jnp.log1p(-jnp.exp2(-5.0 - jnp.arange(H, dtype=jnp.float32)))
    idx = jnp.arange(C, dtype=jnp.float32)
    rel = idx[:, None] - idx[None, :]
    causal = rel >= 0
    decay = jnp.where(causal[None],
                      jnp.exp(jnp.where(causal, rel, 0.0)[None] * log_gamma[:, None, None]),
                      0.0)
    q_decay = jnp.exp((idx[:, None] + 1.0) * log_gamma[None, :])
    k_decay = jnp.exp((C - 1.0 - idx[:, None]) * log_gamma[None, :])
    chunk_decay = jnp.exp(C * log_gamma)

    qc = q.reshape(B, N, C, H, DK)
    kc = k.reshape(B, N, C, H, DK)
    vc = v.reshape(B, N, C, H, DV)

    scores = jnp.einsum('bnqhd,bnkhd->bnhqk', qc, kc) * decay[None, None]
    intra = jnp.einsum('bnhqk,bnkhe->bnqhe', scores, vc)

    def step(state, inp):
        qi, ki, vi = inp
        out = jnp.einsum('bchd,bhde->bche', qi, state) * q_decay[None, :, :, None]
        state = state * chunk_decay[None, :, None, None] + jnp.einsum(
            'bchd,bche->bhde', ki * k_decay[None, :, :, None], vi)
        return state, out

    state0 = jnp.zeros((B, H, DK, DV), jnp.float32)
    _, inter = lax.scan(step, state0, (qc.transpose(1, 0, 2, 3, 4),
                                       kc.transpose(1, 0, 2, 3, 4),
                                       vc.transpose(1, 0, 2, 3, 4)))
    o = (intra + inter.transpose(1, 0, 2, 3, 4)).reshape(B, S, H, DV)

    mu = jnp.mean(o, axis=-1, keepdims=True)
    oc = o - mu
    o = oc * lax.rsqrt(jnp.mean(oc * oc, axis=-1, keepdims=True) + NORM_EPS)
    o = o.reshape(B, S, RET_V_W).astype(x.dtype) * jax.nn.silu(g)
    return o @ w_out

def rglru_mixer(x, w_in, conv_w, conv_b, gate_w, gate_b, a_param, w_out):
    B, S, _ = x.shape
    proj = x @ w_in
    y_branch, u = jnp.split(proj, 2, axis=-1)
    y_branch = jax.nn.gelu(y_branch, approximate=True)

    u = lax.conv_general_dilated(
        u, conv_w[:, None, :], window_strides=(1,), padding=[(LRU_CONV - 1, 0)],
        dimension_numbers=('NWC', 'WIO', 'NWC'), feature_group_count=LRU_WIDTH) + conv_b

    ub = u.reshape(B, S, LRU_BLOCKS, LRU_BLOCK)
    gates = jnp.einsum('bsnk,gnkj->gbsnj', ub, gate_w) + gate_b[:, None, None]
    gates = jax.nn.sigmoid(gates.astype(jnp.float32)).reshape(2, B, S, LRU_WIDTH)
    r, i = gates[0], gates[1]

    log_a = -LRU_C * r * jax.nn.softplus(-a_param.astype(jnp.float32))
    a = jnp.exp(log_a)
    mult = jnp.sqrt(-jnp.expm1(2.0 * log_a))
    b = mult * (i * u.astype(jnp.float32))

    def combine(lhs, rhs):
        a1, b1 = lhs
        a2, b2 = rhs
        return a1 * a2, a2 * b1 + b2

    _, h = lax.associative_scan(combine, (a, b), axis=1)
    return (h.astype(x.dtype) * y_branch) @ w_out

def swiglu_ffn(x, w_in, w_out):
    gate, up = jnp.split(x @ w_in, 2, axis=-1)
    return (jax.nn.silu(gate) * up) @ w_out

def first_inputs(seed: int = 0) -> dict:
    key = jax.random.key(seed)
    ks = jax.random.split(key, 16)
    f32 = jnp.float32

    def normal(k, shape, fan_in):
        return jax.random.normal(k, shape, f32) * (fan_in ** -0.5)

    x = jax.random.normal(ks[0], (BATCH, SEQ, D_MODEL), f32)
    ret_w_in = normal(ks[1], (N_RET, D_MODEL, 2 * RET_QK_W + 2 * RET_V_W), D_MODEL)
    ret_w_out = normal(ks[2], (N_RET, RET_V_W, D_MODEL), RET_V_W)
    lru_w_in = normal(ks[3], (N_LRU, D_MODEL, 2 * LRU_WIDTH), D_MODEL)
    lru_conv_w = normal(ks[4], (N_LRU, LRU_CONV, LRU_WIDTH), LRU_CONV)
    lru_conv_b = 0.01 * jax.random.normal(ks[5], (N_LRU, LRU_WIDTH), f32)
    lru_gate_w = normal(ks[6], (N_LRU, 2, LRU_BLOCKS, LRU_BLOCK, LRU_BLOCK), LRU_BLOCK)
    lru_gate_b = 0.01 * jax.random.normal(ks[7], (N_LRU, 2, LRU_BLOCKS, LRU_BLOCK), f32)
    a0 = jax.random.uniform(ks[8], (N_LRU, LRU_WIDTH), f32, minval=0.9, maxval=0.999)
    lru_a_param = jnp.log(a0) - jnp.log1p(-a0)
    lru_w_out = normal(ks[9], (N_LRU, LRU_WIDTH, D_MODEL), LRU_WIDTH)
    norm_g = 1.0 + 0.02 * jax.random.normal(ks[10], (DEPTH, 4, D_MODEL), f32)
    ffn_w_in = normal(ks[11], (DEPTH, D_MODEL, 2 * D_FF), D_MODEL)
    ffn_w_out = normal(ks[12], (DEPTH, D_FF, D_MODEL), D_FF)
    return {"x": x, "ret_w_in": ret_w_in, "ret_w_out": ret_w_out,
            "lru_w_in": lru_w_in, "lru_conv_w": lru_conv_w, "lru_conv_b": lru_conv_b,
            "lru_gate_w": lru_gate_w, "lru_gate_b": lru_gate_b, "lru_a_param": lru_a_param,
            "lru_w_out": lru_w_out, "norm_g": norm_g,
            "ffn_w_in": ffn_w_in, "ffn_w_out": ffn_w_out}

def first_block(x, ret_w_in, ret_w_out, lru_w_in, lru_conv_w, lru_conv_b, lru_gate_w,
              lru_gate_b, lru_a_param, lru_w_out, norm_g, ffn_w_in, ffn_w_out):
    for layer in range(DEPTH):
        j = layer // N_MIXERS
        h = rms_norm(x, norm_g[layer, 0])
        if layer % N_MIXERS == 0:
            m = retention_mixer(h, ret_w_in[j], ret_w_out[j])
        else:
            m = rglru_mixer(h, lru_w_in[j], lru_conv_w[j], lru_conv_b[j], lru_gate_w[j],
                            lru_gate_b[j], lru_a_param[j], lru_w_out[j])
        x = x + rms_norm(m, norm_g[layer, 1])
        f = swiglu_ffn(rms_norm(x, norm_g[layer, 2]), ffn_w_in[layer], ffn_w_out[layer])
        x = x + rms_norm(f, norm_g[layer, 3])
    return x


DEPTH_2 = 1

GRID_W = 64
CTX_LEN = 256
D_MIX = D_MODEL
HEAD_DIM = 64
RW_W = D_MIX // 4
RW_H = RW_W // HEAD_DIM
RW_DH = HEAD_DIM
RW_LW = 64
RW_LA = 64
RW_LG = 128
NA_W = D_MIX // 2
NA_H = NA_W // HEAD_DIM
NA_KR = 8
NA_KC = 16
SC_W = D_MIX - RW_W - NA_W
SC_K = 3
PEER_H = 8
PEER_NKEYS = 128
PEER_N = PEER_NKEYS * PEER_NKEYS
PEER_DQ = 256
PEER_TOPK = 16
PEER_CHUNK = 128

GN_EPS = 64e-5
NEG_INF = -1e30
IN_SPLITS = (RW_W, RW_W, RW_W, 2 * RW_LW, 2 * RW_LA, RW_LG, NA_W, NA_W, NA_W, SC_W, SC_W, SC_W)
D_IN = sum(IN_SPLITS)


def rmsnorm(x, g):
    xf = x.astype(jnp.float32)
    y = xf * lax.rsqrt(jnp.mean(xf * xf, axis=-1, keepdims=True) + NORM_EPS)
    return (y * g.astype(jnp.float32)).astype(x.dtype)

def split_columns(z):
    offsets = [int(o) for o in np.cumsum(IN_SPLITS)[:-1]]
    return jnp.split(z, offsets, axis=-1)

def short_conv3(u, w):
    up = jnp.pad(u, ((0, 0), (1, 1), (0, 0)))
    return up[:, :-2] * w[0] + up[:, 1:-1] * w[1] + up[:, 2:] * w[2]

def gated_short_conv(z_b, z_c, z_x, w):
    return z_b * short_conv3(z_c * z_x, w)

def rwkv_prepare(z_r, z_k, z_v, z_w, z_a, w0, w_up, a0, a_up, k_k, k_a):
    f32 = jnp.float32
    B, T, _ = z_r.shape
    r, k, v = z_r.astype(f32), z_k.astype(f32), z_v.astype(f32)
    lw = jnp.tanh(z_w.astype(f32).reshape(B, T, 2, RW_LW))
    la = z_a.astype(f32).reshape(B, T, 2, RW_LA)
    w_raw = w0 + jnp.einsum('btdr,drc->btdc', lw, w_up)
    decay = jnp.exp(-jnp.exp(-jax.nn.softplus(-w_raw) - 0.5))
    a = jax.nn.sigmoid(a0 + jnp.einsum('btdr,drc->btdc', la, a_up))
    kk = (k * k_k).reshape(B, T, RW_H, RW_DH)
    kk = (kk * lax.rsqrt(jnp.sum(kk * kk, axis=-1, keepdims=True) + 1e-12)).reshape(B, T, RW_W)
    k_dir = k[:, :, None, :] * (1.0 + (a - 1.0) * k_a)
    b_dir = kk[:, :, None, :] * a
    tm = lambda t: jnp.moveaxis(t.reshape(B, T, RW_H, RW_DH), 1, 0)
    common = (tm(r), tm(kk), tm(v))
    per_dir = tuple((tm(decay[:, :, d]), tm(b_dir[:, :, d]), tm(k_dir[:, :, d])) for d in range(2))
    return common, per_dir

def wkv_scan(state0, r, kk, v, decay, b, k, reverse):
    def step(S, inp):
        r_t, kk_t, v_t, w_t, b_t, k_t = inp
        sa = jnp.einsum('bhij,bhj->bhi', S, kk_t)
        S = S * w_t[:, :, None, :] - sa[..., None] * b_t[:, :, None, :] + v_t[..., None] * k_t[:, :, None, :]
        return S, jnp.einsum('bhij,bhj->bhi', S, r_t)
    return lax.scan(step, state0, (r, kk, v, decay, b, k), reverse=reverse)

def rwkv_output(y_tm, z_r, z_k, z_v, z_g, g_up, r_k, lnx_g):
    f32 = jnp.float32
    B, T, _ = z_r.shape
    y = jnp.moveaxis(y_tm, 0, 1)
    mu = jnp.mean(y, axis=-1, keepdims=True)
    var = jnp.mean(jnp.square(y - mu), axis=-1, keepdims=True)
    y = (y - mu) * lax.rsqrt(var + GN_EPS) * lnx_g.astype(f32).reshape(RW_H, RW_DH)
    hd = lambda t: t.astype(f32).reshape(B, T, RW_H, RW_DH)
    r, k, v = hd(z_r), hd(z_k), hd(z_v)
    y = y + jnp.sum(r * k * r_k, axis=-1, keepdims=True) * v
    gate = jax.nn.sigmoid(z_g.astype(f32)) @ g_up.astype(f32)
    return (y.reshape(B, T, RW_W) * gate).astype(z_r.dtype)

def rwkv_mixer(pc, pl, w0, w_up, a0, a_up, g_up, k_k, k_a, r_k, lnx_g, need_ctx):
    c_common, c_dirs = rwkv_prepare(*pc[:5], w0, w_up, a0, a_up, k_k, k_a)
    l_common, l_dirs = rwkv_prepare(*pl[:5], w0, w_up, a0, a_up, k_k, k_a)
    state0 = jnp.zeros((pl[0].shape[0], RW_H, RW_DH, RW_DH), jnp.float32)
    ys_c, ys_l = [], []
    for d, reverse in enumerate((False, True)):
        ctx_state, y_c = wkv_scan(state0, *c_common, *c_dirs[d], reverse=reverse)
        _, y_l = wkv_scan(ctx_state, *l_common, *l_dirs[d], reverse=reverse)
        ys_c.append(y_c)
        ys_l.append(y_l)
    out_l = rwkv_output(ys_l[0] + ys_l[1], pl[0], pl[1], pl[2], pl[5], g_up, r_k, lnx_g)
    out_c = rwkv_output(ys_c[0] + ys_c[1], pc[0], pc[1], pc[2], pc[5], g_up, r_k, lnx_g) if need_ctx else None
    return out_c, out_l

def neighbourhood_attention(ql, kl, vl, kc, vc, rpb):
    f32 = jnp.float32
    B, S = ql.shape[:2]
    rows = S // GRID_W
    kr = min(NA_KR, rows)
    scale = HEAD_DIM ** -0.5
    grid = lambda t: t.reshape(B, rows, GRID_W, NA_H, HEAD_DIM)
    qg = grid(ql).astype(f32) * scale
    kg, vg = grid(kl).astype(f32), grid(vl)
    ri = jnp.arange(rows)
    row_idx = jnp.clip(ri - kr // 2, 0, rows - kr)[:, None] + jnp.arange(kr)[None, :]
    ci = jnp.arange(GRID_W)
    c0 = jnp.clip(ci - NA_KC // 2, 0, GRID_W - NA_KC)
    col_ok = (ci[None, :] >= c0[:, None]) & (ci[None, :] < c0[:, None] + NA_KC)
    dr = row_idx - ri[:, None] + (NA_KR - 1)
    dc = jnp.clip(ci[None, :] - ci[:, None] + (NA_KC - 1), 0, 2 * NA_KC - 2)
    bias = rpb[:, dr[:, None, :, None], dc[None, :, None, :]].astype(f32)
    k_band = kg[:, row_idx]
    v_band = vg[:, row_idx]
    s_win = jnp.einsum('brqhd,brkwhd->bhrqkw', qg, k_band) + bias[None]
    s_win = jnp.where(col_ok[:, None, :], s_win, NEG_INF)
    s_ctx = jnp.einsum('brqhd,bnhd->bhrqn', qg, kc.astype(f32))
    n_win = kr * GRID_W
    s = jnp.concatenate([s_win.reshape(B, NA_H, rows, GRID_W, n_win), s_ctx], axis=-1)
    p = jax.nn.softmax(s, axis=-1)
    p_win = p[..., :n_win].reshape(B, NA_H, rows, GRID_W, kr, GRID_W).astype(vl.dtype)
    p_ctx = p[..., n_win:].astype(vl.dtype)
    out = jnp.einsum('bhrqkw,brkwhd->brqhd', p_win, v_band) + jnp.einsum('bhrqn,bnhd->brqhd', p_ctx, vc)
    return out.reshape(B, S, NA_W)

def context_attention(qc, kc, vc):
    f32 = jnp.float32
    B, C = qc.shape[:2]
    s = jnp.einsum('bqhd,bkhd->bhqk', qc.astype(f32), kc.astype(f32)) * (HEAD_DIM ** -0.5)
    p = jax.nn.softmax(s, axis=-1).astype(vc.dtype)
    return jnp.einsum('bhqk,bkhd->bqhd', p, vc).reshape(B, C, NA_W)

def token_mixing(hc, hl, w_in, w_out, rw_w0, rw_w_up, rw_a0, rw_a_up, rw_g_up, rw_k_k, rw_k_a,
                 rw_r_k, rw_lnx_g, na_rpb, sc_conv_w, need_ctx):
    B, S = hl.shape[:2]
    C = hc.shape[1]
    pc = split_columns(hc @ w_in)
    pl = split_columns(hl @ w_in)
    y_rw_c, y_rw_l = rwkv_mixer(pc, pl, rw_w0, rw_w_up, rw_a0, rw_a_up, rw_g_up, rw_k_k, rw_k_a,
                                rw_r_k, rw_lnx_g, need_ctx)
    qc, kc, vc = (t.reshape(B, C, NA_H, HEAD_DIM) for t in pc[6:9])
    ql, kl, vl = (t.reshape(B, S, NA_H, HEAD_DIM) for t in pl[6:9])
    y_na_l = neighbourhood_attention(ql, kl, vl, kc, vc, na_rpb)
    y_sc_l = gated_short_conv(*pl[9:12], sc_conv_w)
    yl = jnp.concatenate([y_rw_l, y_na_l, y_sc_l], axis=-1) @ w_out
    if not need_ctx:
        return None, yl
    y_na_c = context_attention(qc, kc, vc)
    y_sc_c = gated_short_conv(*pc[9:12], sc_conv_w)
    yc = jnp.concatenate([y_rw_c, y_na_c, y_sc_c], axis=-1) @ w_out
    return yc, yl

def peer_ffn(h, q_w, sub_keys, u_tab, v_tab):
    f32 = jnp.float32
    lead = h.shape[:-1]
    t = h.reshape(-1, D_MODEL)
    n = t.shape[0]
    q = (t @ q_w).reshape(n, PEER_H, 2, PEER_DQ // 2)
    s = jnp.einsum('thpd,hpnd->thpn', q.astype(f32), sub_keys.astype(f32))
    s1, i1 = lax.top_k(s[:, :, 0], PEER_TOPK)
    s2, i2 = lax.top_k(s[:, :, 1], PEER_TOPK)
    cand_s = (s1[..., :, None] + s2[..., None, :]).reshape(n, PEER_H, PEER_TOPK * PEER_TOPK)
    cand_i = (i1[..., :, None] * PEER_NKEYS + i2[..., None, :]).reshape(n, PEER_H, PEER_TOPK * PEER_TOPK)
    top_s, pos = lax.top_k(cand_s, PEER_TOPK)
    idx = jnp.take_along_axis(cand_i, pos, axis=-1)
    gates = jax.nn.softmax(top_s, axis=-1).astype(h.dtype)

    def chunk(args):
        x_c, i_c, g_c = args
        act = jax.nn.gelu(jnp.einsum('chkd,cd->chk', u_tab[i_c], x_c))
        return jnp.einsum('chk,chkd->cd', g_c * act, v_tab[i_c])

    nc = n // PEER_CHUNK
    out = lax.map(chunk, (t.reshape(nc, PEER_CHUNK, D_MODEL),
                          idx.reshape(nc, PEER_CHUNK, PEER_H, PEER_TOPK),
                          gates.reshape(nc, PEER_CHUNK, PEER_H, PEER_TOPK)))
    return out.reshape(lead + (D_MODEL,))

def second_inputs(seed: int = 0) -> dict:
    key = jax.random.key(seed)
    keys = iter(jax.random.split(key, 32))
    nrm = lambda shape, std: std * jax.random.normal(next(keys), shape, jnp.float32)
    L, D = DEPTH_2, D_MODEL
    return {
        'x': nrm((BATCH, SEQ, D), 1.0),
        'c': nrm((BATCH, D), 1.0),
        'ctx': nrm((BATCH, CTX_LEN, D), 1.0),
        'c_ctx': nrm((D,), 1.0),
        'ada_w': nrm((L, D, 6 * D), 0.5 * D ** -0.5),
        'ada_b': nrm((L, 6 * D), 0.02),
        'norm1_g': 1.0 + nrm((L, D), 0.02),
        'norm2_g': 1.0 + nrm((L, D), 0.02),
        'w_in': nrm((L, D, D_IN), D ** -0.5),
        'rw_w0': jnp.linspace(-5.0, 1.0, RW_W, dtype=jnp.float32) + nrm((L, 2, RW_W), 0.1),
        'rw_w_up': nrm((L, 2, RW_LW, RW_W), 0.5 * RW_LW ** -0.5),
        'rw_a0': nrm((L, 2, RW_W), 0.1),
        'rw_a_up': nrm((L, 2, RW_LA, RW_W), 0.5 * RW_LA ** -0.5),
        'rw_g_up': nrm((L, RW_LG, RW_W), RW_LG ** -0.5),
        'rw_k_k': 0.85 + nrm((L, RW_W), 0.05),
        'rw_k_a': 1.0 + nrm((L, RW_W), 0.05),
        'rw_r_k': nrm((L, RW_H, RW_DH), 0.1),
        'rw_lnx_g': 1.0 + nrm((L, RW_W), 0.02),
        'na_rpb': nrm((L, NA_H, 2 * NA_KR - 1, 2 * NA_KC - 1), 0.1),
        'sc_conv_w': nrm((L, SC_K, SC_W), SC_K ** -0.5),
        'w_out': nrm((L, D_MIX, D), D_MIX ** -0.5),
        'peer_q_w': nrm((L, D, PEER_H * PEER_DQ), D ** -0.5),
        'peer_sub_keys': nrm((L, PEER_H, 2, PEER_NKEYS, PEER_DQ // 2), (PEER_DQ // 2) ** -0.5),
        'peer_u': nrm((L, PEER_N, D), D ** -0.5),
        'peer_v': nrm((L, PEER_N, D), PEER_TOPK ** -0.5),
        'final_g': 1.0 + nrm((D,), 0.02),
    }

def second_block(x, c, ctx, c_ctx, ada_w, ada_b, norm1_g, norm2_g, w_in, rw_w0, rw_w_up, rw_a0,
              rw_a_up, rw_g_up, rw_k_k, rw_k_a, rw_r_k, rw_lnx_g, na_rpb, sc_conv_w, w_out,
              peer_q_w, peer_sub_keys, peer_u, peer_v, final_g):
    xl, xc = x, ctx
    for i in range(DEPTH_2):
        need_ctx = i < DEPTH_2 - 1
        mod_l = jax.nn.silu(c) @ ada_w[i] + ada_b[i]
        mod_c = jax.nn.silu(c_ctx) @ ada_w[i] + ada_b[i]
        sh1, sc1, g1, sh2, sc2, g2 = jnp.split(mod_l[:, None, :], 6, axis=-1)
        csh1, csc1, cg1, csh2, csc2, cg2 = jnp.split(mod_c, 6, axis=-1)
        hl = rmsnorm(xl, norm1_g[i]) * (1.0 + sc1) + sh1
        hc = rmsnorm(xc, norm1_g[i]) * (1.0 + csc1) + csh1
        yc, yl = token_mixing(hc, hl, w_in[i], w_out[i], rw_w0[i], rw_w_up[i], rw_a0[i], rw_a_up[i],
                              rw_g_up[i], rw_k_k[i], rw_k_a[i], rw_r_k[i], rw_lnx_g[i], na_rpb[i],
                              sc_conv_w[i], need_ctx)
        xl = xl + g1 * yl
        hl2 = rmsnorm(xl, norm2_g[i]) * (1.0 + sc2) + sh2
        xl = xl + g2 * peer_ffn(hl2, peer_q_w[i], peer_sub_keys[i], peer_u[i], peer_v[i])
        if need_ctx:
            xc = xc + cg1 * yc
            hc2 = rmsnorm(xc, norm2_g[i]) * (1.0 + csc2) + csh2
            xc = xc + cg2 * peer_ffn(hc2, peer_q_w[i], peer_sub_keys[i], peer_u[i], peer_v[i])
    return rmsnorm(xl, final_g)


def setup_inputs(seed=0):
    out = dict(first_inputs(seed))
    for name, value in second_inputs(seed + 1).items():
        if name != "x":
            out[name + "_2"] = value
    return out


def reference(
    x, ret_w_in, ret_w_out, lru_w_in, lru_conv_w, lru_conv_b, lru_gate_w, lru_gate_b,
    lru_a_param, lru_w_out, norm_g, ffn_w_in, ffn_w_out, c_2, ctx_2, c_ctx_2, ada_w_2, ada_b_2,
    norm1_g_2, norm2_g_2, w_in_2, rw_w0_2, rw_w_up_2, rw_a0_2, rw_a_up_2, rw_g_up_2, rw_k_k_2,
    rw_k_a_2, rw_r_k_2, rw_lnx_g_2, na_rpb_2, sc_conv_w_2, w_out_2, peer_q_w_2, peer_sub_keys_2,
    peer_u_2, peer_v_2, final_g_2,
):
    x = first_block(
        x, ret_w_in, ret_w_out, lru_w_in, lru_conv_w, lru_conv_b, lru_gate_w, lru_gate_b,
        lru_a_param, lru_w_out, norm_g, ffn_w_in, ffn_w_out,
    )
    return second_block(
        x, c_2, ctx_2, c_ctx_2, ada_w_2, ada_b_2, norm1_g_2, norm2_g_2, w_in_2, rw_w0_2,
        rw_w_up_2, rw_a0_2, rw_a_up_2, rw_g_up_2, rw_k_k_2, rw_k_a_2, rw_r_k_2, rw_lnx_g_2,
        na_rpb_2, sc_conv_w_2, w_out_2, peer_q_w_2, peer_sub_keys_2, peer_u_2, peer_v_2,
        final_g_2,
    )


_drawn_inputs = setup_inputs


def setup_inputs(seed=0):
    import zlib

    import numpy as np

    out = dict(_drawn_inputs(seed))
    spreads = {}
    factors = {'lru_gate_b': 8.0,
     'ctx_2': 4.643,
     'ada_b_2': 5.884,
     'norm1_g_2': 8.0,
     'norm2_g_2': 22.01,
     'rw_w_up_2': 64.0,
     'rw_a0_2': 200.0,
     'rw_a_up_2': 37.682,
     'rw_k_k_2': 200.0,
     'rw_k_a_2': 200.0,
     'rw_lnx_g_2': 200.0,
     'na_rpb_2': 200.0,
     'peer_q_w_2': 2.994,
     'peer_sub_keys_2': 3.002,
     'peer_u_2': 3.339,
     'peer_v_2': 2.968,
     'final_g_2': 22.529,
     'c_ctx_2': 2.94,
     'rw_w0_2': 8.0}
    for name, (base, spread) in spreads.items():
        noise = np.random.default_rng([zlib.crc32(name.encode()), seed]).standard_normal(out[name].shape)
        drawn = base * np.exp(spread * noise) if base else spread * noise
        out[name] = jnp.asarray(drawn.astype(out[name].dtype))
    for name, factor in factors.items():
        out[name] = (out[name] * factor).astype(out[name].dtype)
    return out
```

```python
from contextlib import ExitStack

import concourse.bass as bass
import numpy as np
from concourse import mybir

ALU = mybir.AluOpType
ACT = mybir.ActivationFunctionType
AX_X = mybir.AxisListType.X
F32 = mybir.dt.float32
F32R = mybir.dt.float32r
U32 = mybir.dt.uint32

P = 128
D = 1024
S = 256
TT = S // P
KT = D // P
SLOT = 4096
BANK = 512
EPS = 1e-6
RH, RDK, RDV = 4, 256, 512
LRU_W = 1536
LB = LRU_W // P
D_FF = 2816
FI = D_FF // 256


def host_constants():
    f8, f4 = np.float64, np.float32
    out = {"ident": np.eye(P, dtype=f4)}
    half = RDK // 2
    inv = 1.0 / (10000.0 ** (np.arange(half, dtype=f4) / f4(half)))
    ang = (inv.astype(f4)[:, None] * np.arange(S, dtype=f4)[None, :]).astype(f4)
    out["cos"] = np.cos(ang.astype(f8)).astype(f4)
    out["sin"] = np.sin(ang.astype(f8)).astype(f4)
    s, t = np.arange(P)[:, None], np.arange(S)[None, :]
    for h in range(RH):
        lg = np.log1p(-np.exp2(-5.0 - h))
        full = np.where(t >= s, np.exp(np.maximum(t - s, 0) * lg), 0.0) * RDK ** -0.5
        out[f"decay{h}"] = np.concatenate([full, full[:, :P]], axis=1).astype(f4)
    a, b = np.arange(P)[:, None], np.arange(P)[None, :]
    same = a // 64 == b // 64
    for d in range(2):
        after = (lambda u, v: u > v) if d == 0 else (lambda u, v: u < v)
        for n in range(6):
            m = 1 << n
            out[f"level{d}{n}"] = ((a // (2 * m) == b // (2 * m)) & (a // m != b // m) & after(a, b)).astype(f4)
        out[f"strict{d}"] = (same & after(b, a)).astype(f4)
        out[f"incl{d}"] = (same & (after(b, a) | (a == b))).astype(f4)
    out["same"] = same.astype(f4)
    out["chunk"] = (a // 64 == np.arange(2)[None, :]).astype(f4)
    qc, kc = 63 - np.arange(P)[:, None] % 64, np.arange(64)[None, :]
    c0 = np.clip(qc - 8, 0, 48)
    ok = (kc >= c0) & (kc < c0 + 16)
    out["colok"] = ok.astype(f4)
    out["colno"] = np.where(ok, 0.0, -1e30).astype(f4)
    out["flip"] = np.where((a // 64 == b // 64) & (a % 64 + b % 64 == 63), 8.0, 0.0).astype(f4)
    out["iota"] = np.tile(np.arange(P, dtype=f4), (P, 1))
    return out


class Chain:

    def __init__(self, eng, sem):
        self.eng, self.sem, self.n, self.i, self.per = eng, sem, 0, None, 0

    def done(self, ins):
        ins.then_inc(self.sem, 1)
        self.n += 1
        self.eng.wait_ge(self.sem, self.n if self.i is None else self.i * self.per + self.n)

    def enter(self, i, per):
        self.i, self.per, self.start = i, per, self.n

    def leave(self, trips):
        assert self.n - self.start == self.per, (self.n - self.start, self.per)
        self.n, self.i = self.start + trips * self.per, None


PC, PCC, PCW, PCB, PGB, PAP, PSC = 0, 8, 16, 64, 76, 100, 112
PROWS = 118
CONST = host_constants()
CONST_AT = {}
for _name, _a in CONST.items():
    CONST_AT[_name] = (sum(n for _, n in CONST_AT.values()), _a.shape[1])
CONST_N = sum(n for _, n in CONST_AT.values())

SLOTS = {}
UNITS = {}
for _name, _n in [("ada", 12), ("ret_in", 12), ("ret_out", 4), ("ffn0", 2 * FI), ("lru_in", 6),
                  ("lru_gate", 2), ("lru_out", 3), ("ffn1", 2 * FI), ("mix_in", 7), ("mix_out", 2), ("peer_q", 4)]:
    SLOTS[_name] = sum(n for _, n in SLOTS.values()), _n
SLOTS = {k: v[0] for k, v in SLOTS.items()}
RET_STEPS = [("s", 0), ("s", 1), ("o", 0), ("s", 2), ("o", 1), ("s", 3), ("o", 2), ("o", 3),
             ("t", 0), ("t", 1), ("t", 2), ("t", 3)]
RET_UNITS = {"s": 1, "o": 2, "t": 2}
MIX_SLOTS = [(0, 512), (512, 512), (1024, 512), (1536, 512), (2048, 512), (2560, 512), (3072, 384)]
CTX, SEQ = 0, 2
MIX_UNITS = [
    (0, [("n", 2, 0, 512)], ("rk", 0)), (0, [("n", 3, 0, 512)], ("rk", 1)),
    (0, [("n", 0, 256, 256), ("n", 1, 256, 256)], ("k", CTX)),
    (1, [("n", 0, 0, 256), ("n", 1, 0, 256)], ("v", CTX)), (1, [("n", 2, 0, 256), ("n", 3, 0, 256)], ("v", SEQ)),
    (1, [("t", 256, CTX), ("t", 256, SEQ)], ("w", 0)), (1, [("t", 384, CTX), ("t", 384, SEQ)], ("a", 0)),
    (2, [("t", 0, SEQ)], ("g", 0)), (2, [("t", 128, SEQ), ("t", 256, SEQ)], ("q", 0)), (2, [("t", 384, SEQ)], ("q", 2)),
    (3, [("t", 0, SEQ)], ("q", 3)),
    *[(3, [("t", 128 + 128 * j, CTX), ("t", 128 + 128 * j, SEQ)], ("nk", j)) for j in range(3)],
    (4, [("t", 0, CTX), ("t", 0, SEQ)], ("nk", 3)),
    *[(4, [("n", t, 128, 384)], ("nv", t)) for t in range(4)],
    (5, [("n", t, 0, 128) for t in range(4)], ("nv3", 0)),
    (5, [("t", 128, SEQ), ("t", 256, SEQ)], ("z", 0)), (5, [("t", 384, SEQ)], ("z", 2)),
    (6, [("t", 0, SEQ), ("t", 128, SEQ)], ("z", 3)), (6, [("t", 256, SEQ)], ("z", 5)),
]


def rwkv_plan():
    st = lambda k, n: [(k, d, k ^ d, "st", n) for d in range(2)] if k >= 0 else []
    for k in range(4):
        work = ([("cum", 0), ("tr", 0), ("tr", 1), ("ab", 0), ("ab", 1)] + [("l", 0), ("l", 1)] * (k >= 2)
                + [("bv", 0), ("lev", 0)])
        for n in range(1, 6):
            work += [("t", n), ("y", n), ("xy", n)]
        work += [("ug", 0), ("mn", 0), ("mn", 1)] + [("rt", 0)] * (k >= 2)
        for what, n in work:
            for d in range(2):
                yield k, d, k ^ d, what, n
            if what in ("cum", "tr") and (what, n) != ("tr", 1):
                yield from st(k - 1, int(what == "tr"))
    yield from st(3, 0) + st(3, 1)


RW_PLAN = list(rwkv_plan())
RW_UNIT = {(k, d, what, n): u for u, (k, d, t, what, n) in enumerate(x for x in RW_PLAN if x[3] != "st")}
CDECAY = float(np.exp(-0.5))

for _name, _n in [("param", 1), ("ada", 12), ("norm0", 4), ("ret_in", 24), ("ret_heads", 20), ("norm1", 4),
                  ("ffn0", 2 * FI), ("norm2", 4), ("lru_in", 12), ("lru_gate", 12), ("norm3", 4),
                  ("ffn1", 2 * FI), ("norm_c", 4), ("norm_l", 4), ("mix_in", len(MIX_UNITS)), ("decay", 8), ("chunk", 1),
                  ("rwkv", len(RW_UNIT)), ("rw_gate", 1), ("rw_out", 1), ("na", 32), ("na_out", 2), ("norm_p", 4),
                  ("peer_q", 8), ("keys", 4), ("peer_s", 8), ("picks", 2), ("gates", S // 4)]:
    UNITS[_name] = sum(n for _, n in UNITS.values()), _n
UNITS = {k: v[0] for k, v in UNITS.items()}
ROWS = ([("norm", 0, n) for n in range(4)] + [("norm", 1, n) for n in range(4)]
        + [("mod", 1, 1), ("vec", "norm1_g_2", 1), ("mod", 1, 0), ("mod", 0, 1), ("vec", "norm1_g_2", 1),
           ("mod", 0, 0), ("mod", 0, 2), ("mod", 0, 4), ("vec", "norm2_g_2", 1), ("mod", 0, 3), ("mod", 0, 5),
           ("vec", "final_g_2", 0)])
RB = 3


def unit(u0, i=0, per=0):
    return u0 % 4, i * (per // 4) + u0 // 4


def slot(s0, i=0, per=0):
    return s0 % 2, i * (per // 2) + s0 // 2


FFN_HEAD = [("in", 0), ("in", 1), ("out", 0)]
FFN_BODY = [("in", 2), ("out", 1), ("in", 3), ("out", 2)]
FFN_TAIL = [("in", FI - 1), ("out", FI - 2), ("out", FI - 1)]
FFN_TRIPS = (FI - 3) // 2
FFN_BASE = {"ffn0": 0, "ffn1": FI}
FFN_SIZE = {"in": SLOT, "out": 2 * D}


def ffn_steps(eng, base, step, chain=None, per=0):
    for k, (kind, n) in enumerate(FFN_HEAD):
        step(kind, n, base + k)
    with eng.Fori(0, FFN_TRIPS) as i:
        if chain:
            chain.enter(i, per)
        for k, (kind, n) in enumerate(FFN_BODY):
            step(kind, n, base + len(FFN_HEAD) + k, i)
    if chain:
        chain.leave(FFN_TRIPS)
    for k, (kind, n) in enumerate(FFN_TAIL):
        step(kind, n, base + 2 * FI - len(FFN_TAIL) + k)


def rounds(eng, trips, body):
    body(0)
    with eng.Fori(1, trips) as i:
        body(i)


def after(base, s0, last):
    order = FFN_HEAD + FFN_BODY * FFN_TRIPS + FFN_TAIL
    n = s0 - base + 1
    return FFN_SIZE[order[n][0]] if n < len(order) else last


NA_STEPS = TT * 8


def na_scores(i):
    return max(2 * i - 1, 0)


def na_turned(i):
    return min(2 * i + 2, 2 * NA_STEPS - 1)


def peer_steps(eng, first, second, third):
    third = third or (lambda j, i=0: None)
    first(0)
    first(1)
    second(0)
    first(2)
    second(1)
    third(0)
    with eng.Fori(0, P // 2 - 2) as i:
        for j in (1, 2):
            first(j + 2, i)
            second(j + 1, i)
            third(j, i)
    first(P - 1)
    second(P - 2)
    third(P - 3)
    second(P - 1)
    third(P - 2)
    third(P - 1)


def first_and_second_block(nc, A, consts, out, mods, upto=99):
    cols = lambda name: consts[:, CONST_AT[name][0]:sum(CONST_AT[name])]
    with ExitStack() as ctx:
        def sb(name, shape, dt=F32, stack=ctx):
            return stack.enter_context(nc.sbuf_tensor(name, shape, dt))

        def sem(name):
            return ctx.enter_context(nc.semaphore(name))

        PS = ctx.enter_context(nc.psum_tensor("psum", [P, 8, BANK], F32))
        ident = sb("ident", [P, P])
        prow = sb("param_rows", [P, P])
        pcol = sb("param_cols", [P, PROWS])
        sq = sb("square_sums", [P, TT])
        rs = sb("inverse_rms", [P, TT])
        small = sb("small", [P, 192])
        X = sb("residual", [P, TT, D])
        xs_at = nc.sbuf_base
        XS = sb("normed", [P, TT, D])
        hh_at = nc.sbuf_base
        HH = sb("input_hi", [P, KT, S], F32R)
        HL = sb("input_lo", [P, KT, S], F32R)
        rows_at = nc.sbuf_base
        rows = sb("rows", [P, RB, D])
        wraw_at = nc.sbuf_base
        wraw = sb("weights", [P, 2, SLOT])
        whi_at = nc.sbuf_base
        whi = sb("weights_hi", [P, 2, SLOT], F32R)
        wlo = sb("weights_lo", [P, 2, SLOT], F32R)
        stage_at = nc.sbuf_base

        with ExitStack() as st:
            csilu = sb("c_silu", [P, 16], F32, st)
            ch = sb("c_hi", [P, KT, P], F32R, st)
            cl = sb("c_lo", [P, KT, P], F32R, st)
            abias = sb("ada_bias", [P, 4, BANK], F32, st)
            astage = sb("ada_rows", [P, 4, BANK], F32, st)
        with ExitStack() as st:
            QK = sb("qk", [P, 16, S], F32, st)
            V = sb("values", [P, TT, RH * RDV], F32, st)
            SG = sb("gate_silu", [P, TT, RH * RDV], F32, st)
            SC = sb("scores", [P, 2, 384], F32, st)
            rot = sb("rotary", [P, 2, S], F32, st)
            decay = sb("decay", [P, RH, 384], F32, st)
            ON = sb("head_normed", [P, TT, RDV], F32, st)
        with ExitStack() as st:
            OH = sb("ret_hi", [P, 16, S], F32R, st)
            OL = sb("ret_lo", [P, 16, S], F32R, st)
        RT = XS
        with ExitStack() as st:
            fg = sb("ffn_gate", [P, 2, BANK], F32, st)
            fh = sb("ffn_hidden", [P, 2, BANK], F32, st)
            FH = sb("ffn_hi", [P, 2, 2, S], F32R, st)
            FL = sb("ffn_lo", [P, 2, 2, S], F32R, st)
        with ExitStack() as st:
            Y = sb("lru_y", [P, LB, S], F32, st)
            UC = sb("lru_u", [P, LB, S], F32, st)
            UH = sb("lru_hi", [P, LB, S], F32R, st)
            UL = sb("lru_lo", [P, LB, S], F32R, st)
            with ExitStack() as st2:
                UP = sb("lru_padded", [P, 4, S + 3], F32, st2)
            LR = sb("lru_r", [P, 2, BANK], F32, st)
            LI = sb("lru_i", [P, 2, BANK], F32, st)
            LA = sb("lru_a", [P, 2, BANK], F32, st)
            LQ = sb("lru_q", [P, BANK], F32, st)
        acol = small[:, 0:12]
        ancol = small[:, 12:24]
        at = [small[:, 24 + 12 * j:36 + 12 * j] for j in range(4)]
        eps_col, one_col = small[:, 82:83], small[:, 83:84]
        bst = small[:, 84:96].rearrange("p (t s) -> p t s", t=TT)
        bmv = small[:, 78:82].rearrange("p (t s) -> p t s", t=TT)

        class Region:

            def __init__(self, name, start, size):
                self.name, self.at, self.end = name, start, start + size

            def take(self, name, shape, dt=F32):
                size = 4 * int(np.prod(shape[1:]))
                size = -(-size // 32) * 32
                assert self.at + size <= self.end, (self.name, name, self.at + size - self.end)
                self.at += size
                return nc.alloc_sbuf_tensor_at(name, shape, dt, offset=self.at - size)

        KB = 1024
        stage = Region("stage", stage_at, nc.sbuf_usable_end // 32 * 32 - stage_at)
        ZR = stage.take("z_r", [P, TT, 256])
        ZK = stage.take("z_k", [P, 4, 256])
        ZV = stage.take("z_v", [P, 4, 256])
        LWT = stage.take("lora_w", [P, 2 * S])
        LAT = stage.take("lora_a", [P, 2 * S])
        SGT = stage.take("lora_g", [P, S])
        NQ = stage.take("na_q", [P, 4, S])
        NK = stage.take("na_k", [P, 4, 2 * S])
        NV = stage.take("na_v", [P, 4, 512])
        SCZ = stage.take("sc_z", [P, 6, S])
        split_at = stage.at
        CH = stage.take("context_hi", [P, KT, S], F32R)
        CL = stage.take("context_lo", [P, KT, S], F32R)
        XC = stage.take("context", [P, TT, D])
        again = Region("split context", split_at, stage.end - split_at)
        WA = again.take("decay_and_a", [P, 4, 2, 2, 256])
        KD = again.take("rw_k", [P, 4, 512])
        again = Region("split context", split_at, stage.end - split_at)
        BIAS = again.take("na_bias", [P, TT, 8, S])
        ring = Region("ring", whi_at, 64 * KB)
        MASK = ring.take("masks", [P, 16, P])
        RWR = ring.take("rw_rows", [P, 2048])
        KK = ring.take("rw_kk", [P, 4, 256])
        LORA = ring.take("lora_up", [P, 3, 256])
        scratch = Region("idle rows", rows_at, RB * D * 4)
        xs_again = Region("idle scratch", xs_at, 8 * KB)
        BK = [ring.take(f"bv_kappa{d}", [P, 2, 4, 64]) for d in range(2)]
        BE = [ring.take(f"beta{d}", [P, 256]) for d in range(2)]
        KR = [ring.take(f"k_rel{d}", [P, 256]) for d in range(2)]
        RH_ = [ring.take(f"rho{d}", [P, 256]) for d in range(2)]
        TR = [ring.take(f"turned{d}", [P, 4, 2, P]) for d in range(2)]
        AA = [ring.take(f"a_raw{d}", [P, 2, 2, P]) for d in range(2)]
        XX = [ring.take(f"inv_t{d}", [P, 2, 2, P]) for d in range(2)]
        TI = [ring.take(f"inv{d}", [P, 2, 2, P]) for d in range(2)]
        BT = [ring.take(f"b_t{d}", [P, 2, 2, P]) for d in range(2)]
        LL = [xs_again.take(f"l_t{d}", [P, 2, 2, 2, P]) for d in range(2)]
        AM = [scratch.take(f"a_level{d}", [P, 2, 2, P]) for d in range(2)]
        YY = [scratch.take(f"a_x{d}", [P, 2, 2, P]) for d in range(2)]
        NUG = [scratch.take(f"minus_u_g{d}", [P, 2, 4, 64]) for d in range(2)]
        hh_again = Region("idle input", hh_at, 8 * KB)
        MN = [hh_again.take(f"m_n{d}", [P, 2, 4, P]) for d in range(2)]
        EP = AM
        EN = YY
        RTt = [ring.take(f"r_turned{d}", [P, 2, P]) for d in range(2)]
        SB = [ring.take(f"state{d}", [P, 2, P]) for d in range(2)]
        PCD = ring.take("chunk_decay", [P, 4, 2, 2, 2])
        SP = ring.take("sc_padded", [P, 2, S + 2])
        late = Region("masks, later", whi_at, 8 * KB)
        RY = late.take("rw_y", [P, TT, 256])
        RW2 = late.take("rw_y2", [P, TT, 256])
        RG = late.take("rw_gate", [P, TT, 256])
        scratch = Region("idle rows", rows_at, RB * D * 4)
        NS = scratch.take("na_scores", [P, 4, 512])
        NPT = scratch.take("na_probs_t", [P, 2, 512])
        xs_again = Region("idle scratch", xs_at, 8 * KB)
        NY = xs_again.take("na_y", [P, TT, 512])
        CKM = xs_again.take("na_columns", [P, 2, 64])
        FLIP = xs_again.take("na_flip", [P, P])
        top = nc.sbuf_usable_end // 32 * 32
        stage = Region("stage, PEER", stage_at, top - stage_at)
        QT = stage.take("peer_queries", [P, 16, S])
        KN = stage.take("peer_keys", [P, 16, P])
        KTt = stage.take("peer_keys_t", [P, 16, P])
        PSC_ = stage.take("peer_scores", [P, 16, P])
        CAND = stage.take("peer_sums", [P, 8, 16, 16])
        TV = stage.take("top_values", [P, 16, 16])
        TX = stage.take("top_at", [P, 16, 16], U32)
        TF = stage.take("top_at_f", [P, 16, 16])
        CV = stage.take("pick_values", [P, 8, 16])
        CX = stage.take("pick_at", [P, 8, 16], U32)
        CXH = stage.take("pick_at_parts", [P, 2, 8, 16], U32)
        CF = stage.take("pick_at_f", [P, 2, 8, 16])
        PK = stage.take("picks", [P, 3, 8, 16])
        CS = stage.take("gate_sums", [P, 8])
        EQ = Region("keys, later", stage_at + 16 * KB, 8 * KB).take("pick_equal", [P, 8, 16, 16])
        g_at = top - 128 * KB
        GT = Region("gates", g_at, 128 * KB).take("gate_table", [P, P, S])
        low = Region("below the gates", wraw_at, g_at - wraw_at)
        UR = low.take("u_rows", [P, 2, D])
        VR = low.take("v_rows", [P, 2, D])
        GA = low.take("act", [P, 2, S])
        AH = low.take("act_hi", [P, 2, S], F32R)
        AL = low.take("act_lo", [P, 2, S], F32R)
        turned_at = low.at
        UTH = low.take("u_hi", [P, 2, KT, P], F32R)
        UTL = low.take("u_lo", [P, 2, KT, P], F32R)
        low = Region("where u goes later", turned_at, 16 * KB)
        HKT = low.take("picks_t", [P, 3, S])
        ONE1 = low.take("one_hot_first", [P, 8, P])
        ONE2 = low.take("one_hot_second", [P, 8, P])
        IOTA = low.take("iota", [P, P])
        VH = Region("idle scratch", xs_at, 8 * KB).take("v_hi", [P, 2, D], F32R)
        VL = Region("idle rows", rows_at, 8 * KB).take("v_lo", [P, 2, D], F32R)
        eps2_col, eps3_col = small[:, 96:97], small[:, 97:98]
        kn = small[:, 98:114]
        gmu, gvar, gsum = small[:, 114:122], small[:, 122:130], small[:, 130:138]
        nmax = [small[:, 138 + j:139 + j] for j in range(4)]
        nsum = small[:, 142:158]
        chk = small[:, 158:160]

        s_mix = sem("s_mix")
        s_ctx = sem("s_ctx")
        s_bias = sem("s_bias")
        s_sig = sem("s_sig")
        s_kk = sem("s_kk")
        s_kks = sem("s_kks")
        s_rel = sem("s_rel")
        s_aa = sem("s_aa")
        s_am = sem("s_am")
        s_stp = [sem(f"s_stp{d}") for d in range(2)]
        s_st = [sem(f"s_st{d}") for d in range(2)]
        s_y = sem("s_y")
        s_gn = sem("s_gn")
        s_gns = sem("s_gns")
        s_ry = sem("s_ry")
        s_sc = sem("s_sconv")
        s_sch = sem("s_sconvh")
        s_yt = sem("s_yt")
        s_biasm = sem("s_biasm")
        s_ns = sem("s_ns")
        s_nx = sem("s_nx")
        s_no = sem("s_no")
        s_ny = sem("s_ny")
        s_keys = sem("s_keys")
        s_iota = sem("s_iota")
        s_pd = sem("s_pd")
        s_pm = sem("s_pm")
        s_pe = sem("s_pexp")
        s_pk = sem("s_pk")
        s_oh = sem("s_oh")
        s_ur = [sem(f"s_ur{b}") for b in range(2)]
        s_vr = [sem(f"s_vr{b}") for b in range(2)]
        s_ut = [sem(f"s_ut{b}") for b in range(2)]
        s_uh = [sem(f"s_uh{b}") for b in range(2)]
        s_ul = [sem(f"s_ul{b}") for b in range(2)]
        s_vh = sem("s_vh")
        s_vl = sem("s_vl")
        s_ap = sem("s_ap")
        s_ag = sem("s_ag")
        s_aw = sem("s_aw")
        s_as = sem("s_as")
        s_ao = sem("s_ao")

        s_const = sem("s_const")
        s_xload = sem("s_xload")
        s_full = [sem(f"s_full{b}") for b in range(4)]
        s_free = [sem(f"s_free{b}") for b in range(4)]
        s_wload = [sem(f"s_wload{r}") for r in range(2)]
        s_whi = [sem(f"s_whi{r}") for r in range(2)]
        s_wlo = [sem(f"s_wlo{r}") for r in range(2)]
        s_wused = [sem(f"s_wused{r}") for r in range(2)]
        s_row = [sem(f"s_row{r}") for r in range(RB)]
        s_rowused = sem("s_rowused")
        s_xhi = sem("s_xhi")
        s_sq = sem("s_sq")
        s_xs = sem("s_xs")
        s_x = sem("s_x")
        s_acc = sem("s_acc")
        s_accfree = sem("s_accfree")
        s_dve = sem("s_dve")
        s_act = sem("s_act")
        s_pool = sem("s_pool")
        s_csilu = sem("s_csilu")
        s_cparts = sem("s_cparts")
        s_abias = [sem(f"s_abias{b}") for b in range(4)]
        s_amod = [sem(f"s_amod{b}") for b in range(4)]
        s_ast = [sem(f"s_ast{b}") for b in range(4)]
        s_rconst = sem("s_rconst")
        s_rotp = sem("s_rotp")
        s_rot = sem("s_rot")
        s_sc = sem("s_sc")
        s_og = sem("s_og")
        s_fg = sem("s_fg")
        s_fh = sem("s_fh")
        s_fp = sem("s_fp")
        s_fu = sem("s_fu")
        s_pcol = sem("s_pcol")
        s_uc = sem("s_uc")
        s_up = sem("s_up")
        s_alog = sem("s_alog")
        s_acol = sem("s_acol")
        s_lg = sem("s_lg")
        s_la = sem("s_la")
        s_liu = sem("s_liu")
        s_lh = sem("s_lh")
        s_lp = sem("s_lp")
        s_rs = sem("s_rs")
        s_bn = sem("s_bn")
        s_bnr = sem("s_bnr")
        s_lq = sem("s_lq")
        s_lmult = sem("s_lmult")
        s_eps = sem("s_eps")
        s_out = sem("s_out")

        FFN = [("ffn0", 0), ("ffn1", 1)]
        acc = lambda tt, half: PS[:, 4 + 2 * tt + half, :]
        W = {n: A[n][0].rearrange("(k p) n -> p k n", p=P)
             for n in ("ret_w_in", "ret_w_out", "lru_w_in", "lru_w_out", "ada_w_2", "w_in_2", "w_out_2", "peer_q_w_2")}
        ffn_in = [A["ffn_w_in"][l].rearrange("(k p) n -> p k n", p=P) for l in range(2)]
        ffn_out = [A["ffn_w_out"][l].rearrange("(k p) n -> p k n", p=P) for l in range(2)]
        
        block = ctx.enter_context(nc.Block())

        @block.sync
        def _(sp):
            def load(s0, parts, i=0, per=0):
                r, use = slot(s0, i, per)
                sp.wait_ge(s_wlo[r], use)
                for off, k, n, src in parts:
                    dst = wraw[:, r, off:off + k * n].rearrange("p (k n) -> p k n", k=k)
                    sp.dma_start(dst, src).then_inc(s_wload[r], 16)

            def wide(s0, w, n0, i=0, per=0, istep=0):
                view = w[:, :, bass.ds(i * istep + n0, BANK)]
                load(s0, [(0, 4, BANK, view[:, 0:4, :]), (4 * BANK, 4, BANK, view[:, 4:8, :])], i, per)

            def deep(s0, w, k0):
                load(s0, [(0, 2, D, w[:, k0:k0 + 2, :]), (2 * D, 2, D, w[:, k0 + 2:k0 + 4, :])])

            sp.dma_start(ident[:, :], cols("ident")).then_inc(s_const, 16)
            as_rows = lambda a: a.rearrange("(r p) -> r p", p=P)
            for at_, src in [(PC, A["c_2"][0].rearrange("(r p) -> r p", p=P)), (PCC, as_rows(A["c_ctx_2"])),
                             (PCW, A["lru_conv_w"][0].rearrange("j (b p) -> (j b) p", p=P)),
                             (PCB, as_rows(A["lru_conv_b"][0])),
                             (PGB, A["lru_gate_b"][0].rearrange("g n (j p) -> (g n j) p", p=P)),
                             (PAP, as_rows(A["lru_a_param"][0])),
                             (PSC, A["sc_conv_w_2"][0].rearrange("j (b p) -> (j b) p", p=P))]:
                sp.dma_start(prow[at_:at_ + src.shape[0], :], src).then_inc(s_const, 16)
            sp.dma_start(X[:, :, :], A["x"][0].rearrange("(t p) d -> p t d", p=P)).then_inc(s_xload, 16)

            def ada(i):
                for j in range(4):
                    wide(SLOTS["ada"] + j, W["ada_w_2"], j * BANK, i, 4, 4 * BANK)

            rounds(sp, 3, ada)
            for name, n in (("cos", 0), ("sin", 1)):
                sp.dma_start(rot[:, n, :], cols(name)).then_inc(s_rconst, 16)
            for h in range(RH):
                sp.dma_start(decay[:, h, :], cols(f"decay{h}")).then_inc(s_rconst, 16)
            with sp.Fori(0, 6) as i:
                for j in range(2):
                    wide(SLOTS["ret_in"] + j, W["ret_w_in"], j * BANK, i, 2, 2 * BANK)
            for j in range(4):
                deep(SLOTS["ret_out"] + j, W["ret_w_out"], 4 * j)

            def ffn(name, layer):
                def step(kind, n, s0, i=0):
                    r, use = slot(s0, i, 4)
                    sp.wait_ge(s_wlo[r], use)
                    for j in range(2):
                        if kind == "in":
                            dst = wraw[:, r, :].rearrange("p (k n) -> p k n", k=KT)[:, :, j * 256:(j + 1) * 256]
                            src = ffn_in[layer][:, :, bass.ds(i * 512 + n * 256 + j * D_FF, 256)]
                        else:
                            dst = wraw[:, r, j * D:(j + 1) * D]
                            src = A["ffn_w_out"][layer][bass.ds(i * 512 + (2 * n + j) * P, P), :]
                        sp.dma_start(dst, src).then_inc(s_wload[r], 16)

                ffn_steps(sp, SLOTS[name], step)

            ffn("ffn0", 0)
            with sp.Fori(0, 3) as i:
                for j in range(2):
                    wide(SLOTS["lru_in"] + j, W["lru_w_in"], j * LRU_W, i, 2, BANK)
            for j in range(2):
                r, use = slot(SLOTS["lru_gate"] + j)
                sp.wait_ge(s_wlo[r], use)
                for g in range(2):
                    dst = wraw[:, r, g * 1536:(g + 1) * 1536].rearrange("p (n k m) -> p n k m", n=3, k=2)
                    src = A["lru_gate_w"][0, g, 3 * j:3 * j + 3].rearrange("n (k p) m -> p n k m", p=P)
                    sp.dma_start(dst, src).then_inc(s_wload[r], 16)
            for j in range(3):
                deep(SLOTS["lru_out"] + j, W["lru_w_out"], 4 * j)
            ffn("ffn1", 1)
            for j, (c0, n) in enumerate(MIX_SLOTS):
                r, use = slot(SLOTS["mix_in"] + j)
                sp.wait_ge(s_wlo[r], use)
                dst = wraw[:, r, 0:KT * n].rearrange("p (k n) -> p k n", k=KT)
                for h in range(2):
                    sp.dma_start(dst[:, 4 * h:4 * h + 4, :], W["w_in_2"][:, 4 * h:4 * h + 4, c0:c0 + n])\
                        .then_inc(s_wload[r], 16)
                if j == 0:
                    sp.wait_ge(s_acc, 4)
                    sp.dma_start(XC[:, :, :], A["ctx_2"][0].rearrange("(t p) d -> p t d", p=P)).then_inc(s_ctx, 16)
            for j in range(2):
                deep(SLOTS["mix_out"] + j, W["w_out_2"], 4 * j)
            for j in range(2):
                r, use = slot(SLOTS["mix_in"] + 5 + j)
                sp.wait_ge(s_wused[r], use + 1)
            sp.dma_start(MASK[:, :, :], consts[:, CONST_AT["level00"][0]:CONST_AT["same"][0]]
                         .rearrange("p (m n) -> p m n", n=P)).then_inc(s_mix, 16)
            for n, (name, d) in enumerate([("rw_w0_2", 0), ("rw_a0_2", 0), ("rw_w0_2", 1), ("rw_a0_2", 1)]):
                sp.dma_start(RWR[:, n * 256:(n + 1) * 256], A[name][0, d].partition_broadcast(P)).then_inc(s_mix, 16)
            for n, name in enumerate(["rw_k_k_2", "rw_k_a_2", "rw_r_k_2", "rw_lnx_g_2"]):
                src = A[name][0].rearrange("h j -> (h j)") if name == "rw_r_k_2" else A[name][0]
                sp.dma_start(RWR[:, (4 + n) * 256:(5 + n) * 256], src.partition_broadcast(P)).then_inc(s_mix, 16)
            sp.dma_start(LORA[:, 0, :], A["rw_w_up_2"][0].rearrange("d r c -> (d r) c")).then_inc(s_mix, 16)
            sp.dma_start(LORA[:, 1, :], A["rw_a_up_2"][0].rearrange("d r c -> (d r) c")).then_inc(s_mix, 16)
            sp.dma_start(LORA[:, 2, :], A["rw_g_up_2"][0]).then_inc(s_mix, 16)
            sp.dma_start(chk, cols("chunk")).then_inc(s_mix, 16)
            sp.dma_start(prow[:, :], cols("same")).then_inc(s_mix, 16)
            sp.wait_ge(s_rel, 8)
            rpb = A["na_rpb_2"]
            for qr in range(4):
                half, qt = qr % 2, qr // 2
                for kr in range(4):
                    src = bass.AP(rpb.tensor, (kr - qr + 7) * 31 + 15 - 63, [[1, 64], [465, 8], [1, 64]])
                    sp.dma_start(BIAS[64 * half:64 * half + 64, qt, :, 64 * kr:64 * kr + 64], src)\
                        .then_inc(s_bias, 16)
            sp.wait_ge(s_ry, 1)
            sp.dma_start(CKM[:, 0, :], cols("colok")).then_inc(s_bias, 16)
            sp.dma_start(CKM[:, 1, :], cols("colno")).then_inc(s_bias, 16)
            sp.dma_start(FLIP[:, :], cols("flip")).then_inc(s_bias, 16)
            for j in range(4):
                wide(SLOTS["peer_q"] + j, W["peer_q_w_2"], j * BANK)
            sp.wait_ge(s_acc, 5)
            sp.dma_start(KN[:, :, :], A["peer_sub_keys_2"][0].rearrange("h p n d -> n (h p) d")).then_inc(s_keys, 16)
            for j in (2, 3):
                r, use = slot(SLOTS["peer_q"] + j)
                sp.wait_ge(s_wused[r], use + 1)
            sp.dma_start(IOTA[:, :], cols("iota")).then_inc(s_iota, 16)
            u_tab, v_tab = A["peer_u_2"][0], A["peer_v_2"][0]

            def load_rows_of(j, i=0):
                b = j % 2
                if j >= 2 or not isinstance(i, int):
                    sp.wait_ge(s_ut[b], i * 2 + 2 * (j // 2))
                sp.dma_start(UR[:, b, :], u_tab[bass.ds(i * 256 + j * P, P), :]).then_inc(s_ur[b], 16)
                if j >= 2 or not isinstance(i, int):
                    sp.wait_ge(s_vl, i * 2 + j - 1)
                sp.dma_start(VR[:, b, :], v_tab[bass.ds(i * 256 + j * P, P), :]).then_inc(s_vr[b], 16)

            load_rows_of(0)
            load_rows_of(1)
            with sp.Fori(0, P // 2 - 1) as i:
                load_rows_of(2, i)
                load_rows_of(3, i)
            sp.wait_ge(s_x, 12 + 2)
            sp.dma_start(out[0].rearrange("(t p) d -> p t d", p=P), XS[:, :, :]).then_inc(s_out, 16)
            sp.wait_ge(s_out, 16)

        @block.gpsimd
        def _(pool):
            chain = Chain(pool, s_pool)

            def evacuated(u0, i=0, per=0):
                b, use = unit(u0, i, per)
                pool.wait_ge(s_free[b], use + 1)

            def load_rows(first, last):
                for r in range(first, last):
                    if r >= RB:
                        pool.wait_ge(s_rowused, r - RB + 1)
                    pool.dma_start(rows[:, r % RB, :], row_source(r).partition_broadcast(P))\
                        .then_inc(s_row[r % RB], 16)

            def row_source(r):
                kind, a, b = ROWS[r]
                if kind == "norm":
                    return A["norm_g"][a, b]
                if kind == "vec":
                    return A[a][0] if b else A[a]
                return mods[a, b * D:(b + 1) * D]

            def parts(hi, lo, src, semaphore):
                ones = one_col.unsqueeze(2).broadcast_to([P, 2, S])
                chain.done(nc.gpsimd.tensor_tensor(hi, src, ones, ALU.mult))
                nc.gpsimd.tensor_tensor(lo, src, hi.bitcast(F32), ALU.subtract).then_inc(semaphore, 1)

            chain.done(nc.gpsimd.memset(one_col, 1.0))
            load_rows(0, RB)
            for i in range(3):
                for j in range(4):
                    at_ = slice((4 * i + j) * BANK, (4 * i + j + 1) * BANK)
                    evac = UNITS["ada"] + 4 * (i - 1) + j
                    if i:
                        evacuated(evac)
                    pool.dma_start(abias[:, j, :], A["ada_b_2"][0, at_].partition_broadcast(P))\
                        .then_inc(s_abias[j], 16)
                for j in range(4):
                    at_ = slice((4 * i + j) * BANK, (4 * i + j + 1) * BANK)
                    evacuated(UNITS["ada"] + 4 * i + j)
                    for half in range(2):
                        pool.dma_start(mods[half:half + 1, at_], astage[64 * half:64 * half + 1, j, :])\
                            .then_inc(s_ast[j], 16)
            with pool.Fori(0, 2) as i:
                for j in range(4):
                    evacuated(UNITS["ret_in"] + j, i, 4)
                    pc = RT[:, j % 2, 0:512].rearrange("p (x t) -> p x t", x=2)
                    ps = RT[:, j % 2, 512:1024].rearrange("p (x t) -> p x t", x=2)
                    nc.gpsimd.tensor_tensor(QK[:, bass.ds(i * 8 + 2 * j, 1), :], pc[:, 0:1, :], ps[:, 1:2, :],
                                            ALU.subtract)
                    nc.gpsimd.tensor_tensor(QK[:, bass.ds(i * 8 + (2 * j + 1), 1), :], ps[:, 0:1, :],
                                            pc[:, 1:2, :], ALU.add).then_inc(s_rot, 1)
            u = UNITS["ret_heads"]
            for kind, h in RET_STEPS:
                if kind == "o":
                    for tt in range(TT):
                        evacuated(u + tt)
                        og = SG[:, tt, h * RDV:(h + 1) * RDV]
                        nc.gpsimd.tensor_tensor(og, og, ON[:, tt, :], ALU.mult).then_inc(s_og, 1)
                u += RET_UNITS[kind]

            def ffn(name):
                base = FFN_BASE[name]

                def step(kind, n, s0, i=0):
                    if kind == "in":
                        n, par = n + base, (n + base) % 2
                        pool.wait_ge(s_fh, i * 2 + n + 1)
                        if n >= 2 or not isinstance(i, int):
                            pool.wait_ge(s_fu, i * 2 + n - 1)
                        parts(FH[:, par], FL[:, par], fh[:, par, :].rearrange("p (b t) -> p b t", b=2), s_fp)

                ffn_steps(pool, SLOTS[name], step, chain, 2)

            load_rows(RB, 4)
            load_rows(4, 5)
            load_rows(5, 6)
            ffn("ffn0")
            load_rows(6, 7)
            load_rows(7, 8)
            for n in range(LB // 2):
                pool.wait_ge(s_uc, n + 1)
                pair = slice(2 * n, 2 * n + 2)
                parts(UH[:, pair, :], UL[:, pair, :], UC[:, pair, :], s_up)
            for n in range(LB // 2):
                pair = slice(2 * n, 2 * n + 2)
                evacuated(UNITS["lru_gate"] + 2 * n + 1)
                li = LI[:, n % 2, :].rearrange("p (b t) -> p b t", b=2)
                nc.gpsimd.tensor_tensor(li, li, UC[:, pair, :], ALU.mult).then_inc(s_liu, 1)
                pool.wait_ge(s_lh, n + 1)
                parts(UH[:, pair, :], UL[:, pair, :], UC[:, pair, :], s_lp)
            load_rows(8, min(9, len(ROWS)))
            load_rows(9, min(10, len(ROWS)))
            ffn("ffn1")
            load_rows(10, 14)
            for qt in range(TT):
                if qt == 0:
                    pool.wait_ge(s_bias, 16 * 19)
                table = BIAS[:, qt, :, :].rearrange("p h (r c) -> p (h r) c", c=64)
                for j, op in enumerate((ALU.mult, ALU.add)):
                    mask = CKM[:, j:j + 1, :].broadcast_to([P, 32, 64])
                    ins = nc.gpsimd.tensor_tensor(table, table, mask, op)
                    if j == 0:
                        chain.done(ins)
                ins.then_inc(s_biasm, 1)
            evacuated(UNITS["na_out"] + 1)
            load_rows(14, 18)
            def gated_parts(j, i=0):
                pool.wait_ge(s_aw, 2 * i + j + 1)
                if j >= 2 or not isinstance(i, int):
                    pool.wait_ge(s_ao, 2 * i + j - 1)
                b = j % 2
                ones = one_col.broadcast_to([P, S])
                chain.done(nc.gpsimd.tensor_tensor(AH[:, b, :], GA[:, b, :], ones, ALU.mult))
                nc.gpsimd.tensor_tensor(AL[:, b, :], GA[:, b, :], AH[:, b, :].bitcast(F32), ALU.subtract)\
                    .then_inc(s_as, 1)

            gated_parts(0)
            gated_parts(1)
            with pool.Fori(0, P // 2 - 1) as i:
                chain.enter(i, 2)
                gated_parts(2, i)
                gated_parts(3, i)
            chain.leave(P // 2 - 1)
            pool.wait_ge(s_ao, P)
            load_rows(18, 20)

        @block.scalar
        def _(act):
            counts = {"sq": 0}

            def split_hi(s0, i=0, per=0, n=SLOT):
                r, use = slot(s0, i, per)
                act.wait_ge(s_wload[r], use * 32 + 32)
                act.wait_ge(s_wused[r], use)
                for piece in range(2):
                    at_ = slice(piece * n // 2, (piece + 1) * n // 2)
                    nc.scalar.activation(whi[:, r, at_], wraw[:, r, at_], ACT.Copy).then_inc(s_whi[r], 1)

            def take(u0, i=0, per=0):
                b, use = unit(u0, i, per)
                act.wait_ge(s_full[b], use + 1)
                return b

            def squares(src):
                for tt in range(TT):
                    nc.scalar.activation(XS[:, tt, :], src[:, tt], ACT.Square, scale=D ** -0.5,
                                         accum_out=sq[:, tt:tt + 1]).then_inc(s_sq, 1)
                counts["sq"] += TT
                act.wait_ge(s_sq, counts["sq"])
                nc.scalar.activation(rs[:, :], sq[:, :], ACT.Sqrt, bias=eps_col).then_inc(s_rs, 1)

            def transposed_hi(u, dst, tt, k0):
                b = take(u)
                nc.scalar.activation(dst[:, k0:k0 + 4, tt * P:(tt + 1) * P],
                                     PS[:, b, :].rearrange("p (k t) -> p k t", k=4), ACT.Copy).then_inc(s_xhi, 1)

            def norm(n, dst=HH):
                if n == 0:
                    act.wait_ge(s_eps, 1)
                    act.wait_ge(s_xload, 16)
                else:
                    act.wait_ge(s_x, 2 * n)
                squares(X)
                for u in range(4):
                    transposed_hi(UNITS[f"norm{n}"] + u, dst, u // 2, 4 * (u % 2))

            def post_norm(n):
                act.wait_ge(s_acc, n + 1)
                squares(PS[:, 4:8, :].rearrange("p (t h) n -> p t (h n)", t=TT))

            split_hi(0)
            act.wait_ge(s_pcol, 1)
            nc.scalar.activation(csilu[:, :], pcol[:, PC:PC + 16], ACT.Silu).then_inc(s_csilu, 1)
            nc.scalar.activation(at[0], pcol[:, PAP:PAP + 12], ACT.Abs).then_inc(s_alog, 1)
            act.wait_ge(s_alog, 1)
            nc.scalar.activation(at[0], at[0], ACT.Exp, scale=-1.0).then_inc(s_alog, 1)
            act.wait_ge(s_acol, 1)
            nc.scalar.activation(at[2], at[1], ACT.Ln).then_inc(s_alog, 1)

            def ada(i):
                for j in range(4):
                    split_hi(SLOTS["ada"] + j + 1, i, 4)

            rounds(act, 3, ada)
            norm(0)
            with act.Fori(0, 2) as i:
                for j in range(2):
                    split_hi(SLOTS["ret_in"] + j + 1, i, 2)
            for b in range(4):
                act.wait_ge(s_ast[b], 16 * 2 * 3)
            for part, (dst, func) in enumerate(((V, ACT.Copy), (SG, ACT.Silu))):
                with act.Fori(0, 2) as i:
                    for j in range(2):
                        split_hi(SLOTS["ret_in"] + 4 + 4 * part + j + 1, i, 2)
                        for tt in range(TT):
                            b = take(UNITS["ret_in"] + 8 + 8 * part + 2 * j + tt, i, 4)
                            nc.scalar.activation(dst[:, tt, bass.ds(i * 2 * BANK + j * BANK, BANK)],
                                                 PS[:, b, :], func).then_inc(s_free[b], 1)
            u = UNITS["ret_heads"]
            for kind, h in RET_STEPS:
                if kind == "o":
                    act.wait_ge(s_bn, 2 * h + 2)
                    nc.scalar.activation(bmv[:, :, 1:2], bmv[:, :, 1:2], ACT.Sqrt, bias=eps_col).then_inc(s_bnr, 1)
                elif kind == "t":
                    for tt in range(TT):
                        transposed_hi(u + tt, OH, tt, 4 * h)
                u += RET_UNITS[kind]
            for j in range(4):
                split_hi(SLOTS["ret_out"] + j + 1)
            post_norm(0)

            def ffn(name, last):
                base, ub, sbase = FFN_BASE[name], UNITS[name], SLOTS[name]

                def step(kind, n, s0, i=0):
                    split_hi(s0 + 1, i, 4, after(sbase, s0, last))
                    if kind == "in":
                        b = take(ub + 2 * n, i, 4)
                        n, par = n + base, (n + base) % 2
                        if n >= 2 or not isinstance(i, int):
                            act.wait_ge(s_fh, i * 2 + n - 1)
                        nc.scalar.activation(fg[:, par, :], PS[:, b, :], ACT.Silu).then_inc(s_free[b], 1)

                ffn_steps(act, sbase, step)

            norm(1)
            ffn("ffn0", SLOT)
            post_norm(1)
            norm(2)
            with act.Fori(0, 3) as i:
                for j in range(2):
                    split_hi(SLOTS["lru_in"] + j + 1, i, 2)
                    if j == 0:
                        for half in range(2):
                            b = take(UNITS["lru_in"] + half, i, 4)
                            nc.scalar.activation(Y[:, bass.ds(i * 4 + 2 * half, 2), :],
                                                 PS[:, b, :].rearrange("p (b t) -> p b t", b=2),
                                                 ACT.Gelu_apprx_tanh).then_inc(s_free[b], 1)
            split_hi(SLOTS["lru_gate"] + 1, n=3072)
            act.wait_ge(s_uc, LB // 2)
            for n in range(LB // 2):
                if n == 3:
                    split_hi(SLOTS["lru_out"])
                par = n % 2
                if n >= 2:
                    act.wait_ge(s_lh, n - 1)
                for g, dst in enumerate((LR, LI)):
                    b = take(UNITS["lru_gate"] + 2 * n + g)
                    for j in range(2):
                        at_ = slice(j * S, (j + 1) * S)
                        ins = nc.scalar.activation(dst[:, par, at_], PS[:, b, at_], ACT.Sigmoid,
                                                   bias=pcol[:, PGB + 12 * g + 2 * n + j:PGB + 12 * g + 2 * n + j + 1])
                    ins.then_inc(s_free[b], 1)
                b, use = unit(UNITS["lru_gate"] + 2 * n)
                act.wait_ge(s_free[b], use + 1)
                for j in range(2):
                    at_, c = slice(j * S, (j + 1) * S), slice(2 * n + j, 2 * n + j + 1)
                    nc.scalar.activation(LA[:, par, at_], LR[:, par, at_], ACT.Exp, scale=acol[:, c]).then_inc(s_la, 1)
                act.wait_ge(s_la, 4 * n + 2)
                for j in range(2):
                    at_, c = slice(j * S, (j + 1) * S), slice(2 * n + j, 2 * n + j + 1)
                    nc.scalar.activation(LR[:, par, at_], LR[:, par, at_], ACT.Tanh, scale=ancol[:, c]).then_inc(s_la, 1)
                act.wait_ge(s_lq, n + 1)
                nc.scalar.activation(LQ[:, :], LQ[:, :], ACT.Sqrt).then_inc(s_lmult, 1)
            for j in range(3):
                split_hi(SLOTS["lru_out"] + j + 1)
            post_norm(2)
            norm(3)
            ffn("ffn1", SLOT)
            post_norm(3)
            def evacuated(u0, i=0, per=0):
                b, use = unit(u0, i, per)
                act.wait_ge(s_free[b], use + 1)

            def out_of(u, dst, func=ACT.Copy, src=None, **kw):
                b = take(u)
                src = PS[:, b, :] if src is None else src(PS[:, b, :])
                nc.scalar.activation(dst, src, func, **kw).then_inc(s_free[b], 1)

            act.wait_ge(s_x, 8)
            act.wait_ge(s_ctx, 16)
            squares(XC)
            for u in range(4):
                transposed_hi(UNITS["norm_c"] + u, CH, u // 2, 4 * (u % 2))
            squares(X)
            for u in range(4):
                transposed_hi(UNITS["norm_l"] + u, HH, u // 2, 4 * (u % 2))
            at_unit = UNITS["mix_in"]
            for j, (_, n_cols) in enumerate(MIX_SLOTS):
                if j + 1 < len(MIX_SLOTS):
                    split_hi(SLOTS["mix_in"] + j + 1, n=KT * MIX_SLOTS[j + 1][1])
                for s, parts_, (where, n) in MIX_UNITS:
                    if s != j:
                        continue
                    first = lambda size: lambda ps: ps[:, 0:size]
                    two = lambda ps: ps.rearrange("p (a b) -> p a b", a=2)
                    if where == "rk":
                        b = take(at_unit)
                        nc.scalar.activation(ZR[:, n, :], PS[:, b, 0:256], ACT.Copy)
                        nc.scalar.activation(ZK[:, SEQ + n, :], PS[:, b, 256:512], ACT.Copy).then_inc(s_free[b], 1)
                    elif where == "k":
                        out_of(at_unit, ZK[:, n:n + 2, :], src=two)
                    elif where == "v":
                        out_of(at_unit, ZV[:, n:n + 2, :], src=two)
                    elif where == "w":
                        out_of(at_unit, LWT[:, :], ACT.Tanh)
                    elif where == "a":
                        out_of(at_unit, LAT[:, :])
                    elif where == "g":
                        out_of(at_unit, SGT[:, :], ACT.Sigmoid, src=first(S))
                    elif where == "nk":
                        out_of(at_unit, NK[:, n, :])
                    elif where == "nv":
                        out_of(at_unit, NV[:, n, 0:384], src=first(384))
                    elif where == "nv3":
                        out_of(at_unit, NV[:, :, 384:512], src=lambda ps: ps.rearrange("p (t n) -> p t n", t=4))
                    else:
                        dst, count = NQ if where == "q" else SCZ, len(parts_)
                        out_of(at_unit, dst[:, n:n + count, :], src=lambda ps, count=count:
                               ps[:, 0:count * S].rearrange("p (a b) -> p a b", a=count))
                    at_unit += 1
            for u in range(8):
                t, d = divmod(u, 2)
                evacuated(UNITS["decay"] + u)
                nc.scalar.activation(WA[:, t, d], WA[:, t, d], ACT.Sigmoid).then_inc(s_sig, 1)
            act.wait_ge(s_kk, 1)
            nc.scalar.activation(kn, kn, ACT.Sqrt, bias=eps2_col).then_inc(s_kks, 1)
            out_of(UNITS["chunk"], PCD[:, :, :, :, :].rearrange("p t d h c -> p (t d h c)"), ACT.Exp,
                   src=lambda ps: ps[:, 0:32], scale=-CDECAY)
            U = lambda k, d, what, n=0: UNITS["rwkv"] + RW_UNIT[k, d, what, n]
            for k, d, t, what, n in RW_PLAN:
                if what == "st":
                    continue
                u = U(k, d, what, n)
                if what == "cum":
                    b = take(u)
                    if k:
                        evacuated(U(k - 1, d, "mn", 1))
                    if k == 3:
                        evacuated(U(2, d, "rt"))
                    nc.scalar.activation(EP[d][:, :, :, :].rearrange("p a b c -> p (a b c)"), PS[:, b, :], ACT.Exp,
                                         scale=-CDECAY)
                    nc.scalar.activation(EN[d][:, :, :, :].rearrange("p a b c -> p (a b c)")[:, 0:256],
                                         PS[:, b, 0:256], ACT.Exp, scale=CDECAY).then_inc(s_free[b], 1)
                elif what == "tr":
                    size = 1 if n and k < 2 else 2
                    out_of(u, TR[d][:, 2 * n:2 * n + size, :, :].rearrange("p a b c -> p (a b c)"),
                           src=lambda ps, size=size: ps[:, 0:256 * size])
                elif what == "ab":
                    b = take(u)
                    nc.scalar.activation(AA[d][:, n, :, :].rearrange("p a b -> p (a b)"), PS[:, b, 0:256], ACT.Copy)\
                        .then_inc(s_aa, 1)
                elif what == "bv":
                    out_of(u, BK[d][:, 0, :, :], src=lambda ps: ps[:, 0:256].rearrange("p (h j) -> p h j", h=4))
                elif what == "t":
                    out_of(u, TI[d][:, :, :, :].rearrange("p a b c -> p (a b c)"))
                elif what == "y":
                    if n == 1:
                        act.wait_ge(s_rel, 2 * k + d + 1)
                    out_of(u, YY[d][:, :, :, :].rearrange("p a b c -> p (a b c)"))
                elif what == "ug":
                    for kind in range(2):
                        b = take(u)
                        ins = nc.scalar.activation(NUG[d][:, kind, :, :], PS[:, b, :]
                                                   .rearrange("p (h a j) -> p a h j", h=4, a=2)[:, kind], ACT.Copy,
                                                   scale=-1.0)
                    ins.then_inc(s_free[b], 1)
            act.wait_ge(s_gn, 1)
            nc.scalar.activation(gvar, gvar, ACT.Sqrt, bias=eps3_col, scale=1.0 / 64).then_inc(s_gns, 1)
            b = take(UNITS["rw_out"])
            nc.scalar.activation(HH[:, 0:2, :], PS[:, b, :].rearrange("p (k t) -> p k t", k=2), ACT.Copy)\
                .then_inc(s_xhi, 1)
            act.wait_ge(s_sc, 1)
            nc.scalar.activation(HH[:, 6:8, :], SCZ[:, 4:6, :], ACT.Copy).then_inc(s_sch, 1)

            for i in range(NA_STEPS):
                if i >= 4:
                    evacuated(UNITS["na"] + na_turned(i - 4))
                act.wait_ge(s_ns, i + 1)
                b = unit(UNITS["na"] + na_scores(i))[0]
                nc.scalar.activation(NS[:, i % 4, :], PS[:, b, :], ACT.Exp, bias=nmax[i % 4], scale=64 ** -0.5,
                                     accum_out=nsum[:, i:i + 1]).then_inc(s_nx, 1)
                act.wait_ge(s_nx, i + 1)
                act.sem_inc(s_free[b], 1)
                if i:
                    out_of(UNITS["na"] + na_turned(i - 1), NPT[:, (i - 1) % 2, :])
            out_of(UNITS["na"] + na_turned(NA_STEPS - 1), NPT[:, (NA_STEPS - 1) % 2, :])
            for tt in range(TT):
                transposed_hi(UNITS["na_out"] + tt, HH, tt, 2)
            evacuated(UNITS["na_out"] + 1)
            for j in range(2):
                split_hi(SLOTS["mix_out"] + j)
            split_hi(SLOTS["peer_q"])
            act.wait_ge(s_x, 10)
            squares(X)
            for u in range(4):
                transposed_hi(UNITS["norm_p"] + u, HH, u // 2, 4 * (u % 2))
            for j in range(4):
                if j < 3:
                    split_hi(SLOTS["peer_q"] + j + 1)
                for half in range(2):
                    at_ = 4 * j + 2 * half
                    out_of(UNITS["peer_q"] + 2 * j + half, QT[:, at_:at_ + 2, :],
                           src=lambda ps: ps.rearrange("p (a b) -> p a b", a=2))
            quarter = lambda ps: ps.rearrange("p (a b) -> p a b", a=4)
            for q in range(4):
                out_of(UNITS["keys"] + q, KTt[:, 4 * q:4 * q + 4, :], src=quarter)

            def scores_out(tt):
                if tt:
                    act.wait_ge(s_pd, tt)
                for q in range(4):
                    out_of(UNITS["peer_s"] + 4 * tt + q, PSC_[:, 4 * q:4 * q + 4, :], src=quarter)

            scores_out(0)
            for tt in range(TT):
                if tt + 1 < TT:
                    scores_out(tt + 1)
                act.wait_ge(s_pm, tt + 1)
                nc.scalar.activation(CV[:, :, :], CV[:, :, :], ACT.Exp).then_inc(s_pe, 1)
                out_of(UNITS["picks"] + tt, HKT[:, :, tt * P:(tt + 1) * P],
                       src=lambda ps: ps[:, 0:3 * P].rearrange("p (a b) -> p a b", a=3))
            with act.Fori(0, S // 16) as i:
                for j in range(4):
                    b = take(UNITS["gates"] + j, i, 4)
                    nc.scalar.activation(GT[:, :, bass.ds(i * 16 + 4 * j, 4)],
                                         PS[:, b, :].rearrange("p (t n) -> p n t", t=4), ACT.Copy)\
                        .then_inc(s_free[b], 1)
            def u_high(j, i=0):
                b, use = j % 2, i + j // 2
                if j >= 2 or not isinstance(i, int):
                    act.wait_ge(s_ap, 2 * i + j - 1)
                for h in range(2):
                    act.wait_ge(s_ut[b], 2 * use + h + 1)
                    nc.scalar.activation(UTH[:, b, 4 * h:4 * h + 4, :], PS[:, h, :].rearrange("p (k e) -> p k e", k=4),
                                         ACT.Copy).then_inc(s_uh[b], 1)

            def gelu(j, i=0):
                b = j % 2
                act.wait_ge(s_ap, 2 * i + j + 1)
                if j >= 2 or not isinstance(i, int):
                    act.wait_ge(s_as, 2 * i + j - 1)
                nc.scalar.activation(GA[:, b, :], PS[:, 2 + b, 0:S], ACT.Gelu_apprx_tanh).then_inc(s_ag, 1)

            def v_high(j, i=0):
                b, use = j % 2, i + j // 2
                act.wait_ge(s_vr[b], use * 16 + 16)
                if j >= 2 or not isinstance(i, int):
                    act.wait_ge(s_ao, 2 * i + j - 1)
                nc.scalar.activation(VH[:, b, :], VR[:, b, :], ACT.Copy).then_inc(s_vh, 1)

            peer_steps(act, u_high, lambda *a: (gelu(*a), v_high(*a)), None)
            act.wait_ge(s_x, 12)
            squares(X)

        @block.vector
        def _(dve):
            chain = Chain(dve, s_dve)
            counts = {"rs": 0, "xhi": 0, "row": 0}

            def split_lo(s0, i=0, per=0, n=SLOT):
                r, use = slot(s0, i, per)
                for piece in range(2):
                    at_ = slice(piece * n // 2, (piece + 1) * n // 2)
                    dve.wait_ge(s_whi[r], use * 2 + piece + 1)
                    ins = nc.vector.tensor_tensor(wlo[:, r, at_], wraw[:, r, at_], whi[:, r, at_].bitcast(F32),
                                                  ALU.subtract)
                ins.then_inc(s_wlo[r], 1)

            def take(u0, i=0, per=0):
                b, use = unit(u0, i, per)
                dve.wait_ge(s_full[b], use + 1)
                return b

            def row():
                r = counts["row"]
                counts["row"] += 1
                dve.wait_ge(s_row[r % RB], 16 * (r // RB + 1))
                return rows[:, r % RB, :]

            def inverse_rms():
                counts["rs"] += 1
                dve.wait_ge(s_rs, counts["rs"])
                chain.done(nc.vector.reciprocal(rs[:, :], rs[:, :]))

            def transposed_lo(u, hi, lo, tt, k0):
                b = unit(u)[0]
                counts["xhi"] += 1
                dve.wait_ge(s_xhi, counts["xhi"])
                at_ = (slice(None), slice(k0, k0 + 4), slice(tt * P, (tt + 1) * P))
                nc.vector.tensor_tensor(lo[at_], PS[:, b, :].rearrange("p (k t) -> p k t", k=4),
                                        hi[at_].bitcast(F32), ALU.subtract).then_inc(s_free[b], 1)

            def norm(n):
                gain = row()
                inverse_rms()
                for tt in range(TT):
                    nc.vector.scalar_tensor_tensor(XS[:, tt, :], X[:, tt, :], rs[:, tt:tt + 1], gain,
                                                   ALU.mult, ALU.mult).then_inc(s_xs, 1)
                dve.wait_ge(s_xs, 2 * n + 2)
                dve.sem_inc(s_rowused, 1)
                for u in range(4):
                    transposed_lo(UNITS[f"norm{n}"] + u, HH, HL, u // 2, 4 * (u % 2))

            def post_norm(n):
                gain = row()
                inverse_rms()
                for tt in range(TT):
                    nc.vector.scalar_tensor_tensor(XS[:, tt, :], PS[:, 4 + 2 * tt:6 + 2 * tt, :]
                                                   .rearrange("p h n -> p (h n)"), rs[:, tt:tt + 1], gain,
                                                   ALU.mult, ALU.mult).then_inc(s_accfree, 1)
                dve.wait_ge(s_accfree, 2 * n + 2)
                dve.sem_inc(s_rowused, 1)
                for tt in range(TT):
                    nc.vector.tensor_tensor(X[:, tt, :], X[:, tt, :], XS[:, tt, :], ALU.add).then_inc(s_x, 1)

            nc.vector.memset(eps_col, EPS).then_inc(s_eps, 1)
            b = take(UNITS["param"])
            nc.vector.tensor_copy(pcol[:, :], PS[:, b, 0:PROWS]).then_inc(s_pcol, 1)
            dve.wait_ge(s_pcol, 1)
            dve.sem_inc(s_free[b], 1)
            for g in range(2):
                dve.wait_ge(s_csilu, 1)
                half = (slice(None), slice(None), slice(64 * g, 64 * g + 64))
                src = csilu[:, 8 * g:8 * g + 8].unsqueeze(2).broadcast_to([P, KT, 64])
                chain.done(nc.vector.tensor_copy(ch[half], src))
                nc.vector.tensor_tensor(cl[half], src, ch[half].bitcast(F32), ALU.subtract).then_inc(s_cparts, 1)
            split_lo(0)
            dve.wait_ge(s_alog, 2)
            nc.vector.tensor_scalar(at[1], at[0], 1.0, None, ALU.add).then_inc(s_acol, 1)
            dve.wait_ge(s_alog, 3)
            chain.done(nc.vector.tensor_scalar(at[1], at[1], -1.0, None, ALU.add))
            chain.done(nc.vector.tensor_scalar(at[3], at[1], 0.0, None, ALU.is_equal))
            chain.done(nc.vector.tensor_tensor(at[1], at[1], at[3], ALU.add))
            chain.done(nc.vector.reciprocal(at[1], at[1]))
            chain.done(nc.vector.tensor_tensor(at[2], at[2], at[1], ALU.mult))
            chain.done(nc.vector.tensor_tensor(at[2], at[2], at[3], ALU.add))
            chain.done(nc.vector.tensor_tensor(at[2], at[2], at[0], ALU.mult))
            chain.done(nc.vector.tensor_scalar(at[3], pcol[:, PAP:PAP + 12], -1.0, 0.0, ALU.mult, ALU.max))
            chain.done(nc.vector.tensor_tensor(at[2], at[2], at[3], ALU.add))
            chain.done(nc.vector.tensor_scalar(acol, at[2], -8.0, None, ALU.mult))
            nc.vector.tensor_scalar(ancol, at[2], 8.0, None, ALU.mult).then_inc(s_acol, 1)

            def ada(i):
                for j in range(4):
                    split_lo(SLOTS["ada"] + j + 1, i, 4)
                    b = take(UNITS["ada"] + j, i, 4)
                    dve.wait_ge(s_abias[j], i * 16 + 16)
                    dve.wait_ge(s_ast[j], i * 32)
                    nc.vector.tensor_tensor(astage[:, j, :], PS[:, b, :], abias[:, j, :], ALU.add)\
                        .then_inc(s_free[b], 1)

            rounds(dve, 3, ada)
            norm(0)
            dve.wait_ge(s_rconst, 16 * (2 + RH))

            def rotate(i):
                for j in range(2):
                    split_lo(SLOTS["ret_in"] + j + 1, i, 2)
                    for half in range(2):
                        n = 2 * j + half
                        b = take(UNITS["ret_in"] + n, i, 4)
                        dve.wait_ge(s_rot, i * 4 + max(n - 1, 0) if n else i * 4)
                        src = PS[:, b, :].rearrange("p (x t) -> p x t", x=2)
                        for table in range(2):
                            ins = nc.vector.tensor_tensor(
                                RT[:, n % 2, 512 * table:512 * (table + 1)].rearrange("p (x t) -> p x t", x=2),
                                src, rot[:, table:table + 1, :].broadcast_to([P, 2, S]), ALU.mult)
                        ins.then_inc(s_free[b], 1)

            rounds(dve, 2, rotate)
            for part in range(2):
                with dve.Fori(0, 2) as i:
                    for j in range(2):
                        split_lo(SLOTS["ret_in"] + 4 + 4 * part + j + 1, i, 2)
            u = UNITS["ret_heads"]
            for kind, h in RET_STEPS:
                if kind == "s":
                    b = take(u)
                    nc.vector.tensor_tensor(SC[:, h % 2, :], PS[:, b, 0:384], decay[:, h, :], ALU.mult)\
                        .then_inc(s_free[b], 1)
                elif kind == "o":
                    for tt in range(TT):
                        b = take(u + tt)
                        chain.done(nc.vector.bn_stats(bst[:, tt, :], PS[:, b, :]))
                        nc.vector.bn_aggr(bmv[:, tt, :], bst[:, tt, :]).then_inc(s_bn, 1)
                    dve.wait_ge(s_bnr, h + 1)
                    chain.done(nc.vector.reciprocal(bmv[:, :, 1:2], bmv[:, :, 1:2]))
                    for tt in range(TT):
                        b = unit(u + tt)[0]
                        if h:
                            dve.wait_ge(s_og, 2 * h - 1 + tt)
                        nc.vector.tensor_scalar(ON[:, tt, :], PS[:, b, :], bmv[:, tt, 0:1], bmv[:, tt, 1:2],
                                                ALU.subtract, ALU.mult).then_inc(s_free[b], 1)
                else:
                    for tt in range(TT):
                        transposed_lo(u + tt, OH, OL, tt, 4 * h)
                u += RET_UNITS[kind]
            for j in range(4):
                split_lo(SLOTS["ret_out"] + j + 1)
            post_norm(0)

            def ffn(name, last):
                base, ub, sbase = FFN_BASE[name], UNITS[name], SLOTS[name]

                def step(kind, n, s0, i=0):
                    split_lo(s0 + 1, i, 4, after(sbase, s0, last))
                    if kind == "in":
                        g, use = unit(ub + 2 * n, i, 4)
                        b = take(ub + 2 * n + 1, i, 4)
                        n, par = n + base, (n + base) % 2
                        dve.wait_ge(s_free[g], use + 1)
                        if n >= 2 or not isinstance(i, int):
                            dve.wait_ge(s_fp, i * 2 + n - 1)
                        nc.vector.tensor_tensor(fh[:, par, :], PS[:, b, :], fg[:, par, :], ALU.mult)\
                            .then_inc(s_fh, 1)
                        dve.wait_ge(s_fh, i * 2 + n + 1)
                        dve.sem_inc(s_free[b], 1)

                ffn_steps(dve, sbase, step)

            norm(1)
            ffn("ffn0", SLOT)
            post_norm(1)
            norm(2)
            chain.done(nc.vector.memset(UP[:, :, 0:3], 0.0))
            with dve.Fori(0, 3) as i:
                chain.enter(i, 2 * 9)
                for j in range(2):
                    split_lo(SLOTS["lru_in"] + j + 1, i, 2)
                    if j == 0:
                        continue
                    for half in range(2):
                        b = take(UNITS["lru_in"] + 2 + half, i, 4)
                        chain.done(nc.vector.tensor_copy(UP[:, 2 * half:2 * half + 2, 3:3 + S],
                                                         PS[:, b, :].rearrange("p (b t) -> p b t", b=2)))
                        dve.sem_inc(s_free[b], 1)
                        for q in range(2):
                            o = UC[:, bass.ds(i * 4 + (2 * half + q), 1), :]
                            col = lambda c: pcol[:, bass.ds(i * 4 + (c + 2 * half + q), 1)]
                            src = lambda tap: UP[:, 2 * half + q:2 * half + q + 1, tap:tap + S]
                            chain.done(nc.vector.tensor_scalar(o, src(0), col(PCW), col(PCB), ALU.mult, ALU.add))
                            for tap in range(1, 4):
                                ins = nc.vector.scalar_tensor_tensor(o, src(tap), col(PCW + 12 * tap), o,
                                                                     ALU.mult, ALU.add)
                                chain.done(ins)
                        dve.sem_inc(s_uc, 1)
            chain.leave(3)
            split_lo(SLOTS["lru_gate"] + 1, n=3072)
            for n in range(LB // 2):
                if n == 3:
                    split_lo(SLOTS["lru_out"])
                par, pair = n % 2, slice(2 * n, 2 * n + 2)
                dve.wait_ge(s_la, 4 * n + 4)
                chain.done(nc.vector.tensor_tensor(LQ[:, :], LA[:, par, :], LA[:, par, :], ALU.mult))
                chain.done(nc.vector.scalar_tensor_tensor(LQ[:, :], LQ[:, :], 1.0, LR[:, par, :], ALU.add, ALU.mult))
                nc.vector.tensor_scalar(LQ[:, :], LQ[:, :], 2.0 ** -100, None, ALU.max).then_inc(s_lq, 1)
                dve.wait_ge(s_liu, n + 1)
                dve.wait_ge(s_lmult, n + 1)
                chain.done(nc.vector.tensor_tensor(LI[:, par, :], LI[:, par, :], LQ[:, :], ALU.mult))
                for j in range(2):
                    at_ = slice(j * S, (j + 1) * S)
                    ins = nc.vector.tensor_tensor_scan(LQ[:, at_], LA[:, par, at_], LI[:, par, at_], 0.0,
                                                       ALU.mult, ALU.add)
                    chain.done(ins)
                nc.vector.tensor_tensor(UC[:, pair, :], LQ[:, :].rearrange("p (b t) -> p b t", b=2), Y[:, pair, :],
                                        ALU.mult).then_inc(s_lh, 1)
                dve.wait_ge(s_lh, n + 1)
            for j in range(3):
                split_lo(SLOTS["lru_out"] + j + 1)
            post_norm(2)
            norm(3)
            ffn("ffn1", SLOT)
            post_norm(3)
            def evacuated(u0, i=0, per=0):
                b, use = unit(u0, i, per)
                dve.wait_ge(s_free[b], use + 1)

            def modulated(name, src, hi, lo):
                scale, gain = row(), row()
                chain.done(nc.vector.scalar_tensor_tensor(scale, scale, 1.0, gain, ALU.add, ALU.mult))
                shift = row()
                inverse_rms()
                for tt in range(TT):
                    chain.done(nc.vector.scalar_tensor_tensor(XS[:, tt, :], src[:, tt, :], rs[:, tt:tt + 1], scale,
                                                              ALU.mult, ALU.mult))
                    chain.done(nc.vector.tensor_tensor(XS[:, tt, :], XS[:, tt, :], shift, ALU.add))
                    dve.sem_inc(s_xs, 1)
                dve.sem_inc(s_rowused, 3)
                for u in range(4):
                    transposed_lo(UNITS[name] + u, hi, lo, u // 2, 4 * (u % 2))

            chain.done(nc.vector.memset(eps2_col, 1e-12))
            chain.done(nc.vector.memset(eps3_col, 64e-5))
            modulated("norm_c", XC, CH, CL)
            modulated("norm_l", X, HH, HL)
            for j in range(1, len(MIX_SLOTS)):
                split_lo(SLOTS["mix_in"] + j, n=KT * MIX_SLOTS[j][1])
            U = lambda k, d, what, n=0: UNITS["rwkv"] + RW_UNIT[k, d, what, n]
            vec = lambda n: RWR[:, n * 256:(n + 1) * 256]
            dve.wait_ge(s_mix, 16 * 14)
            evacuated(UNITS["mix_in"] + len(MIX_UNITS) - 1)
            for u in range(8):
                t, d = divmod(u, 2)
                b = take(UNITS["decay"] + u)
                nc.vector.tensor_tensor(WA[:, t, d].rearrange("p a c -> p (a c)"), PS[:, b, :],
                                        RWR[:, 512 * d:512 * d + 512], ALU.add).then_inc(s_free[b], 1)
            chain.done(nc.vector.tensor_tensor(KK[:, :, :], ZK[:, :, :], vec(4).unsqueeze(1).broadcast_to([P, 4, 256]),
                                               ALU.mult))
            square = TR[0][:, :, :, :].rearrange("p a b c -> p a (b c)")
            chain.done(nc.vector.tensor_tensor(square, KK[:, :, :], KK[:, :, :], ALU.mult))
            nc.vector.tensor_reduce(kn, TR[0][:, :, :, :].rearrange("p a b (e j) -> p (a b e) j", j=64), AX_X, ALU.add)\
                .then_inc(s_kk, 1)
            for d in range(2):
                chain.done(nc.vector.memset(SB[d][:, :, :], 0.0))
                dve.sem_inc(s_st[d], 1)
            dve.wait_ge(s_sig, 8)
            for d in range(2):
                kd = KD[:, :, d * 256:(d + 1) * 256]
                chain.done(nc.vector.scalar_tensor_tensor(kd, WA[:, :, d, 1, :], -1.0,
                                                          vec(5).unsqueeze(1).broadcast_to([P, 4, 256]),
                                                          ALU.add, ALU.mult))
                chain.done(nc.vector.scalar_tensor_tensor(kd, kd, 1.0, ZK[:, :, :], ALU.add, ALU.mult))
            dve.wait_ge(s_kks, 1)
            chain.done(nc.vector.reciprocal(kn, kn))
            kk16 = KK[:, :, :].rearrange("p t (h j) -> p (t h) j", j=64)
            chain.done(nc.vector.tensor_tensor(kk16, kk16, kn.unsqueeze(2).broadcast_to([P, 16, 64]), ALU.mult))
            for d in range(2):
                chain.done(nc.vector.tensor_tensor(WA[:, :, d, 1, :], WA[:, :, d, 1, :], KK[:, :, :], ALU.mult))
            four = lambda m: m.unsqueeze(1).broadcast_to([P, 4, P])
            flat = lambda x: x[:, :, :, :].rearrange("p a b c -> p (a b) c")
            for k, d, t, what, n in RW_PLAN:
                mask = lambda m: MASK[:, 8 * d + m, :]
                level = None
                u = UNITS["rwkv"] + RW_UNIT[k, d, what, n] if what != "st" else None
                if what == "cum":
                    evacuated(u)
                    ep = EP[d][:, :, :, :].rearrange("p a b c -> p (a b c)")
                    en = EN[d][:, :, :, :].rearrange("p a b c -> p (a b c)")[:, 0:256]
                    nc.vector.tensor_tensor(BK[d][:, 1, :, :], KK[:, t, :].rearrange("p (h j) -> p h j", j=64),
                                            ep[:, 256:512].rearrange("p (h j) -> p h j", j=64), ALU.mult)
                    nc.vector.tensor_tensor(BE[d][:, :], WA[:, t, d, 1, :], en, ALU.mult)
                    ins = nc.vector.tensor_tensor(KR[d][:, :], KD[:, t, d * 256:(d + 1) * 256], en, ALU.mult)
                    if k >= 2:
                        ins = nc.vector.tensor_tensor(RH_[d][:, :], ZR[:, t - SEQ, :], ep[:, 0:256], ALU.mult)
                    ins.then_inc(s_rel, 1)
                elif what == "ab":
                    dve.wait_ge(s_aa, 4 * k + 2 * n + d + 1)
                    b = unit(u)[0]
                    nc.vector.tensor_tensor(BT[d][:, n, :, :], PS[:, b, 256:512].rearrange("p (a c) -> p a c", a=2),
                                            mask(6).unsqueeze(1).broadcast_to([P, 2, P]), ALU.mult)\
                        .then_inc(s_free[b], 1)
                elif what == "l":
                    b = take(u)
                    nc.vector.tensor_tensor(LL[d][:, n].rearrange("p a b c -> p (a b) c"),
                                            PS[:, b, :].rearrange("p (a c) -> p a c", a=4), four(mask(7)), ALU.mult)\
                        .then_inc(s_free[b], 1)
                elif what == "lev":
                    dve.wait_ge(s_rel, 2 * k + d + 1)
                    nc.vector.tensor_tensor(flat(AM[d]), flat(AA[d]), four(mask(0)), ALU.mult).then_inc(s_am, 1)
                    b = take(u)
                    nc.vector.tensor_tensor(flat(XX[d]), four(ident[:, :]), PS[:, b, :].rearrange("p (a c) -> p a c", a=4),
                                            ALU.subtract).then_inc(s_free[b], 1)
                elif what == "t":
                    nc.vector.tensor_tensor(flat(AM[d]), flat(AA[d]), four(mask(n)), ALU.mult).then_inc(s_am, 1)
                elif what == "xy":
                    b = take(u)
                    evacuated(U(k, d, "xy", n - 1) if n > 1 else U(k, d, "lev"))
                    nc.vector.tensor_tensor(flat(XX[d]), flat(XX[d]), PS[:, b, :].rearrange("p (a c) -> p a c", a=4),
                                            ALU.subtract).then_inc(s_free[b], 1)
                elif what == "mn":
                    b = take(u)
                    if k and n == 0:
                        dve.wait_ge(s_stp[d], 2 * k)
                    nc.vector.tensor_tensor(MN[d][:, n, :, :], PS[:, b, :].rearrange("p (a c) -> p a c", a=4),
                                            four(prow[:, :]), ALU.mult).then_inc(s_free[b], 1)
                elif what == "rt":
                    b = take(u)
                    nc.vector.tensor_tensor(RTt[d][:, :, :], PS[:, b, 0:256].rearrange("p (a c) -> p a c", a=2),
                                            TR[d][:, 3, :, :], ALU.add).then_inc(s_free[b], 1)
                elif what == "st" and (k, n) != (3, 1):
                    dve.wait_ge(s_stp[d], 2 * k + n + 1)
                    c = n ^ d
                    for hp in range(2):
                        ins = nc.vector.tensor_scalar(SB[d][:, hp, :], PS[:, 5 + d, hp * P:(hp + 1) * P],
                                                      PCD[:, t, d, hp, c:c + 1], None, ALU.mult)
                    ins.then_inc(s_st[d], 1)
            dve.wait_ge(s_y, 1)
            y = PS[:, 4, :].rearrange("p (g j) -> p g j", j=64)
            over = lambda c: c.unsqueeze(2).broadcast_to([P, 8, 64])
            groups = lambda x: x[:, :, :].rearrange("p t (h j) -> p (t h) j", j=64)
            both = lambda v: v.unsqueeze(1).broadcast_to([P, TT, 256])
            chain.done(nc.vector.tensor_reduce(gmu, y, AX_X, ALU.add))
            chain.done(nc.vector.tensor_scalar(gmu, gmu, 1.0 / 64, None, ALU.mult))
            chain.done(nc.vector.tensor_tensor(groups(RY), y, over(gmu), ALU.subtract))
            chain.done(nc.vector.tensor_tensor(RW2[:, :, :], RY[:, :, :], RY[:, :, :], ALU.mult))
            nc.vector.tensor_reduce(gvar, groups(RW2), AX_X, ALU.add).then_inc(s_gn, 1)
            dve.wait_ge(s_gn, 1)
            chain.done(nc.vector.tensor_tensor(RW2[:, :, :], ZR[:, :, :], ZK[:, SEQ:SEQ + 2, :], ALU.mult))
            chain.done(nc.vector.tensor_tensor(RW2[:, :, :], RW2[:, :, :], both(vec(6)), ALU.mult))
            chain.done(nc.vector.tensor_reduce(gsum, groups(RW2), AX_X, ALU.add))
            chain.done(nc.vector.tensor_tensor(groups(RW2), ZV[:, SEQ:SEQ + 2, :].rearrange("p t (h j) -> p (t h) j", j=64),
                                               over(gsum), ALU.mult))
            dve.wait_ge(s_gns, 1)
            chain.done(nc.vector.reciprocal(gvar, gvar))
            chain.done(nc.vector.tensor_tensor(groups(RY), groups(RY), over(gvar), ALU.mult))
            chain.done(nc.vector.tensor_tensor(RY[:, :, :], RY[:, :, :], both(vec(7)), ALU.mult))
            chain.done(nc.vector.tensor_tensor(RY[:, :, :], RY[:, :, :], RW2[:, :, :], ALU.add))
            b = take(UNITS["rw_gate"])
            chain.done(nc.vector.tensor_tensor(RY[:, :, :], RY[:, :, :], PS[:, b, :].rearrange("p (t c) -> p t c", t=TT),
                                               ALU.mult))
            dve.sem_inc(s_free[b], 1)
            dve.sem_inc(s_ry, 1)
            counts["xhi"] += 1
            dve.wait_ge(s_xhi, counts["xhi"])
            b = unit(UNITS["rw_out"])[0]
            nc.vector.tensor_tensor(HL[:, 0:2, :], PS[:, b, :].rearrange("p (k t) -> p k t", k=2),
                                    HH[:, 0:2, :].bitcast(F32), ALU.subtract).then_inc(s_free[b], 1)
            chain.done(nc.vector.memset(SP[:, :, 0:1], 0.0))
            chain.done(nc.vector.memset(SP[:, :, S + 1:S + 2], 0.0))
            chain.done(nc.vector.tensor_tensor(SP[:, :, 1:S + 1], SCZ[:, 2:4, :], SCZ[:, 4:6, :], ALU.mult))
            for blk in range(2):
                tap = lambda k: pcol[:, PSC + 2 * k + blk:PSC + 2 * k + blk + 1]
                o = SCZ[:, 4 + blk, :]
                chain.done(nc.vector.tensor_scalar(o, SP[:, blk, 0:S], tap(0), None, ALU.mult))
                for k in (1, 2):
                    chain.done(nc.vector.scalar_tensor_tensor(o, SP[:, blk, k:k + S], tap(k), o, ALU.mult, ALU.add))
            nc.vector.tensor_tensor(SCZ[:, 4:6, :], SCZ[:, 4:6, :], SCZ[:, 0:2, :], ALU.mult).then_inc(s_sc, 1)
            dve.wait_ge(s_sch, 1)
            nc.vector.tensor_tensor(HL[:, 6:8, :], SCZ[:, 4:6, :], HH[:, 6:8, :].bitcast(F32), ALU.subtract)\
                .then_inc(s_yt, 1)
            for i in range(NA_STEPS):
                b = take(UNITS["na"] + na_scores(i))
                if i >= 4:
                    dve.wait_ge(s_nx, i - 3)
                chain.done(nc.vector.tensor_reduce(nmax[i % 4], PS[:, b, :], AX_X, ALU.max))
                nc.vector.tensor_scalar(nmax[i % 4], nmax[i % 4], -(64 ** -0.5), None, ALU.mult).then_inc(s_ns, 1)
            dve.wait_ge(s_nx, NA_STEPS)
            chain.done(nc.vector.reciprocal(nsum, nsum))
            dve.wait_ge(s_no, 1)
            for tt in range(TT):
                nc.vector.tensor_tensor(NY[:, tt, :].rearrange("p (h j) -> p h j", j=64),
                                        PS[:, 5 + tt, :].rearrange("p (h j) -> p h j", j=64),
                                        nsum[:, 8 * tt:8 * tt + 8].unsqueeze(2).broadcast_to([P, 8, 64]), ALU.mult)\
                    .then_inc(s_ny, 1)
            for tt in range(TT):
                transposed_lo(UNITS["na_out"] + tt, HH, HL, tt, 2)
            for j in range(2):
                split_lo(SLOTS["mix_out"] + j)

            def gated_add(number):
                gate = row()
                dve.wait_ge(s_acc, number)
                for tt in range(TT):
                    nc.vector.tensor_tensor(XS[:, tt, :], PS[:, 4 + 2 * tt:6 + 2 * tt, :].rearrange("p h n -> p (h n)"),
                                            gate, ALU.mult).then_inc(s_accfree, 1)
                dve.wait_ge(s_accfree, 2 * number)
                dve.sem_inc(s_rowused, 1)
                for tt in range(TT):
                    nc.vector.tensor_tensor(X[:, tt, :], X[:, tt, :], XS[:, tt, :], ALU.add).then_inc(s_x, 1)

            gated_add(5)
            split_lo(SLOTS["peer_q"])
            dve.wait_ge(s_x, 10)
            modulated("norm_p", X, HH, HL)
            for j in range(3):
                split_lo(SLOTS["peer_q"] + j + 1)

            def top16(values, at_, src):
                for r in range(2):
                    half = slice(8 * r, 8 * r + 8)
                    chain.done(nc.vector.max(values[:, half], src))
                    ins = nc.vector.max_index(at_[:, half], values[:, half], src)
                    if r == 0:
                        chain.done(ins)
                        chain.done(nc.vector.match_replace(src, values[:, half], src, -3e38))
                return ins

            dve.wait_ge(s_iota, 16)
            for tt in range(TT):
                evacuated(UNITS["peer_s"] + 4 * tt + 3)
                for g in range(16):
                    chain.done(top16(TV[:, g, :], TX[:, g, :], PSC_[:, g, :]))
                dve.sem_inc(s_pd, 1)
                chain.done(nc.vector.tensor_copy(TF[:, :, :], TX[:, :, :]))
                tv = TV[:, :, :].rearrange("p (h s) k -> p h s k", s=2)
                tf = TF[:, :, :].rearrange("p (h s) k -> p h s k", s=2)
                chain.done(nc.vector.tensor_tensor(CAND[:, :, :, :], tv[:, :, 0, :].unsqueeze(3).broadcast_to([P, 8, 16, 16]),
                                                   tv[:, :, 1, :].unsqueeze(2).broadcast_to([P, 8, 16, 16]), ALU.add))
                for h in range(8):
                    chain.done(top16(CV[:, h, :], CX[:, h, :], CAND[:, h].rearrange("p a b -> p (a b)")))
                chain.done(nc.vector.tensor_scalar(CXH[:, 0], CX[:, :, :], 4, None, ALU.logical_shift_right))
                chain.done(nc.vector.tensor_scalar(CXH[:, 1], CX[:, :, :], 15, None, ALU.bitwise_and))
                chain.done(nc.vector.tensor_copy(CF[:, :, :, :], CXH[:, :, :, :]))
                chain.done(nc.vector.tensor_copy(CS[:, :], CV[:, :, 0]))
                nc.vector.tensor_tensor(CV[:, :, :], CV[:, :, :], CS[:, :].unsqueeze(2).broadcast_to([P, 8, 16]),
                                        ALU.subtract).then_inc(s_pm, 1)
                if tt:
                    evacuated(UNITS["picks"] + tt - 1)
                for s in range(2):
                    chain.done(nc.vector.tensor_tensor(EQ[:, :, :, :], CF[:, s].unsqueeze(3).broadcast_to([P, 8, 16, 16]),
                                                       IOTA[:, 0:16].unsqueeze(1).unsqueeze(1)
                                                       .broadcast_to([P, 8, 16, 16]), ALU.is_equal))
                    chain.done(nc.vector.tensor_tensor(EQ[:, :, :, :], EQ[:, :, :, :],
                                                       tf[:, :, s, :].unsqueeze(2).broadcast_to([P, 8, 16, 16]), ALU.mult))
                    chain.done(nc.vector.tensor_reduce(PK[:, s], EQ[:, :, :, :], AX_X, ALU.add))
                dve.wait_ge(s_pe, tt + 1)
                chain.done(nc.vector.tensor_reduce(CS[:, :], CV[:, :, :], AX_X, ALU.add))
                chain.done(nc.vector.reciprocal(CS[:, :], CS[:, :]))
                nc.vector.tensor_tensor(PK[:, 2], CV[:, :, :], CS[:, :].unsqueeze(2).broadcast_to([P, 8, 16]), ALU.mult)\
                    .then_inc(s_pk, 1)
                dve.wait_ge(s_pk, tt + 1)
            evacuated(UNITS["picks"] + TT - 1)
            with dve.Fori(0, S // 16) as i:
                for j in range(4):
                    half = slice(4 * (j % 2), 4 * (j % 2) + 4)
                    b, use = unit(UNITS["gates"] + j - 2, i, 4)
                    dve.wait_ge(s_full[b], use + 1)
                    token = lambda n, x: HKT[:, n, bass.ds(i * 16 + 4 * j + x, 1)]
                    nc.vector.tensor_tensor(ONE2[:, half, :], IOTA[:, :].unsqueeze(1).broadcast_to([P, 4, P]),
                                            HKT[:, 1, bass.ds(i * 16 + 4 * j, 4)].unsqueeze(2).broadcast_to([P, 4, P]),
                                            ALU.is_equal)
                    for x in range(4):
                        ins = nc.vector.tensor_scalar(ONE1[:, 4 * (j % 2) + x, :], IOTA[:, :], token(0, x), token(2, x),
                                                      ALU.is_equal, ALU.mult)
                    ins.then_inc(s_oh, 1)
            def u_low(j, i=0):
                b, use = j % 2, i + j // 2
                for h in range(2):
                    dve.wait_ge(s_uh[b], 2 * use + h + 1)
                    nc.vector.tensor_tensor(UTL[:, b, 4 * h:4 * h + 4, :], PS[:, h, :].rearrange("p (k e) -> p k e", k=4),
                                            UTH[:, b, 4 * h:4 * h + 4, :].bitcast(F32), ALU.subtract)\
                        .then_inc(s_ul[b], 1)

            def gate_and_v(j, i=0):
                b = j % 2
                dve.wait_ge(s_ag, 2 * i + j + 1)
                nc.vector.tensor_tensor(GA[:, b, :], GA[:, b, :],
                                        GT[:, bass.ds(2 * i + j, 1), :].rearrange("p a t -> p (a t)"), ALU.mult)\
                    .then_inc(s_aw, 1)
                dve.wait_ge(s_vh, 2 * i + j + 1)
                nc.vector.tensor_tensor(VL[:, b, :], VR[:, b, :], VH[:, b, :].bitcast(F32), ALU.subtract)\
                    .then_inc(s_vl, 1)

            peer_steps(dve, u_low, gate_and_v, None)
            gated_add(6)
            gain = row()
            inverse_rms()
            for tt in range(TT):
                nc.vector.scalar_tensor_tensor(XS[:, tt, :], X[:, tt, :], rs[:, tt:tt + 1], gain, ALU.mult, ALU.mult)\
                    .then_inc(s_x, 1)

        @block.tensor
        def _(pe):
            def mm3(o, ah, al, bh, bl, start, stop):
                nc.tensor.matmul(o, ah, bh, start=start, stop=False)
                nc.tensor.matmul(o, ah, bl, start=False, stop=False)
                return nc.tensor.matmul(o, al, bh, start=False, stop=stop)

            def free_bank(u0, i=0, per=0):
                b, use = unit(u0, i, per)
                pe.wait_ge(s_free[b], use)
                return b

            def evacuated(u0, i=0, per=0):
                b, use = unit(u0, i, per)
                pe.wait_ge(s_free[b], use + 1)

            def weights(s0, i=0, per=0):
                r, use = slot(s0, i, per)
                pe.wait_ge(s_wlo[r], use + 1)
                return r

            def wview(r, k=KT, n=None):
                n = n or SLOT
                return [w[:, r, 0:n].rearrange("p (k n) -> p k n", k=k) for w in (whi, wlo)]

            def t_unit(u0, i, per, wv, n0, blocks=2, hi=HH, lo=HL):
                b = free_bank(u0, i, per)
                for blk in range(blocks):
                    at_ = slice(n0 + blk * P, n0 + (blk + 1) * P)
                    for k in range(KT):
                        ins = mm3(PS[:, b, blk * S:(blk + 1) * S], wv[0][:, k, at_], wv[1][:, k, at_],
                                  hi[:, k, :], lo[:, k, :], k == 0, k == KT - 1)
                ins.then_inc(s_full[b], 1)
                return ins

            def n_unit(u0, i, per, wv, tt, n0=0, n=BANK, hi=HH, lo=HL):
                b = free_bank(u0, i, per)
                tok = slice(tt * P, (tt + 1) * P)
                for k in range(KT):
                    ins = mm3(PS[:, b, 0:n], hi[:, k, tok], lo[:, k, tok], wv[0][:, k, n0:n0 + n],
                              wv[1][:, k, n0:n0 + n], k == 0, k == KT - 1)
                ins.then_inc(s_full[b], 1)

            def used(r):
                pe.drain().then_inc(s_wused[r], 1)

            def transposes(n):
                for u in range(4):
                    tt = u // 2
                    if u % 2 == 0:
                        pe.wait_ge(s_xs, 2 * n + tt + 1)
                    b = free_bank(UNITS[f"norm{n}"] + u)
                    for j in range(4):
                        at_ = slice((4 * (u % 2) + j) * P, (4 * (u % 2) + j + 1) * P)
                        ins = nc.tensor.transpose(PS[:, b, j * P:(j + 1) * P], XS[:, tt, at_], ident[:, :])
                    ins.then_inc(s_full[b], 1)
                for u in range(4):
                    evacuated(UNITS[f"norm{n}"] + u)

            def into_acc(r, hi, lo, kts, first, last, w):
                for kk, kt in enumerate(kts):
                    for tt in range(TT):
                        tok = slice(tt * P, (tt + 1) * P)
                        for half in range(2):
                            at_ = slice(half * BANK, (half + 1) * BANK)
                            ins = mm3(acc(tt, half), hi[:, kt, tok], lo[:, kt, tok], w[0][:, kk, at_], w[1][:, kk, at_],
                                      first and kk == 0, last and kk == len(kts) - 1)
                return ins

            def project_acc(name, n_slots, hi, lo, number):
                for j in range(n_slots):
                    r = weights(SLOTS[name] + j)
                    if j == 0 and number:
                        pe.wait_ge(s_accfree, 2 * number)
                    ins = into_acc(r, hi, lo, range(4 * j, 4 * j + 4), j == 0, j == n_slots - 1, wview(r, 4))
                    ins.then_inc(s_wused[r], 1)
                pe.drain().then_inc(s_acc, 1)

            pe.wait_ge(s_const, 16 * 8)
            b = free_bank(UNITS["param"])
            nc.tensor.transpose(PS[:, b, 0:PROWS], prow[0:PROWS, :], ident[0:PROWS, 0:PROWS]).then_inc(s_full[b], 1)
            pe.wait_ge(s_cparts, 2)

            def ada(i):
                for j in range(4):
                    r = weights(SLOTS["ada"] + j, i, 4)
                    wv = wview(r)
                    b = free_bank(UNITS["ada"] + j, i, 4)
                    for k in range(KT):
                        ins = mm3(PS[:, b, :], ch[:, k, :], cl[:, k, :], wv[0][:, k, :], wv[1][:, k, :],
                                  k == 0, k == KT - 1)
                    ins.then_inc(s_full[b], 1)
                    used(r)

            rounds(pe, 3, ada)
            transposes(0)
            with pe.Fori(0, 2) as i:
                for j in range(2):
                    r = weights(SLOTS["ret_in"] + j, i, 2)
                    for half in range(2):
                        t_unit(UNITS["ret_in"] + 2 * j + half, i, 4, wview(r), half * 2 * P)
                    used(r)
            with pe.Fori(0, 4) as i:
                for j in range(2):
                    r = weights(SLOTS["ret_in"] + 4 + j, i, 2)
                    for tt in range(TT):
                        n_unit(UNITS["ret_in"] + 8 + 2 * j + tt, i, 4, wview(r), tt)
                    used(r)
            u = UNITS["ret_heads"]
            for kind, h in RET_STEPS:
                hd = slice(h * RDV, (h + 1) * RDV)
                if kind == "s":
                    if h == 0:
                        pe.wait_ge(s_rot, 8)
                    b = free_bank(u)
                    for at_, keys, queries in ((slice(0, S), slice(0, P), slice(0, S)),
                                               (slice(S, S + P), slice(P, S), slice(P, S))):
                        for x in range(2):
                            ins = nc.tensor.matmul(PS[:, b, at_], QK[:, 8 + 2 * h + x, keys],
                                                   QK[:, 2 * h + x, queries], start=x == 0, stop=x == 1)
                    ins.then_inc(s_full[b], 1)
                    scores_unit = {**(scores_unit if h else {}), h: u}
                elif kind == "o":
                    if h == 0:
                        for v in range(16):
                            evacuated(UNITS["ret_in"] + 8 + v)
                    evacuated(scores_unit[h])
                    b = free_bank(u)
                    nc.tensor.matmul(PS[:, b, :], SC[:, h % 2, 0:P], V[:, 0, hd], start=True, stop=True)\
                        .then_inc(s_full[b], 1)
                    b = free_bank(u + 1)
                    nc.tensor.matmul(PS[:, b, :], SC[:, h % 2, P:2 * P], V[:, 0, hd], start=True, stop=False)
                    nc.tensor.matmul(PS[:, b, :], SC[:, h % 2, 2 * P:3 * P], V[:, 1, hd], start=False, stop=True)\
                        .then_inc(s_full[b], 1)
                else:
                    for tt in range(TT):
                        pe.wait_ge(s_og, 2 * h + tt + 1)
                        b = free_bank(u + tt)
                        for j in range(4):
                            ins = nc.tensor.transpose(PS[:, b, j * P:(j + 1) * P],
                                                      SG[:, tt, h * RDV + j * P:h * RDV + (j + 1) * P], ident[:, :])
                        ins.then_inc(s_full[b], 1)
                u += RET_UNITS[kind]
            for v in range(8):
                evacuated(u - 8 + v)
            project_acc("ret_out", 4, OH, OL, 0)

            def ffn(name, number):
                base, ub, sbase = FFN_BASE[name], UNITS[name], SLOTS[name]

                def step(kind, n, s0, i=0):
                    r = weights(s0, i, 4)
                    if kind == "in":
                        for half in range(2):
                            t_unit(ub + 2 * n + half, i, 4, wview(r), half * 256)
                        used(r)
                        return
                    if n == 0:
                        pe.wait_ge(s_accfree, 2 * number)
                    first, last = n == 0, n == FI - 1
                    n, par = n + base, (n + base) % 2
                    pe.wait_ge(s_fp, i * 2 + n + 1)
                    into_acc(r, FH[:, par], FL[:, par], range(2), first, last, wview(r, 2, 2 * D))\
                        .then_inc(s_wused[r], 1)
                    pe.wait_ge(s_wused[r], slot(s0, i, 4)[1] + 1)
                    pe.sem_inc(s_fu, 1)

                ffn_steps(pe, sbase, step)
                pe.drain().then_inc(s_acc, 1)

            transposes(1)
            ffn("ffn0", 1)
            transposes(2)
            with pe.Fori(0, 3) as i:
                for j in range(2):
                    r = weights(SLOTS["lru_in"] + j, i, 2)
                    for half in range(2):
                        t_unit(UNITS["lru_in"] + 2 * j + half, i, 4, wview(r), half * 2 * P)
                    used(r)
            for n in range(LB // 2):
                if n % 3 == 0:
                    r = weights(SLOTS["lru_gate"] + n // 3)
                pe.wait_ge(s_up, n + 1)
                for g in range(2):
                    b = free_bank(UNITS["lru_gate"] + 2 * n + g)
                    for blk in range(2):
                        for k in range(2):
                            o = g * 1536 + (n % 3) * 512 + k * 256 + blk * P
                            ins = mm3(PS[:, b, blk * S:(blk + 1) * S], whi[:, r, o:o + P], wlo[:, r, o:o + P],
                                      UH[:, 2 * n + k, :], UL[:, 2 * n + k, :], k == 0, k == 1)
                    ins.then_inc(s_full[b], 1)
                if n % 3 == 2:
                    used(r)
            for n in range(LB // 2):
                pe.wait_ge(s_lp, n + 1)
            project_acc("lru_out", 3, UH, UL, 2)
            transposes(3)
            ffn("ffn1", 3)
            def normed_transposes(name, n):
                for u in range(4):
                    tt = u // 2
                    if u % 2 == 0:
                        pe.wait_ge(s_xs, 2 * n + tt + 1)
                    b = free_bank(UNITS[name] + u)
                    for j in range(4):
                        at_ = slice((4 * (u % 2) + j) * P, (4 * (u % 2) + j + 1) * P)
                        ins = nc.tensor.transpose(PS[:, b, j * P:(j + 1) * P], XS[:, tt, at_], ident[:, :])
                    ins.then_inc(s_full[b], 1)
                for u in range(4):
                    evacuated(UNITS[name] + u)

            normed_transposes("norm_c", 4)
            normed_transposes("norm_l", 5)
            tokens = ((CH, CL), (HH, HL))
            at_unit = UNITS["mix_in"]
            for j, (_, n_cols) in enumerate(MIX_SLOTS):
                r = weights(SLOTS["mix_in"] + j)
                wv = wview(r, n=KT * n_cols)
                for s, parts_, _ in MIX_UNITS:
                    if s != j:
                        continue
                    b, o = free_bank(at_unit), 0
                    for part in parts_:
                        if part[0] == "n":
                            _, t, c, n = part
                            hi, lo = tokens[t // 2]
                            tok = slice((t % 2) * P, (t % 2 + 1) * P)
                            for k in range(KT):
                                ins = mm3(PS[:, b, o:o + n], hi[:, k, tok], lo[:, k, tok], wv[0][:, k, c:c + n],
                                          wv[1][:, k, c:c + n], k == 0, k == KT - 1)
                            o += n
                        else:
                            _, c, t = part
                            hi, lo = tokens[t // 2]
                            for k in range(KT):
                                ins = mm3(PS[:, b, o:o + S], wv[0][:, k, c:c + P], wv[1][:, k, c:c + P], hi[:, k, :],
                                          lo[:, k, :], k == 0, k == KT - 1)
                            o += S
                    ins.then_inc(s_full[b], 1)
                    at_unit += 1
                used(r)
            pe.wait_ge(s_mix, 16 * 14)
            for v in range(4):
                evacuated(at_unit - 1 - v)
            for u in range(8):
                t, d = divmod(u, 2)
                b = free_bank(UNITS["decay"] + u)
                rows_, tok = slice(64 * d, 64 * d + 64), slice(t * P, (t + 1) * P)
                for j, x in enumerate((LWT, LAT)):
                    ins = nc.tensor.matmul(PS[:, b, j * 256:(j + 1) * 256], x[rows_, tok], LORA[rows_, j, :],
                                           start=True, stop=True)
                ins.then_inc(s_full[b], 1)
            b = free_bank(UNITS["chunk"])
            for u in range(8):
                t, d = divmod(u, 2)
                if u == 0:
                    pe.wait_ge(s_sig, 8)
                for hp in range(2):
                    ins = nc.tensor.matmul(PS[:, b, 4 * u + 2 * hp:4 * u + 2 * hp + 2], WA[:, t, d, 0, hp * P:(hp + 1) * P],
                                           chk, start=True, stop=True)
            ins.then_inc(s_full[b], 1)
            first_y = True
            for k, d, t, what, n in RW_PLAN:
                U = lambda what, n=0: UNITS["rwkv"] + RW_UNIT[k, d, what, n]
                quarter = lambda q: PS[:, b, q * P:(q + 1) * P]
                pairs = lambda x, kind, hp: x[d][:, kind, hp, :]
                if what == "st":
                    c = n ^ d
                    ch_ = slice(64 * c, 64 * c + 64)
                    if n == 0:
                        evacuated(U("mn", 0))
                        evacuated(U("mn", 1))
                        if k >= 2:
                            evacuated(U("rt"))
                    if k == 0 and n == 0:
                        evacuated(UNITS["chunk"])
                    pe.wait_ge(s_st[d], 2 * k + n + 1)
                    if k >= 2:
                        for hp in range(2):
                            o = (t - SEQ) * 256 + hp * P
                            nc.tensor.matmul(PS[ch_, 4, o:o + P], RTt[d][:, hp, ch_], SB[d][:, hp, :], start=False,
                                             stop=False, skip_group_check=True)
                    if (k, n) != (3, 1):
                        for hp in range(2):
                            o = PS[:, 5 + d, hp * P:(hp + 1) * P]
                            nc.tensor.matmul(o, ident[:, :], SB[d][:, hp, :], start=hp == 0, stop=False,
                                             skip_group_check=True)
                            nc.tensor.matmul(o, ident[:, :], MN[d][:, c, 2 + hp, :], start=False, stop=False,
                                             skip_group_check=True)
                            ins = nc.tensor.matmul(o, MN[d][:, c, hp, :], SB[d][:, hp, :], start=False, stop=hp == 1,
                                                   skip_group_check=True)
                        ins.then_inc(s_stp[d], 1)
                    continue
                b = free_bank(U(what, n))
                if what == "cum":
                    for j, m in enumerate((7, 6)):
                        ins = nc.tensor.matmul(PS[:, b, j * 256:(j + 1) * 256], MASK[:, 8 * d + m, :], WA[:, t, d, 0, :],
                                               start=True, stop=True)
                elif what == "tr":
                    if n == 0:
                        pe.wait_ge(s_rel, 2 * k + d + 1)
                    for j in range(2 if n and k < 2 else 4):
                        kind, hp = j // 2, j % 2
                        if (n, kind) == (0, 0):
                            src = BK[d][:, 1, 2 * hp:2 * hp + 2, :].rearrange("p h j -> p (h j)")
                        else:
                            src = ((None, BE[d]) if n == 0 else (KR[d], RH_[d]))[kind][:, hp * P:(hp + 1) * P]
                        ins = nc.tensor.transpose(quarter(j), src, ident[:, :])
                elif what in ("ab", "l"):
                    if (what, n) == ("ab", 0):
                        evacuated(U("tr", 0))
                        evacuated(U("tr", 1))
                    half = slice(64 * n, 64 * n + 64)
                    for j in range(4):
                        kind, hp = j // 2, j % 2
                        if what == "ab":
                            left, right = ((0, 1), (2, 0))[kind]
                        else:
                            left, right = ((1, 3), (2, 3))[kind]
                        ins = nc.tensor.matmul(quarter(j), TR[d][half, left, hp, :], TR[d][half, right, hp, :],
                                               start=True, stop=True)
                elif what == "bv":
                    evacuated(U("ab", 0))
                    evacuated(U("ab", 1))
                    for h in range(4):
                        ins = nc.tensor.matmul(PS[:, b, h * 64:(h + 1) * 64], BT[d][:, h % 2, h // 2, :],
                                               ZV[:, t, h * 64:(h + 1) * 64], start=True, stop=True)
                elif what == "lev":
                    pe.wait_ge(s_am, 12 * k + d + 1)
                    for j in range(4):
                        ins = nc.tensor.transpose(quarter(j), AM[d][:, j // 2, j % 2, :], ident[:, :])
                elif what == "t":
                    evacuated(U("xy", n - 1) if n > 1 else U("lev"))
                    for j in range(4):
                        ins = nc.tensor.transpose(quarter(j), XX[d][:, j // 2, j % 2, :], ident[:, :])
                elif what == "y":
                    pe.wait_ge(s_am, 12 * k + 2 * n + d + 1)
                    for j in range(4):
                        ins = nc.tensor.matmul(quarter(j), AM[d][:, j // 2, j % 2, :], XX[d][:, j // 2, j % 2, :],
                                               start=True, stop=True)
                elif what == "xy":
                    evacuated(U("t", n))
                    evacuated(U("y", n))
                    for j in range(4):
                        ins = nc.tensor.matmul(quarter(j), TI[d][:, j // 2, j % 2, :], YY[d][:, j // 2, j % 2, :],
                                               start=True, stop=True)
                elif what == "ug":
                    evacuated(U("xy", 5))
                    evacuated(U("bv"))
                    for h in range(4):
                        ins = nc.tensor.matmul(quarter(h), XX[d][:, h % 2, h // 2, :],
                                               BK[d][:, :, h, :], start=True, stop=True)
                elif what == "mn":
                    if n == 0:
                        evacuated(U("ug"))
                    half = slice(64 * n, 64 * n + 64)
                    for hp in range(2):
                        cols_ = slice(hp * P, (hp + 1) * P)
                        nc.tensor.matmul(quarter(hp), NUG[d][half, 1, 2 * hp:2 * hp + 2, :].rearrange("p h j -> p (h j)"), BE[d][half, cols_],
                                         start=True, stop=True)
                        nc.tensor.matmul(quarter(2 + hp), BE[d][half, cols_], NUG[d][half, 0, 2 * hp:2 * hp + 2, :].rearrange("p h j -> p (h j)"),
                                         start=True, stop=False)
                        ins = nc.tensor.matmul(quarter(2 + hp), KR[d][half, cols_], ZV[half, t, cols_],
                                               start=False, stop=True)
                elif what == "rt":
                    if k >= 2:
                        evacuated(U("l", 0))
                        evacuated(U("l", 1))
                    for h in range(4):
                        par, hp = h % 2, h // 2
                        o = PS[:, 4, (t - SEQ) * 256 + h * 64:(t - SEQ) * 256 + h * 64 + 64]
                        if first_y:
                            pe.wait_ge(s_accfree, 8)
                        nc.tensor.matmul(o, LL[d][:, par, 1, hp, :], ZV[:, t, h * 64:(h + 1) * 64], start=first_y,
                                         stop=False, skip_group_check=True)
                        first_y = False
                        nc.tensor.matmul(o, LL[d][:, par, 0, hp, :], NUG[d][:, 0, h, :], start=False, stop=False,
                                         skip_group_check=True)
                    for h in range(4):
                        par, hp = h % 2, h // 2
                        ins = nc.tensor.matmul(PS[64 * par:64 * par + 64, b, hp * P:(hp + 1) * P], NUG[d][:, 1, h, :],
                                               LL[d][:, par, 0, hp, :], start=True, stop=True, skip_group_check=True)
                ins.then_inc(s_full[b], 1)
            pe.drain().then_inc(s_y, 1)
            b = free_bank(UNITS["rw_gate"])
            for tt in range(TT):
                ins = nc.tensor.matmul(PS[:, b, tt * 256:(tt + 1) * 256], SGT[:, tt * P:(tt + 1) * P], LORA[:, 2, :],
                                       start=True, stop=True)
            ins.then_inc(s_full[b], 1)
            pe.wait_ge(s_ry, 1)
            b = free_bank(UNITS["rw_out"])
            for blk in range(2):
                for tt in range(TT):
                    o = (2 * blk + tt) * P
                    ins = nc.tensor.transpose(PS[:, b, o:o + P], RY[:, tt, blk * P:(blk + 1) * P], ident[:, :])
            ins.then_inc(s_full[b], 1)
            def na_score(i):
                qt, h = divmod(i, 8)
                half = slice(64 * (h % 2), 64 * (h % 2) + 64)
                b = free_bank(UNITS["na"] + na_scores(i))
                if h == 0:
                    pe.wait_ge(s_biasm, qt + 1)
                nc.tensor.matmul(PS[:, b, :], NQ[half, h // 2, qt * P:(qt + 1) * P], NK[half, h // 2, :],
                                 start=True, stop=False, skip_group_check=True)
                nc.tensor.matmul(PS[:, b, S:2 * S], FLIP[:, :], BIAS[:, qt, h, :], start=False, stop=True,
                                 skip_group_check=True).then_inc(s_full[b], 1)

            def na_turn(i):
                b = free_bank(UNITS["na"] + na_turned(i))
                pe.wait_ge(s_nx, i + 1)
                for j in range(4):
                    ins = nc.tensor.transpose(PS[:, b, j * P:(j + 1) * P], NS[:, i % 4, j * P:(j + 1) * P], ident[:, :])
                ins.then_inc(s_full[b], 1)

            def na_output(i):
                qt, h = divmod(i, 8)
                evacuated(UNITS["na"] + na_turned(i))
                for j in range(4):
                    nc.tensor.matmul(PS[:, 5 + qt, h * 64:(h + 1) * 64], NPT[:, i % 2, j * P:(j + 1) * P],
                                     NV[:, j, h * 64:(h + 1) * 64], start=(h, j) == (0, 0), stop=(h, j) == (7, 3),
                                     skip_group_check=True)

            na_score(0)
            for i in range(NA_STEPS):
                if i + 1 < NA_STEPS:
                    na_score(i + 1)
                na_turn(i)
                if i:
                    na_output(i - 1)
            na_output(NA_STEPS - 1)
            pe.drain().then_inc(s_no, 1)
            for tt in range(TT):
                pe.wait_ge(s_ny, tt + 1)
                b = free_bank(UNITS["na_out"] + tt)
                for j in range(4):
                    ins = nc.tensor.transpose(PS[:, b, j * P:(j + 1) * P], NY[:, tt, j * P:(j + 1) * P], ident[:, :])
                ins.then_inc(s_full[b], 1)
            evacuated(UNITS["rw_out"])
            for tt in range(TT):
                evacuated(UNITS["na_out"] + tt)
            pe.wait_ge(s_yt, 1)
            project_acc("mix_out", 2, HH, HL, 4)
            normed_transposes("norm_p", 6)
            for j in range(4):
                r = weights(SLOTS["peer_q"] + j)
                for half in range(2):
                    t_unit(UNITS["peer_q"] + 2 * j + half, 0, 0, wview(r), half * 2 * P)
                used(r)
            pe.wait_ge(s_keys, 16)
            for q in range(4):
                b = free_bank(UNITS["keys"] + q)
                for j in range(4):
                    ins = nc.tensor.transpose(PS[:, b, j * P:(j + 1) * P], KN[:, 4 * q + j, :], ident[:, :])
                ins.then_inc(s_full[b], 1)
            for q in range(4):
                evacuated(UNITS["keys"] + q)
            for tt in range(TT):
                for q in range(4):
                    b = free_bank(UNITS["peer_s"] + 4 * tt + q)
                    for j in range(4):
                        ins = nc.tensor.matmul(PS[:, b, j * P:(j + 1) * P], QT[:, 4 * q + j, tt * P:(tt + 1) * P],
                                               KTt[:, 4 * q + j, :], start=True, stop=True)
                    ins.then_inc(s_full[b], 1)
            for tt in range(TT):
                pe.wait_ge(s_pk, tt + 1)
                b = free_bank(UNITS["picks"] + tt)
                for j in range(3):
                    ins = nc.tensor.transpose(PS[:, b, j * P:(j + 1) * P], PK[:, j].rearrange("p h k -> p (h k)"),
                                              ident[:, :])
                ins.then_inc(s_full[b], 1)
            with pe.Fori(0, S // 16) as i:
                for j in range(4):
                    b = free_bank(UNITS["gates"] + j, i, 4)
                    pe.wait_ge(s_oh, i * 4 + j + 1)
                    for x in range(4):
                        s = 4 * (j % 2) + x
                        ins = nc.tensor.matmul(PS[:, b, x * P:(x + 1) * P], ONE2[:, s, :], ONE1[:, s, :],
                                               start=True, stop=True)
                    ins.then_inc(s_full[b], 1)
            for q in range(4):
                evacuated(UNITS["gates"] + S // 4 - 4 + q)
            def turn_u(j, i=0):
                b, use = j % 2, i + j // 2
                pe.wait_ge(s_ur[b], use * 16 + 16)
                for h in range(2):
                    if j or not isinstance(i, int):
                        pe.wait_ge(s_ul[1 - b], 2 * (i + (j - 1) // 2) + h + 1)
                    for q in range(4):
                        at_ = (4 * h + q) * P
                        ins = nc.tensor.transpose(PS[:, h, q * P:(q + 1) * P], UR[:, b, at_:at_ + P], ident[:, :])
                    ins.then_inc(s_ut[b], 1)

            def activations(j, i=0):
                b, use = j % 2, i + j // 2
                pe.wait_ge(s_ul[b], 2 * use + 2)
                if j >= 2 or not isinstance(i, int):
                    pe.wait_ge(s_ag, 2 * i + j - 1)
                for k in range(KT):
                    ins = mm3(PS[:, 2 + b, 0:S], UTH[:, b, k, :], UTL[:, b, k, :], HH[:, k, :], HL[:, k, :],
                              k == 0, k == KT - 1)
                ins.then_inc(s_ap, 1)

            def add_v(j, i=0):
                b = j % 2
                pe.wait_ge(s_as, 2 * i + j + 1)
                pe.wait_ge(s_vl, 2 * i + j + 1)
                if j == 0 and isinstance(i, int):
                    pe.wait_ge(s_accfree, 10)
                for tt in range(TT):
                    tok = slice(tt * P, (tt + 1) * P)
                    for half in range(2):
                        at_ = slice(half * BANK, (half + 1) * BANK)
                        ins = mm3(acc(tt, half), AH[:, b, tok], AL[:, b, tok], VH[:, b, at_], VL[:, b, at_],
                                  isinstance(i, int) and j == 0, isinstance(i, int) and j == P - 1)
                ins.then_inc(s_ao, 1)

            peer_steps(pe, turn_u, activations, add_v)
            pe.drain().then_inc(s_acc, 1)


_INS = ['x', 'ret_w_in', 'ret_w_out', 'lru_w_in', 'lru_conv_w', 'lru_conv_b', 'lru_gate_w', 'lru_gate_b',
        'lru_a_param', 'lru_w_out', 'norm_g', 'ffn_w_in', 'ffn_w_out', 'c_2', 'ctx_2', 'c_ctx_2', 'ada_w_2',
        'ada_b_2', 'norm1_g_2', 'norm2_g_2', 'w_in_2', 'rw_w0_2', 'rw_w_up_2', 'rw_a0_2', 'rw_a_up_2',
        'rw_g_up_2', 'rw_k_k_2', 'rw_k_a_2', 'rw_r_k_2', 'rw_lnx_g_2', 'na_rpb_2', 'sc_conv_w_2', 'w_out_2',
        'peer_q_w_2', 'peer_sub_keys_2', 'peer_u_2', 'peer_v_2', 'final_g_2']


def kernel(**inputs):
    import numpy as _np
    import concourse.bacc as _bacc
    from concourse import mybir as _mybir
    from concourse.bass_utils import run_bass_kernel_spmd as _run

    nc = _bacc.Bacc("TRN2", target_bir_lowering=False, num_devices=1,
                    dynamic_dma_scratch_size=8192)
    arrays, args = {}, {}
    for name in _INS:
        a = _np.ascontiguousarray(inputs[name])
        arrays[f"in_{name}_dram"] = a
        args[name] = nc.dram_tensor(f"in_{name}_dram", a.shape, _mybir.dt.from_np(a.dtype), kind="ExternalInput").ap()
    tables = _np.concatenate([_np.broadcast_to(CONST[n], (P, CONST[n].shape[1])) for n in CONST], axis=1)
    arrays["tables_dram"] = _np.ascontiguousarray(tables)
    consts = nc.dram_tensor("tables_dram", tables.shape, F32, kind="ExternalInput").ap()
    out = nc.dram_tensor("out_dram", (1, S, D), F32, kind="ExternalOutput").ap()
    mods = nc.dram_tensor("mods_dram", (2, 6 * D), F32, kind="Internal").ap()
    first_and_second_block(nc, args, consts, out, mods)
    r = _run(nc, [arrays], core_ids=[0])
    return r.results[0]["out_dram"]
```

```python
from contextlib import ExitStack

import concourse.bass as bass
import numpy as np
from concourse import mybir

ALU = mybir.AluOpType
ACT = mybir.ActivationFunctionType
AX_X = mybir.AxisListType.X
F32 = mybir.dt.float32
F32R = mybir.dt.float32r
U32 = mybir.dt.uint32

P = 128
D = 1024
S = 256
TT = S // P
KT = D // P
PIECES = 4
SLOT = 4096
BANK = 512
EPS = 1e-6
RH, RDK, RDV = 4, 256, 512
LRU_W = 1536
LB = LRU_W // P
D_FF = 2816
FI = D_FF // 256


def host_constants():
    f8, f4 = np.float64, np.float32
    out = {"ident": np.eye(P, dtype=f4)}
    half = RDK // 2
    inv = 1.0 / (10000.0 ** (np.arange(half, dtype=f4) / f4(half)))
    ang = (inv.astype(f4)[:, None] * np.arange(S, dtype=f4)[None, :]).astype(f4)
    out["cos"] = np.cos(ang.astype(f8)).astype(f4)
    out["sin"] = np.sin(ang.astype(f8)).astype(f4)
    s, t = np.arange(P)[:, None], np.arange(S)[None, :]
    for h in range(RH):
        lg = np.log1p(-np.exp2(-5.0 - h))
        full = np.where(t >= s, np.exp(np.maximum(t - s, 0) * lg), 0.0) * RDK ** -0.5
        out[f"decay{h}"] = np.concatenate([full, full[:, :P]], axis=1).astype(f4)
    a, b = np.arange(P)[:, None], np.arange(P)[None, :]
    same = a // 64 == b // 64
    for d in range(2):
        after = (lambda u, v: u > v) if d == 0 else (lambda u, v: u < v)
        for n in range(6):
            m = 1 << n
            out[f"level{d}{n}"] = ((a // (2 * m) == b // (2 * m)) & (a // m != b // m) & after(a, b)).astype(f4)
        out[f"strict{d}"] = (same & after(b, a)).astype(f4)
        out[f"incl{d}"] = (same & (after(b, a) | (a == b))).astype(f4)
    out["same"] = same.astype(f4)
    out["chunk"] = (a // 64 == np.arange(2)[None, :]).astype(f4)
    qc, kc = 63 - np.arange(P)[:, None] % 64, np.arange(64)[None, :]
    c0 = np.clip(qc - 8, 0, 48)
    ok = (kc >= c0) & (kc < c0 + 16)
    out["colok"] = ok.astype(f4)
    out["colno"] = np.where(ok, 0.0, -1e30).astype(f4)
    out["flip"] = np.where((a // 64 == b // 64) & (a % 64 + b % 64 == 63), 8.0, 0.0).astype(f4)
    out["iota"] = np.tile(np.arange(P, dtype=f4), (P, 1))
    return out


class Chain:

    def __init__(self, eng, sem):
        self.eng, self.sem, self.n, self.i, self.per = eng, sem, 0, None, 0

    def done(self, ins):
        ins.then_inc(self.sem, 1)
        self.n += 1
        self.eng.wait_ge(self.sem, self.n if self.i is None else self.i * self.per + self.n)

    def enter(self, i, per):
        self.i, self.per, self.start = i, per, self.n

    def leave(self, trips):
        assert self.n - self.start == self.per, (self.n - self.start, self.per)
        self.n, self.i = self.start + trips * self.per, None


PC, PCC, PCW, PCB, PGB, PAP, PSC = 0, 8, 16, 64, 76, 100, 112
PROWS = 118
CONST = host_constants()
CONST_AT = {}
for _name, _a in CONST.items():
    CONST_AT[_name] = (sum(n for _, n in CONST_AT.values()), _a.shape[1])
CONST_N = sum(n for _, n in CONST_AT.values())

SLOTS = {}
UNITS = {}
for _name, _n in [("ada", 12), ("ret_in", 12), ("ret_out", 4), ("ffn0", 2 * FI), ("lru_in", 6),
                  ("lru_gate", 2), ("lru_out", 3), ("ffn1", 2 * FI), ("mix_in", 7), ("mix_out", 2), ("peer_q", 4)]:
    SLOTS[_name] = sum(n for _, n in SLOTS.values()), _n
SLOTS = {k: v[0] for k, v in SLOTS.items()}
RET_STEPS = [("s", 0), ("s", 1), ("o", 0), ("s", 2), ("o", 1), ("s", 3), ("o", 2), ("o", 3),
             ("t", 0), ("t", 1), ("t", 2), ("t", 3)]
RET_UNITS = {"s": 1, "o": 2, "t": 2}
MIX_SLOTS = [(0, 512), (512, 512), (1024, 512), (1536, 512), (2048, 512), (2560, 512), (3072, 384)]
CTX, SEQ = 0, 2
MIX_UNITS = [
    (0, [("n", 2, 0, 512)], ("rk", 0)), (0, [("n", 3, 0, 512)], ("rk", 1)),
    (0, [("n", 0, 256, 256), ("n", 1, 256, 256)], ("k", CTX)),
    (1, [("n", 0, 0, 256), ("n", 1, 0, 256)], ("v", CTX)), (1, [("n", 2, 0, 256), ("n", 3, 0, 256)], ("v", SEQ)),
    (1, [("t", 256, CTX), ("t", 256, SEQ)], ("w", 0)), (1, [("t", 384, CTX), ("t", 384, SEQ)], ("a", 0)),
    (2, [("t", 0, SEQ)], ("g", 0)), (2, [("t", 128, SEQ), ("t", 256, SEQ)], ("q", 0)), (2, [("t", 384, SEQ)], ("q", 2)),
    (3, [("t", 0, SEQ)], ("q", 3)),
    *[(3, [("t", 128 + 128 * j, CTX), ("t", 128 + 128 * j, SEQ)], ("nk", j)) for j in range(3)],
    (4, [("t", 0, CTX), ("t", 0, SEQ)], ("nk", 3)),
    *[(4, [("n", t, 128, 384)], ("nv", t)) for t in range(4)],
    (5, [("n", t, 0, 128) for t in range(4)], ("nv3", 0)),
    (5, [("t", 128, SEQ), ("t", 256, SEQ)], ("z", 0)), (5, [("t", 384, SEQ)], ("z", 2)),
    (6, [("t", 0, SEQ), ("t", 128, SEQ)], ("z", 3)), (6, [("t", 256, SEQ)], ("z", 5)),
]


def rwkv_plan():
    st = lambda k, n: [(k, d, k ^ d, "st", n) for d in range(2)] if k >= 0 else []
    for k in range(4):
        work = ([("cum", 0), ("tr", 0), ("tr", 1), ("ab", 0), ("ab", 1)] + [("l", 0), ("l", 1)] * (k >= 2)
                + [("bv", 0), ("lev", 0)])
        for n in range(1, 6):
            work += [("t", n), ("y", n), ("xy", n)]
        work += [("ug", 0), ("mn", 0), ("mn", 1)] + [("rt", 0)] * (k >= 2)
        for what, n in work:
            for d in range(2):
                yield k, d, k ^ d, what, n
            if what in ("cum", "tr") and (what, n) != ("tr", 1):
                yield from st(k - 1, int(what == "tr"))
    yield from st(3, 0) + st(3, 1)


RW_PLAN = list(rwkv_plan())
RW_UNIT = {(k, d, what, n): u for u, (k, d, t, what, n) in enumerate(x for x in RW_PLAN if x[3] != "st")}
CDECAY = float(np.exp(-0.5))

for _name, _n in [("param", 1), ("ada", 12), ("norm0", 4), ("ret_in", 24), ("ret_heads", 20), ("norm1", 4),
                  ("ffn0", 2 * FI), ("norm2", 4), ("lru_in", 12), ("lru_gate", 12), ("norm3", 4),
                  ("ffn1", 2 * FI + 4), ("norm_l", 4), ("mix_in", len(MIX_UNITS)), ("decay", 8), ("chunk", 1),
                  ("rwkv", len(RW_UNIT)), ("rw_gate", 1), ("rw_out", 1), ("na", 32), ("na_out", 2), ("norm_p", 4),
                  ("peer_q", 8), ("keys", 4), ("peer_s", 8), ("gates", S // 4)]:
    UNITS[_name] = sum(n for _, n in UNITS.values()), _n
UNITS = {k: v[0] for k, v in UNITS.items()}
UNITS["norm_c"] = UNITS["ffn1"] + 4
ROWS = ([("norm", 0, n) for n in range(4)] + [("norm", 1, n) for n in range(3)]
        + [("mod", 1, 1), ("vec", "norm1_g_2", 1), ("mod", 1, 0), ("norm", 1, 3), ("mod", 0, 1), ("vec", "norm1_g_2", 1),
           ("mod", 0, 0), ("mod", 0, 2), ("mod", 0, 4), ("vec", "norm2_g_2", 1), ("mod", 0, 3), ("mod", 0, 5),
           ("vec", "final_g_2", 0)])
RB = 3


def unit(u0, i=0, per=0):
    return u0 % 4, i * (per // 4) + u0 // 4


def slot(s0, i=0, per=0):
    return s0 % 2, i * (per // 2) + s0 // 2


FFN_HEAD = [("in", 0), ("in", 1), ("out", 0)]
FFN_BODY = [("in", 2), ("out", 1), ("in", 3), ("out", 2)]
FFN_TAIL = [("in", FI - 1), ("out", FI - 2), ("out", FI - 1)]
FFN_TRIPS = (FI - 3) // 2
FFN_BASE = {"ffn0": 0, "ffn1": FI}
FFN_SIZE = {"in": SLOT, "out": 2 * D}


def ffn_steps(eng, base, step, chain=None, per=0, early=None, late=None):
    for k, (kind, n) in enumerate(FFN_HEAD):
        step(kind, n, base + k)
    if early:
        early()
    with eng.Fori(0, FFN_TRIPS) as i:
        if chain:
            chain.enter(i, per)
        for k, (kind, n) in enumerate(FFN_BODY):
            step(kind, n, base + len(FFN_HEAD) + k, i)
    if chain:
        chain.leave(FFN_TRIPS)
    if late:
        late()
    for k, (kind, n) in enumerate(FFN_TAIL):
        step(kind, n, base + 2 * FI - len(FFN_TAIL) + k)


def rounds(eng, trips, body):
    body(0)
    with eng.Fori(1, trips) as i:
        body(i)


def ffn_unit(name, n):
    return UNITS[name] + 2 * n + (4 if name == "ffn1" and n >= 2 else 0)


def after(base, s0, last):
    order = FFN_HEAD + FFN_BODY * FFN_TRIPS + FFN_TAIL
    n = s0 - base + 1
    return FFN_SIZE[order[n][0]] if n < len(order) else last


NA_STEPS = TT * 8


def na_scores(i):
    return max(2 * i - 1, 0)


def na_turned(i):
    return min(2 * i + 2, 2 * NA_STEPS - 1)


def peer_picks():
    for tt in range(TT):
        yield from [("keys", tt, g) for g in range(0, 16, 2)]
        yield from [("sums", tt, 0)] + [("picks", tt, h) for h in range(8)]
        yield from [("places", tt, 0), ("match", tt, 0), ("match", tt, 1), ("gate", tt, 0)]


PICKS = list(peer_picks())


def u_steps(eng, first, second, beside=None):
    first(0)
    n = len(PICKS) + 4
    assert n % 2 == 0
    for j in range(n):
        first(j + 1)
        second(j)
        if beside:
            beside(j)
    with eng.Fori(0, (P - n) // 2 - 1) as i:
        for j in (n, n + 1):
            first(j + 1, i)
            second(j, i)
    first(P - 1)
    second(P - 2)
    second(P - 1)


def v_steps(eng, first, second):
    first(0)
    for j in range(4):
        first(j + 1)
        second(j)
    with eng.Fori(0, P // 4 - 2) as i:
        for j in range(4, 8):
            first(j + 1, i)
            second(j, i)
    for j in range(P - 4, P):
        if j + 1 < P:
            first(j + 1)
        second(j)


def first_and_second_block(nc, A, consts, out, mods):
    cols = lambda name: consts[:, CONST_AT[name][0]:sum(CONST_AT[name])]
    with ExitStack() as ctx:
        def sb(name, shape, dt=F32, stack=ctx):
            return stack.enter_context(nc.sbuf_tensor(name, shape, dt))

        def sem(name):
            return ctx.enter_context(nc.semaphore(name))

        PS = ctx.enter_context(nc.psum_tensor("psum", [P, 8, BANK], F32))
        ident = sb("ident", [P, P])
        prow = sb("param_rows", [P, P])
        pcol = sb("param_cols", [P, PROWS])
        sq = sb("square_sums", [P, TT])
        rs = sb("inverse_rms", [P, TT])
        small = sb("small", [P, 192])
        X = sb("residual", [P, TT, D])
        xs_at = nc.sbuf_base
        XS = sb("normed", [P, TT, D])
        hh_at = nc.sbuf_base
        HH = sb("input_hi", [P, KT, S], F32R)
        HL = sb("input_lo", [P, KT, S], F32R)
        rows_at = nc.sbuf_base
        rows = sb("rows", [P, RB, D])
        wraw_at = nc.sbuf_base
        wraw = sb("weights", [P, 2, SLOT])
        whi_at = nc.sbuf_base
        whi = sb("weights_hi", [P, 2, SLOT], F32R)
        wlo = sb("weights_lo", [P, 2, SLOT], F32R)
        stage_at = nc.sbuf_base

        with ExitStack() as st:
            csilu = sb("c_silu", [P, 16], F32, st)
            ch = sb("c_hi", [P, KT, P], F32R, st)
            cl = sb("c_lo", [P, KT, P], F32R, st)
            abias = sb("ada_bias", [P, 4, BANK], F32, st)
            astage = sb("ada_rows", [P, 4, BANK], F32, st)
        with ExitStack() as st:
            QK = sb("qk", [P, 16, S], F32, st)
            V = sb("values", [P, TT, RH * RDV], F32, st)
            SG = sb("gate_silu", [P, TT, RH * RDV], F32, st)
            SC = sb("scores", [P, 2, 384], F32, st)
            rot = sb("rotary", [P, 2, S], F32, st)
            decay = sb("decay", [P, RH, 384], F32, st)
            ON = sb("head_normed", [P, TT, RDV], F32, st)
        with ExitStack() as st:
            OH = sb("ret_hi", [P, 16, S], F32R, st)
            OL = sb("ret_lo", [P, 16, S], F32R, st)
        RT = XS
        with ExitStack() as st:
            fg = sb("ffn_gate", [P, 2, BANK], F32, st)
            fh = sb("ffn_hidden", [P, 2, BANK], F32, st)
            FH = sb("ffn_hi", [P, 2, 2, S], F32R, st)
            FL = sb("ffn_lo", [P, 2, 2, S], F32R, st)
        with ExitStack() as st:
            Y = sb("lru_y", [P, LB, S], F32, st)
            UC = sb("lru_u", [P, LB, S], F32, st)
            UH = sb("lru_hi", [P, LB, S], F32R, st)
            UL = sb("lru_lo", [P, LB, S], F32R, st)
            with ExitStack() as st2:
                UP = sb("lru_padded", [P, 4, S + 3], F32, st2)
            LR = sb("lru_r", [P, 2, BANK], F32, st)
            LI = sb("lru_i", [P, 2, BANK], F32, st)
            LA = sb("lru_a", [P, 2, BANK], F32, st)
            LQ = sb("lru_q", [P, 2, BANK], F32, st)
        acol = small[:, 0:12]
        ancol = small[:, 12:24]
        at = [small[:, 24 + 12 * j:36 + 12 * j] for j in range(4)]
        eps_col, one_col = small[:, 82:83], small[:, 83:84]
        bst = small[:, 84:96].rearrange("p (t s) -> p t s", t=TT)
        bmv = small[:, 78:82].rearrange("p (t s) -> p t s", t=TT)

        class Region:

            def __init__(self, name, start, size):
                self.name, self.at, self.end = name, start, start + size

            def take(self, name, shape, dt=F32):
                size = 4 * int(np.prod(shape[1:]))
                size = -(-size // 32) * 32
                assert self.at + size <= self.end, (self.name, name, self.at + size - self.end)
                self.at += size
                return nc.alloc_sbuf_tensor_at(name, shape, dt, offset=self.at - size)

        KB = 1024
        stage = Region("stage", stage_at, nc.sbuf_usable_end // 32 * 32 - stage_at)
        ZR = stage.take("z_r", [P, TT, 256])
        ZK = stage.take("z_k", [P, 4, 256])
        ZV = stage.take("z_v", [P, 4, 256])
        LWT = stage.take("lora_w", [P, 2 * S])
        LAT = stage.take("lora_a", [P, 2 * S])
        SGT = stage.take("lora_g", [P, S])
        NQ = stage.take("na_q", [P, 4, S])
        NK = stage.take("na_k", [P, 4, 2 * S])
        NV = stage.take("na_v", [P, 4, 512])
        SCZ = stage.take("sc_z", [P, 6, S])
        split_at = stage.at
        CH = stage.take("context_hi", [P, KT, S], F32R)
        CL = stage.take("context_lo", [P, KT, S], F32R)
        XC = stage.take("context", [P, TT, D])
        again = Region("split context", split_at, stage.end - split_at)
        WA = again.take("decay_and_a", [P, 4, 2, 2, 256])
        KD = again.take("rw_k", [P, 4, 512])
        CKM = again.take("na_columns", [P, 2, 64])
        FLIP = again.take("na_flip", [P, P])
        again = Region("split context", split_at, stage.end - split_at)
        BIAS = again.take("na_bias", [P, TT, 8, S])
        ring = Region("ring", whi_at, 64 * KB)
        MASK = ring.take("masks", [P, 16, P])
        RWR = ring.take("rw_rows", [P, 2048])
        KK = ring.take("rw_kk", [P, 4, 256])
        LORA = ring.take("lora_up", [P, 3, 256])
        scratch = Region("idle rows", rows_at, RB * D * 4)
        xs_again = Region("idle scratch", xs_at, 8 * KB)
        BK = [ring.take(f"bv_kappa{d}", [P, 2, 4, 64]) for d in range(2)]
        BE = [ring.take(f"beta{d}", [P, 256]) for d in range(2)]
        KR = [ring.take(f"k_rel{d}", [P, 256]) for d in range(2)]
        RH_ = [ring.take(f"rho{d}", [P, 256]) for d in range(2)]
        TR = [ring.take(f"turned{d}", [P, 4, 2, P]) for d in range(2)]
        AA = [ring.take(f"a_raw{d}", [P, 2, 2, P]) for d in range(2)]
        XX = [ring.take(f"inv_t{d}", [P, 2, 2, P]) for d in range(2)]
        TI = [ring.take(f"inv{d}", [P, 2, 2, P]) for d in range(2)]
        BT = [ring.take(f"b_t{d}", [P, 2, 2, P]) for d in range(2)]
        LL = [xs_again.take(f"l_t{d}", [P, 2, 2, 2, P]) for d in range(2)]
        AM = [scratch.take(f"a_level{d}", [P, 2, 2, P]) for d in range(2)]
        YY = [scratch.take(f"a_x{d}", [P, 2, 2, P]) for d in range(2)]
        NUG = [scratch.take(f"minus_u_g{d}", [P, 2, 4, 64]) for d in range(2)]
        hh_again = Region("idle input", hh_at, 8 * KB)
        MN = [hh_again.take(f"m_n{d}", [P, 2, 4, P]) for d in range(2)]
        EP = AM
        EN = YY
        RTt = [ring.take(f"r_turned{d}", [P, 2, P]) for d in range(2)]
        SB = [ring.take(f"state{d}", [P, 2, P]) for d in range(2)]
        PCD = ring.take("chunk_decay", [P, 4, 2, 2, 2])
        SP = ring.take("sc_padded", [P, 2, S + 2])
        late = Region("masks, later", whi_at, 8 * KB)
        RY = late.take("rw_y", [P, TT, 256])
        RW2 = late.take("rw_y2", [P, TT, 256])
        RG = late.take("rw_gate", [P, TT, 256])
        scratch = Region("idle rows", rows_at, RB * D * 4)
        NS = scratch.take("na_scores", [P, 4, 512])
        NPT = scratch.take("na_probs_t", [P, 2, 512])
        xs_again = Region("idle scratch", xs_at, 8 * KB)
        NY = xs_again.take("na_y", [P, TT, 512])
        top = nc.sbuf_usable_end // 32 * 32
        stage = Region("stage, PEER", stage_at, top - stage_at)
        QT = stage.take("peer_queries", [P, 16, S])
        KN = stage.take("peer_keys", [P, 16, P])
        KTt = stage.take("peer_keys_t", [P, 16, P])
        PSC_ = [Region("idle scratch", xs_at, 8 * KB).take("peer_scores0", [P, 16, P]),
                stage.take("peer_scores1", [P, 16, P])]
        CAND = stage.take("peer_sums", [P, 8, 16, 16])
        TV = stage.take("top_values", [P, 16, 16])
        TX = stage.take("top_at", [P, 16, 16], U32)
        TF = stage.take("top_at_f", [P, 16, 16])
        CV = stage.take("pick_values", [P, 8, 16])
        CX = stage.take("pick_at", [P, 8, 16], U32)
        CXH = stage.take("pick_at_parts", [P, 2, 8, 16], U32)
        CF = stage.take("pick_at_f", [P, 2, 8, 16])
        PK = stage.take("picks", [P, 3, 8, 16])
        CS = stage.take("gate_sums", [P, 8])
        EQ = Region("keys, later", stage_at + 16 * KB, 8 * KB).take("pick_equal", [P, 8, 16, 16])
        at_table = top - 128 * KB
        GT = Region("activations", at_table, 128 * KB).take("act_table", [P, P, S])
        assert at_table + (len(PICKS) + 5) * KB <= stage_at
        low = Region("below the table", wraw_at, at_table - wraw_at)
        turned_at = low.at
        UR = low.take("u_rows", [P, 2, D])
        UTH = low.take("u_hi", [P, 2, KT, P], F32R)
        UTL = low.take("u_lo", [P, 2, KT, P], F32R)
        ONE1 = low.take("one_hot_first", [P, 8, P])
        ONE2 = low.take("one_hot_second", [P, 8, P])
        HKT = low.take("picks_t", [P, 3, S])
        IOTA = low.take("iota", [P, P])
        low = Region("where u was", turned_at, 24 * KB)
        VR = low.take("v_rows", [P, 4, D])
        AH = low.take("act_hi", [P, 2, S], F32R)
        AL = low.take("act_lo", [P, 2, S], F32R)
        GE = low.take("gates", [P, 2, 4, P])
        VH = Region("idle scratch", xs_at, 8 * KB).take("v_hi", [P, 2, D], F32R)
        VL = Region("idle rows", rows_at, 8 * KB).take("v_lo", [P, 2, D], F32R)
        eps2_col, eps3_col = small[:, 96:97], small[:, 97:98]
        kn = small[:, 98:114]
        gmu, gvar, gsum = small[:, 114:122], small[:, 122:130], small[:, 130:138]
        nmax = [small[:, 138 + j:139 + j] for j in range(4)]
        nsum = small[:, 142:158]
        chk = small[:, 158:160]

        s_mix = sem("s_mix")
        s_mask = sem("s_mask")
        s_ctx = sem("s_ctx")
        s_bias = sem("s_bias")
        s_sig = sem("s_sig")
        s_kk = sem("s_kk")
        s_kks = sem("s_kks")
        s_rel = sem("s_rel")
        s_aa = sem("s_aa")
        s_am = sem("s_am")
        s_stp = [sem(f"s_stp{d}") for d in range(2)]
        s_st = [sem(f"s_st{d}") for d in range(2)]
        s_y = sem("s_y")
        s_gn = sem("s_gn")
        s_gns = sem("s_gns")
        s_ry = sem("s_ry")
        s_sc = sem("s_sconv")
        s_sch = sem("s_sconvh")
        s_yt = sem("s_yt")
        s_biasm = sem("s_biasm")
        s_ns = sem("s_ns")
        s_nx = sem("s_nx")
        s_no = sem("s_no")
        s_ny = sem("s_ny")
        s_keys = sem("s_keys")
        s_iota = sem("s_iota")
        s_pm = sem("s_pm")
        s_pe = sem("s_pexp")
        s_pk = sem("s_pk")
        s_oh = sem("s_oh")
        s_ur = [sem(f"s_ur{b}") for b in range(2)]
        s_vr = [sem(f"s_vr{b}") for b in range(4)]
        s_ut = [sem(f"s_ut{b}") for b in range(2)]
        s_uh = [sem(f"s_uh{b}") for b in range(2)]
        s_ul = [sem(f"s_ul{b}") for b in range(2)]
        s_vh = sem("s_vh")
        s_vl = sem("s_vl")
        s_ap = sem("s_ap")
        s_ag = sem("s_ag")
        s_pt = sem("s_pt")
        s_hk = sem("s_hk")
        s_ge = sem("s_ge")
        s_gm = sem("s_gm")
        s_gbuf = sem("s_gbuf")
        s_ah = sem("s_ah")
        s_as = sem("s_as")
        s_go = sem("s_go")
        s_ao = sem("s_ao")

        s_const = sem("s_const")
        s_xload = sem("s_xload")
        s_full = [sem(f"s_full{b}") for b in range(4)]
        s_free = [sem(f"s_free{b}") for b in range(4)]
        s_wload = [sem(f"s_wload{r}") for r in range(2)]
        s_whi = [sem(f"s_whi{r}") for r in range(2)]
        s_wlo = [sem(f"s_wlo{r}") for r in range(2)]
        s_wused = [sem(f"s_wused{r}") for r in range(2)]
        s_row = [sem(f"s_row{r}") for r in range(RB)]
        s_rowused = sem("s_rowused")
        s_xhi = sem("s_xhi")
        s_sq = sem("s_sq")
        s_xs = sem("s_xs")
        s_x = sem("s_x")
        s_acc = sem("s_acc")
        s_accfree = sem("s_accfree")
        s_dve = sem("s_dve")
        s_act = sem("s_act")
        s_pool = sem("s_pool")
        s_csilu = sem("s_csilu")
        s_cparts = sem("s_cparts")
        s_abias = [sem(f"s_abias{b}") for b in range(4)]
        s_amod = [sem(f"s_amod{b}") for b in range(4)]
        s_ast = [sem(f"s_ast{b}") for b in range(4)]
        s_rconst = sem("s_rconst")
        s_rotp = sem("s_rotp")
        s_rot = sem("s_rot")
        s_sc = sem("s_sc")
        s_og = sem("s_og")
        s_fg = sem("s_fg")
        s_fh = sem("s_fh")
        s_fp = sem("s_fp")
        s_fu = sem("s_fu")
        s_pcol = sem("s_pcol")
        s_uc = sem("s_uc")
        s_up = sem("s_up")
        s_alog = sem("s_alog")
        s_acol = sem("s_acol")
        s_lg = sem("s_lg")
        s_la = sem("s_la")
        s_liu = sem("s_liu")
        s_lh = sem("s_lh")
        s_lp = sem("s_lp")
        s_rs = sem("s_rs")
        s_bn = sem("s_bn")
        s_bnr = sem("s_bnr")
        s_lq = sem("s_lq")
        s_lmult = sem("s_lmult")
        s_eps = sem("s_eps")
        s_out = sem("s_out")

        FFN = [("ffn0", 0), ("ffn1", 1)]
        acc = lambda tt, half: PS[:, 4 + 2 * tt + half, :]
        W = {n: A[n][0].rearrange("(k p) n -> p k n", p=P)
             for n in ("ret_w_in", "ret_w_out", "lru_w_in", "lru_w_out", "ada_w_2", "w_in_2", "w_out_2", "peer_q_w_2")}
        ffn_in = [A["ffn_w_in"][l].rearrange("(k p) n -> p k n", p=P) for l in range(2)]
        ffn_out = [A["ffn_w_out"][l].rearrange("(k p) n -> p k n", p=P) for l in range(2)]
        
        block = ctx.enter_context(nc.Block())

        @block.sync
        def _(sp):
            def load(s0, parts, i=0, per=0):
                r, use = slot(s0, i, per)
                sp.wait_ge(s_wlo[r], use)
                for off, k, n, src in parts:
                    dst = wraw[:, r, off:off + k * n].rearrange("p (k n) -> p k n", k=k)
                    sp.dma_start(dst, src).then_inc(s_wload[r], 16)

            def wide(s0, w, n0, i=0, per=0, istep=0):
                view = w[:, :, bass.ds(i * istep + n0, BANK)]
                load(s0, [(0, 4, BANK, view[:, 0:4, :]), (4 * BANK, 4, BANK, view[:, 4:8, :])], i, per)

            def deep(s0, w, k0):
                load(s0, [(0, 2, D, w[:, k0:k0 + 2, :]), (2 * D, 2, D, w[:, k0 + 2:k0 + 4, :])])

            sp.dma_start(ident[:, :], cols("ident")).then_inc(s_const, 16)
            as_rows = lambda a: a.rearrange("(r p) -> r p", p=P)
            for at_, src in [(PC, A["c_2"][0].rearrange("(r p) -> r p", p=P)), (PCC, as_rows(A["c_ctx_2"])),
                             (PCW, A["lru_conv_w"][0].rearrange("j (b p) -> (j b) p", p=P)),
                             (PCB, as_rows(A["lru_conv_b"][0])),
                             (PGB, A["lru_gate_b"][0].rearrange("g n (j p) -> (g n j) p", p=P)),
                             (PAP, as_rows(A["lru_a_param"][0])),
                             (PSC, A["sc_conv_w_2"][0].rearrange("j (b p) -> (j b) p", p=P))]:
                sp.dma_start(prow[at_:at_ + src.shape[0], :], src).then_inc(s_const, 16)

            def ada(i):
                for j in range(4):
                    wide(SLOTS["ada"] + j, W["ada_w_2"], j * BANK, i, 4, 4 * BANK)

            ada(0)
            sp.dma_start(X[:, :, :], A["x"][0].rearrange("(t p) d -> p t d", p=P)).then_inc(s_xload, 16)
            with sp.Fori(1, 3) as i:
                ada(i)
            for name, n in (("cos", 0), ("sin", 1)):
                sp.dma_start(rot[:, n, :], cols(name)).then_inc(s_rconst, 16)
            for h in range(RH):
                sp.dma_start(decay[:, h, :], cols(f"decay{h}")).then_inc(s_rconst, 16)
            with sp.Fori(0, 6) as i:
                for j in range(2):
                    wide(SLOTS["ret_in"] + j, W["ret_w_in"], j * BANK, i, 2, 2 * BANK)
            for j in range(4):
                deep(SLOTS["ret_out"] + j, W["ret_w_out"], 4 * j)

            def ffn(name, layer):
                def step(kind, n, s0, i=0):
                    r, use = slot(s0, i, 4)
                    sp.wait_ge(s_wlo[r], use)
                    for j in range(2):
                        if kind == "in":
                            dst = wraw[:, r, :].rearrange("p (k n) -> p k n", k=KT)[:, :, j * 256:(j + 1) * 256]
                            src = ffn_in[layer][:, :, bass.ds(i * 512 + n * 256 + j * D_FF, 256)]
                        else:
                            dst = wraw[:, r, j * D:(j + 1) * D]
                            src = A["ffn_w_out"][layer][bass.ds(i * 512 + (2 * n + j) * P, P), :]
                        sp.dma_start(dst, src).then_inc(s_wload[r], 16)

                def load_context():
                    sp.wait_ge(s_acc, 6)
                    sp.dma_start(XC[:, :, :], A["ctx_2"][0].rearrange("(t p) d -> p t d", p=P)).then_inc(s_ctx, 16)

                ffn_steps(sp, SLOTS[name], step, early=load_context if name == "ffn1" else None)

            ffn("ffn0", 0)
            with sp.Fori(0, 3) as i:
                for j in range(2):
                    wide(SLOTS["lru_in"] + j, W["lru_w_in"], j * LRU_W, i, 2, BANK)
            for j in range(2):
                r, use = slot(SLOTS["lru_gate"] + j)
                sp.wait_ge(s_wlo[r], use)
                for g in range(2):
                    dst = wraw[:, r, g * 1536:(g + 1) * 1536].rearrange("p (n k m) -> p n k m", n=3, k=2)
                    src = A["lru_gate_w"][0, g, 3 * j:3 * j + 3].rearrange("n (k p) m -> p n k m", p=P)
                    sp.dma_start(dst, src).then_inc(s_wload[r], 16)
            for j in range(3):
                deep(SLOTS["lru_out"] + j, W["lru_w_out"], 4 * j)
            ffn("ffn1", 1)
            for j, (c0, n) in enumerate(MIX_SLOTS):
                r, use = slot(SLOTS["mix_in"] + j)
                sp.wait_ge(s_wlo[r], use)
                dst = wraw[:, r, 0:KT * n].rearrange("p (k n) -> p k n", k=KT)
                for h in range(2):
                    sp.dma_start(dst[:, 4 * h:4 * h + 4, :], W["w_in_2"][:, 4 * h:4 * h + 4, c0:c0 + n])\
                        .then_inc(s_wload[r], 16)
            for j in range(2):
                deep(SLOTS["mix_out"] + j, W["w_out_2"], 4 * j)
            for j in range(2):
                r, use = slot(SLOTS["mix_in"] + 5 + j)
                sp.wait_ge(s_wused[r], use + 1)
            for n, (name, d) in enumerate([("rw_w0_2", 0), ("rw_a0_2", 0), ("rw_w0_2", 1), ("rw_a0_2", 1)]):
                sp.dma_start(RWR[:, n * 256:(n + 1) * 256], A[name][0, d].partition_broadcast(P)).then_inc(s_mix, 16)
            for n, name in enumerate(["rw_k_k_2", "rw_k_a_2", "rw_r_k_2", "rw_lnx_g_2"]):
                src = A[name][0].rearrange("h j -> (h j)") if name == "rw_r_k_2" else A[name][0]
                sp.dma_start(RWR[:, (4 + n) * 256:(5 + n) * 256], src.partition_broadcast(P)).then_inc(s_mix, 16)
            sp.dma_start(LORA[:, 0, :], A["rw_w_up_2"][0].rearrange("d r c -> (d r) c")).then_inc(s_mix, 16)
            sp.dma_start(LORA[:, 1, :], A["rw_a_up_2"][0].rearrange("d r c -> (d r) c")).then_inc(s_mix, 16)
            sp.dma_start(LORA[:, 2, :], A["rw_g_up_2"][0]).then_inc(s_mix, 16)
            sp.dma_start(chk, cols("chunk")).then_inc(s_mix, 16)
            sp.dma_start(prow[:, :], cols("same")).then_inc(s_mix, 16)
            sp.dma_start(MASK[:, :, :], consts[:, CONST_AT["level00"][0]:CONST_AT["same"][0]]
                         .rearrange("p (m n) -> p m n", n=P)).then_inc(s_mask, 16)
            sp.dma_start(CKM[:, 0, :], cols("colok")).then_inc(s_bias, 16)
            sp.dma_start(CKM[:, 1, :], cols("colno")).then_inc(s_bias, 16)
            sp.dma_start(FLIP[:, :], cols("flip")).then_inc(s_bias, 16)
            sp.wait_ge(s_rel, 8)
            rpb = A["na_rpb_2"]
            for qr in range(4):
                half, qt = qr % 2, qr // 2
                for kr in range(4):
                    src = bass.AP(rpb.tensor, (kr - qr + 7) * 31 + 15 - 63, [[1, 64], [465, 8], [1, 64]])
                    sp.dma_start(BIAS[64 * half:64 * half + 64, qt, :, 64 * kr:64 * kr + 64], src)\
                        .then_inc(s_bias, 16)
            for j in range(4):
                wide(SLOTS["peer_q"] + j, W["peer_q_w_2"], j * BANK)
            sp.wait_ge(s_acc, 10)
            sp.dma_start(KN[:, :, :], A["peer_sub_keys_2"][0].rearrange("h p n d -> n (h p) d")).then_inc(s_keys, 16)
            for j in (2, 3):
                r, use = slot(SLOTS["peer_q"] + j)
                sp.wait_ge(s_wused[r], use + 1)
            sp.dma_start(IOTA[:, :], cols("iota")).then_inc(s_iota, 16)
            u_tab, v_tab = A["peer_u_2"][0], A["peer_v_2"][0]

            def load_u(j, i=0):
                b = j % 2
                if j >= 2 or not isinstance(i, int):
                    sp.wait_ge(s_ut[b], i * 2 + 2 * (j // 2))
                sp.dma_start(UR[:, b, :], u_tab[bass.ds(i * 256 + j * P, P), :]).then_inc(s_ur[b], 16)

            def load_v(j, i=0):
                if j >= 4 or not isinstance(i, int):
                    sp.wait_ge(s_vl, i * 4 + j - 3)
                sp.dma_start(VR[:, j % 4, :], v_tab[bass.ds(i * 512 + j * P, P), :]).then_inc(s_vr[j % 4], 16)

            load_u(0)
            load_u(1)
            with sp.Fori(0, P // 2 - 1) as i:
                load_u(2, i)
                load_u(3, i)
            sp.wait_ge(s_ag, P)
            for j in range(4):
                load_v(j)
            with sp.Fori(0, P // 4 - 1) as i:
                for j in range(4, 8):
                    load_v(j, i)
            sp.wait_ge(s_x, 12 + 2)
            sp.dma_start(out[0].rearrange("(t p) d -> p t d", p=P), XS[:, :, :]).then_inc(s_out, 16)
            sp.wait_ge(s_out, 16)

        @block.gpsimd
        def _(pool):
            chain = Chain(pool, s_pool)

            def evacuated(u0, i=0, per=0):
                b, use = unit(u0, i, per)
                pool.wait_ge(s_free[b], use + 1)

            def load_rows(first, last):
                for r in range(first, last):
                    if r >= RB:
                        pool.wait_ge(s_rowused, r - RB + 1)
                    pool.dma_start(rows[:, r % RB, :], row_source(r).partition_broadcast(P))\
                        .then_inc(s_row[r % RB], 16)

            def row_source(r):
                kind, a, b = ROWS[r]
                if kind == "norm":
                    return A["norm_g"][a, b]
                if kind == "vec":
                    return A[a][0] if b else A[a]
                return mods[a, b * D:(b + 1) * D]

            def parts(hi, lo, src, semaphore):
                ones = one_col.unsqueeze(2).broadcast_to([P, 2, S])
                chain.done(nc.gpsimd.tensor_tensor(hi, src, ones, ALU.mult))
                nc.gpsimd.tensor_tensor(lo, src, hi.bitcast(F32), ALU.subtract).then_inc(semaphore, 1)

            chain.done(nc.gpsimd.memset(one_col, 1.0))
            load_rows(0, RB)
            for i in range(3):
                for j in range(4):
                    at_ = slice((4 * i + j) * BANK, (4 * i + j + 1) * BANK)
                    evac = UNITS["ada"] + 4 * (i - 1) + j
                    if i:
                        evacuated(evac)
                    pool.dma_start(abias[:, j, :], A["ada_b_2"][0, at_].partition_broadcast(P))\
                        .then_inc(s_abias[j], 16)
                for j in range(4):
                    at_ = slice((4 * i + j) * BANK, (4 * i + j + 1) * BANK)
                    evacuated(UNITS["ada"] + 4 * i + j)
                    for half in range(2):
                        pool.dma_start(mods[half:half + 1, at_], astage[64 * half:64 * half + 1, j, :])\
                            .then_inc(s_ast[j], 16)
            with pool.Fori(0, 2) as i:
                for j in range(4):
                    evacuated(UNITS["ret_in"] + j, i, 4)
                    pc = RT[:, j % 2, 0:512].rearrange("p (x t) -> p x t", x=2)
                    ps = RT[:, j % 2, 512:1024].rearrange("p (x t) -> p x t", x=2)
                    nc.gpsimd.tensor_tensor(QK[:, bass.ds(i * 8 + 2 * j, 1), :], pc[:, 0:1, :], ps[:, 1:2, :],
                                            ALU.subtract)
                    nc.gpsimd.tensor_tensor(QK[:, bass.ds(i * 8 + (2 * j + 1), 1), :], ps[:, 0:1, :],
                                            pc[:, 1:2, :], ALU.add).then_inc(s_rot, 1)
            u = UNITS["ret_heads"]
            for kind, h in RET_STEPS:
                if kind == "o":
                    for tt in range(TT):
                        evacuated(u + tt)
                        og = SG[:, tt, h * RDV:(h + 1) * RDV]
                        nc.gpsimd.tensor_tensor(og, og, ON[:, tt, :], ALU.mult).then_inc(s_og, 1)
                u += RET_UNITS[kind]

            def ffn(name):
                base = FFN_BASE[name]

                def step(kind, n, s0, i=0):
                    if kind == "in":
                        n, par = n + base, (n + base) % 2
                        pool.wait_ge(s_fh, i * 2 + n + 1)
                        if n >= 2 or not isinstance(i, int):
                            pool.wait_ge(s_fu, i * 2 + n - 1)
                        parts(FH[:, par], FL[:, par], fh[:, par, :].rearrange("p (b t) -> p b t", b=2), s_fp)

                ffn_steps(pool, SLOTS[name], step, chain, 2, late=lambda: name == "ffn1" and load_rows(10, 13))

            load_rows(RB, 4)
            load_rows(4, 5)
            load_rows(5, 6)
            ffn("ffn0")
            load_rows(6, 7)
            load_rows(7, 8)
            for n in range(LB // 2):
                pool.wait_ge(s_uc, n + 1)
                pair = slice(2 * n, 2 * n + 2)
                parts(UH[:, pair, :], UL[:, pair, :], UC[:, pair, :], s_up)
            for n in range(LB // 2):
                pair = slice(2 * n, 2 * n + 2)
                evacuated(UNITS["lru_gate"] + 2 * n + 1)
                li = LI[:, n % 2, :].rearrange("p (b t) -> p b t", b=2)
                nc.gpsimd.tensor_tensor(li, li, UC[:, pair, :], ALU.mult).then_inc(s_liu, 1)
                pool.wait_ge(s_lh, n + 1)
                parts(UH[:, pair, :], UL[:, pair, :], UC[:, pair, :], s_lp)
            load_rows(8, 10)
            ffn("ffn1")
            load_rows(13, 14)
            for qt in range(TT):
                if qt == 0:
                    pool.wait_ge(s_bias, 16 * 19)
                table = BIAS[:, qt, :, :].rearrange("p h (r c) -> p (h r) c", c=64)
                for j, op in enumerate((ALU.mult, ALU.add)):
                    mask = CKM[:, j:j + 1, :].broadcast_to([P, 32, 64])
                    ins = nc.gpsimd.tensor_tensor(table, table, mask, op)
                    if j == 0:
                        chain.done(ins)
                ins.then_inc(s_biasm, 1)
            evacuated(UNITS["na_out"] + 1)
            load_rows(14, 18)
            def gate_four(j, i):
                pool.wait_ge(s_ge, i * 4 + j + 1)
                pool.sem_inc(s_go, 1)
                at_ = GT[:, :, bass.ds(i * 16 + 4 * j, 4)]
                nc.gpsimd.tensor_tensor(at_, at_, GE[:, j % 2].rearrange("p t n -> p n t"), ALU.mult).then_inc(s_gm, 1)

            pool.wait_ge(s_ag, P)
            pool.sem_inc(s_gbuf, 2)
            with pool.Fori(0, S // 16) as i:
                for j in range(4):
                    gate_four(j, i)
                    pool.wait_ge(s_gm, i * 4 + j + 1)
                    pool.sem_inc(s_gbuf, 1)

            pool.wait_ge(s_ao, P)
            load_rows(18, 20)

        @block.scalar
        def _(act):
            counts = {"sq": 0}

            def split_hi(s0, i=0, per=0, n=SLOT):
                r, use = slot(s0, i, per)
                act.wait_ge(s_wload[r], use * 32 + 32)
                act.wait_ge(s_wused[r], use)
                for piece in range(PIECES):
                    at_ = slice(piece * n // PIECES, (piece + 1) * n // PIECES)
                    nc.scalar.activation(whi[:, r, at_], wraw[:, r, at_], ACT.Copy).then_inc(s_whi[r], 1)

            def take(u0, i=0, per=0):
                b, use = unit(u0, i, per)
                act.wait_ge(s_full[b], use + 1)
                return b

            def squares(src, ready=None, count=0):
                for tt in range(TT):
                    if ready is not None:
                        act.wait_ge(ready, count + tt + 1)
                    nc.scalar.activation(XS[:, tt, :], src[:, tt], ACT.Square, scale=D ** -0.5,
                                         accum_out=sq[:, tt:tt + 1]).then_inc(s_sq, 1)
                    counts["sq"] += 1
                    act.wait_ge(s_sq, counts["sq"])
                    nc.scalar.activation(rs[:, tt:tt + 1], sq[:, tt:tt + 1], ACT.Sqrt, bias=eps_col).then_inc(s_rs, 1)

            def transposed_hi(u, dst, tt, k0):
                b = take(u)
                nc.scalar.activation(dst[:, k0:k0 + 4, tt * P:(tt + 1) * P],
                                     PS[:, b, :].rearrange("p (k t) -> p k t", k=4), ACT.Copy).then_inc(s_xhi, 1)

            def norm(n, dst=HH):
                if n == 0:
                    act.wait_ge(s_eps, 1)
                    act.wait_ge(s_xload, 16)
                    squares(X)
                else:
                    squares(X, s_x, 2 * n - 2)
                for u in range(4):
                    transposed_hi(UNITS[f"norm{n}"] + u, dst, u // 2, 4 * (u % 2))

            def post_norm(n):
                squares(PS[:, 4:8, :].rearrange("p (t h) n -> p t (h n)", t=TT), s_acc, 2 * n)

            act.wait_ge(s_pcol, 1)
            nc.scalar.activation(csilu[:, :], pcol[:, PC:PC + 16], ACT.Silu).then_inc(s_csilu, 1)
            nc.scalar.activation(at[0], pcol[:, PAP:PAP + 12], ACT.Abs).then_inc(s_alog, 1)
            act.wait_ge(s_alog, 1)
            nc.scalar.activation(at[0], at[0], ACT.Exp, scale=-1.0).then_inc(s_alog, 1)
            act.wait_ge(s_acol, 1)
            nc.scalar.activation(at[2], at[1], ACT.Ln).then_inc(s_alog, 1)
            split_hi(0)

            def ada(i):
                for j in range(4):
                    split_hi(SLOTS["ada"] + j + 1, i, 4)

            rounds(act, 3, ada)
            norm(0)
            with act.Fori(0, 2) as i:
                for j in range(2):
                    split_hi(SLOTS["ret_in"] + j + 1, i, 2)
            for b in range(4):
                act.wait_ge(s_ast[b], 16 * 2 * 3)
            for part, (dst, func) in enumerate(((V, ACT.Copy), (SG, ACT.Silu))):
                with act.Fori(0, 2) as i:
                    for j in range(2):
                        split_hi(SLOTS["ret_in"] + 4 + 4 * part + j + 1, i, 2)
                        for tt in range(TT):
                            b = take(UNITS["ret_in"] + 8 + 8 * part + 2 * j + tt, i, 4)
                            nc.scalar.activation(dst[:, tt, bass.ds(i * 2 * BANK + j * BANK, BANK)],
                                                 PS[:, b, :], func).then_inc(s_free[b], 1)
            u = UNITS["ret_heads"]
            for kind, h in RET_STEPS:
                if kind == "o":
                    act.wait_ge(s_bn, 2 * h + 2)
                    nc.scalar.activation(bmv[:, :, 1:2], bmv[:, :, 1:2], ACT.Sqrt, bias=eps_col).then_inc(s_bnr, 1)
                elif kind == "t":
                    for tt in range(TT):
                        transposed_hi(u + tt, OH, tt, 4 * h)
                u += RET_UNITS[kind]
            for j in range(4):
                split_hi(SLOTS["ret_out"] + j + 1)
            post_norm(0)

            def ffn(name, last):
                base, sbase = FFN_BASE[name], SLOTS[name]

                def step(kind, n, s0, i=0):
                    split_hi(s0 + 1, i, 4, after(sbase, s0, last))
                    if kind == "in":
                        b = take(ffn_unit(name, n), i, 4)
                        n, par = n + base, (n + base) % 2
                        if n >= 2 or not isinstance(i, int):
                            act.wait_ge(s_fh, i * 2 + n - 1)
                        nc.scalar.activation(fg[:, par, :], PS[:, b, :], ACT.Silu).then_inc(s_free[b], 1)

                def context():
                    act.wait_ge(s_ctx, 16)
                    squares(XC)
                    for u in range(4):
                        transposed_hi(UNITS["norm_c"] + u, CH, u // 2, 4 * (u % 2))

                ffn_steps(act, sbase, step, early=context if name == "ffn1" else None)

            norm(1)
            ffn("ffn0", SLOT)
            post_norm(1)
            norm(2)
            with act.Fori(0, 3) as i:
                for j in range(2):
                    split_hi(SLOTS["lru_in"] + j + 1, i, 2)
                    if j == 0:
                        for half in range(2):
                            b = take(UNITS["lru_in"] + half, i, 4)
                            nc.scalar.activation(Y[:, bass.ds(i * 4 + 2 * half, 2), :],
                                                 PS[:, b, :].rearrange("p (b t) -> p b t", b=2),
                                                 ACT.Gelu_apprx_tanh).then_inc(s_free[b], 1)
            split_hi(SLOTS["lru_gate"] + 1, n=3072)
            act.wait_ge(s_uc, LB // 2)
            for group in range(LB // 4):
                pairs = (2 * group, 2 * group + 1)
                for n in pairs:
                    par = n % 2
                    if n >= 2:
                        act.wait_ge(s_lh, n - 1)
                    for g, dst in enumerate((LR, LI)):
                        b = take(UNITS["lru_gate"] + 2 * n + g)
                        for j in range(2):
                            at_, c = slice(j * S, (j + 1) * S), PGB + 12 * g + 2 * n + j
                            ins = nc.scalar.activation(dst[:, par, at_], PS[:, b, at_], ACT.Sigmoid,
                                                       bias=pcol[:, c:c + 1])
                        ins.then_inc(s_free[b], 1)
                if group >= 1:
                    split_hi(SLOTS["lru_out"] + group - 1)
                for n in pairs:
                    par = n % 2
                    b, use = unit(UNITS["lru_gate"] + 2 * n)
                    act.wait_ge(s_free[b], use + 1)
                    for j in range(2):
                        at_, c = slice(j * S, (j + 1) * S), slice(2 * n + j, 2 * n + j + 1)
                        nc.scalar.activation(LA[:, par, at_], LR[:, par, at_], ACT.Exp, scale=acol[:, c])\
                            .then_inc(s_la, 1)
                    act.wait_ge(s_la, 4 * n + 2)
                    for j in range(2):
                        at_, c = slice(j * S, (j + 1) * S), slice(2 * n + j, 2 * n + j + 1)
                        nc.scalar.activation(LR[:, par, at_], LR[:, par, at_], ACT.Tanh, scale=ancol[:, c])\
                            .then_inc(s_la, 1)
                for n in pairs:
                    act.wait_ge(s_lq, n + 1)
                    nc.scalar.activation(LQ[:, n % 2, :], LQ[:, n % 2, :], ACT.Sqrt).then_inc(s_lmult, 1)
            for j in range(1, 3):
                split_hi(SLOTS["lru_out"] + j + 1)
            post_norm(2)
            norm(3)
            ffn("ffn1", SLOT)
            post_norm(3)
            def evacuated(u0, i=0, per=0):
                b, use = unit(u0, i, per)
                act.wait_ge(s_free[b], use + 1)

            def out_of(u, dst, func=ACT.Copy, src=None, **kw):
                b = take(u)
                src = PS[:, b, :] if src is None else src(PS[:, b, :])
                nc.scalar.activation(dst, src, func, **kw).then_inc(s_free[b], 1)

            squares(X, s_x, 6)
            for u in range(4):
                transposed_hi(UNITS["norm_l"] + u, HH, u // 2, 4 * (u % 2))
            at_unit = UNITS["mix_in"]
            for j, (_, n_cols) in enumerate(MIX_SLOTS):
                if j + 1 < len(MIX_SLOTS):
                    split_hi(SLOTS["mix_in"] + j + 1, n=KT * MIX_SLOTS[j + 1][1])
                for s, parts_, (where, n) in MIX_UNITS:
                    if s != j:
                        continue
                    first = lambda size: lambda ps: ps[:, 0:size]
                    two = lambda ps: ps.rearrange("p (a b) -> p a b", a=2)
                    if where == "rk":
                        b = take(at_unit)
                        nc.scalar.activation(ZR[:, n, :], PS[:, b, 0:256], ACT.Copy)
                        nc.scalar.activation(ZK[:, SEQ + n, :], PS[:, b, 256:512], ACT.Copy).then_inc(s_free[b], 1)
                    elif where == "k":
                        out_of(at_unit, ZK[:, n:n + 2, :], src=two)
                    elif where == "v":
                        out_of(at_unit, ZV[:, n:n + 2, :], src=two)
                    elif where == "w":
                        out_of(at_unit, LWT[:, :], ACT.Tanh)
                    elif where == "a":
                        out_of(at_unit, LAT[:, :])
                    elif where == "g":
                        out_of(at_unit, SGT[:, :], ACT.Sigmoid, src=first(S))
                    elif where == "nk":
                        out_of(at_unit, NK[:, n, :])
                    elif where == "nv":
                        out_of(at_unit, NV[:, n, 0:384], src=first(384))
                    elif where == "nv3":
                        out_of(at_unit, NV[:, :, 384:512], src=lambda ps: ps.rearrange("p (t n) -> p t n", t=4))
                    else:
                        dst, count = NQ if where == "q" else SCZ, len(parts_)
                        out_of(at_unit, dst[:, n:n + count, :], src=lambda ps, count=count:
                               ps[:, 0:count * S].rearrange("p (a b) -> p a b", a=count))
                    at_unit += 1
            for u in range(8):
                t, d = divmod(u, 2)
                evacuated(UNITS["decay"] + u)
                nc.scalar.activation(WA[:, t, d], WA[:, t, d], ACT.Sigmoid).then_inc(s_sig, 1)
            act.wait_ge(s_kk, 1)
            nc.scalar.activation(kn, kn, ACT.Sqrt, bias=eps2_col).then_inc(s_kks, 1)
            out_of(UNITS["chunk"], PCD[:, :, :, :, :].rearrange("p t d h c -> p (t d h c)"), ACT.Exp,
                   src=lambda ps: ps[:, 0:32], scale=-CDECAY)
            U = lambda k, d, what, n=0: UNITS["rwkv"] + RW_UNIT[k, d, what, n]
            for k, d, t, what, n in RW_PLAN:
                if what == "st":
                    continue
                u = U(k, d, what, n)
                if what == "cum":
                    b = take(u)
                    if k:
                        evacuated(U(k - 1, d, "mn", 1))
                    if k == 3:
                        evacuated(U(2, d, "rt"))
                    nc.scalar.activation(EP[d][:, :, :, :].rearrange("p a b c -> p (a b c)"), PS[:, b, :], ACT.Exp,
                                         scale=-CDECAY)
                    nc.scalar.activation(EN[d][:, :, :, :].rearrange("p a b c -> p (a b c)")[:, 0:256],
                                         PS[:, b, 0:256], ACT.Exp, scale=CDECAY).then_inc(s_free[b], 1)
                elif what == "tr":
                    size = 1 if n and k < 2 else 2
                    out_of(u, TR[d][:, 2 * n:2 * n + size, :, :].rearrange("p a b c -> p (a b c)"),
                           src=lambda ps, size=size: ps[:, 0:256 * size])
                elif what == "ab":
                    b = take(u)
                    nc.scalar.activation(AA[d][:, n, :, :].rearrange("p a b -> p (a b)"), PS[:, b, 0:256], ACT.Copy)\
                        .then_inc(s_aa, 1)
                elif what == "bv":
                    out_of(u, BK[d][:, 0, :, :], src=lambda ps: ps[:, 0:256].rearrange("p (h j) -> p h j", h=4))
                elif what == "t":
                    out_of(u, TI[d][:, :, :, :].rearrange("p a b c -> p (a b c)"))
                elif what == "y":
                    if n == 1:
                        act.wait_ge(s_rel, 2 * k + d + 1)
                    out_of(u, YY[d][:, :, :, :].rearrange("p a b c -> p (a b c)"))
                elif what == "ug":
                    for kind in range(2):
                        b = take(u)
                        ins = nc.scalar.activation(NUG[d][:, kind, :, :], PS[:, b, :]
                                                   .rearrange("p (h a j) -> p a h j", h=4, a=2)[:, kind], ACT.Copy,
                                                   scale=-1.0)
                    ins.then_inc(s_free[b], 1)
            act.wait_ge(s_gn, 1)
            nc.scalar.activation(gvar, gvar, ACT.Sqrt, bias=eps3_col, scale=1.0 / 64).then_inc(s_gns, 1)
            b = take(UNITS["rw_out"])
            nc.scalar.activation(HH[:, 0:2, :], PS[:, b, :].rearrange("p (k t) -> p k t", k=2), ACT.Copy)\
                .then_inc(s_xhi, 1)
            act.wait_ge(s_sc, 1)
            nc.scalar.activation(HH[:, 6:8, :], SCZ[:, 4:6, :], ACT.Copy).then_inc(s_sch, 1)

            for i in range(NA_STEPS):
                if i >= 4:
                    evacuated(UNITS["na"] + na_turned(i - 4))
                act.wait_ge(s_ns, i + 1)
                b = unit(UNITS["na"] + na_scores(i))[0]
                nc.scalar.activation(NS[:, i % 4, :], PS[:, b, :], ACT.Exp, bias=nmax[i % 4], scale=64 ** -0.5,
                                     accum_out=nsum[:, i:i + 1]).then_inc(s_nx, 1)
                act.wait_ge(s_nx, i + 1)
                act.sem_inc(s_free[b], 1)
                if i:
                    out_of(UNITS["na"] + na_turned(i - 1), NPT[:, (i - 1) % 2, :])
            out_of(UNITS["na"] + na_turned(NA_STEPS - 1), NPT[:, (NA_STEPS - 1) % 2, :])
            for tt in range(TT):
                transposed_hi(UNITS["na_out"] + tt, HH, tt, 2)
            evacuated(UNITS["na_out"] + 1)
            for j in range(2):
                split_hi(SLOTS["mix_out"] + j)
            split_hi(SLOTS["peer_q"])
            squares(X, s_x, 8)
            for u in range(4):
                transposed_hi(UNITS["norm_p"] + u, HH, u // 2, 4 * (u % 2))
            for j in range(4):
                if j < 3:
                    split_hi(SLOTS["peer_q"] + j + 1)
                for half in range(2):
                    at_ = 4 * j + 2 * half
                    out_of(UNITS["peer_q"] + 2 * j + half, QT[:, at_:at_ + 2, :],
                           src=lambda ps: ps.rearrange("p (a b) -> p a b", a=2))
            quarter = lambda ps: ps.rearrange("p (a b) -> p a b", a=4)
            for q in range(4):
                out_of(UNITS["keys"] + q, KTt[:, 4 * q:4 * q + 4, :], src=quarter)

            for tt in range(TT):
                for q in range(4):
                    out_of(UNITS["peer_s"] + 4 * tt + q, PSC_[tt][:, 4 * q:4 * q + 4, :], src=quarter)

            def u_high(j, i=0):
                b, use = j % 2, i + j // 2
                if j >= 2 or not isinstance(i, int):
                    act.wait_ge(s_ap, 2 * i + j - 1)
                for h in range(2):
                    act.wait_ge(s_ut[b], 2 * use + h + 1)
                    nc.scalar.activation(UTH[:, b, 4 * h:4 * h + 4, :], PS[:, h, :].rearrange("p (k e) -> p k e", k=4),
                                         ACT.Copy).then_inc(s_uh[b], 1)

            def gelu(j, i=0):
                act.wait_ge(s_ap, 2 * i + j + 1)
                nc.scalar.activation(GT[:, bass.ds(2 * i + j, 1), :], PS[:, 2 + j % 2:3 + j % 2, 0:S],
                                     ACT.Gelu_apprx_tanh).then_inc(s_ag, 1)

            def beside(j):
                if j < len(PICKS) and PICKS[j][0] == "places":
                    act.wait_ge(s_pm, PICKS[j][1] + 1)
                    nc.scalar.activation(CV[:, :, :], CV[:, :, :], ACT.Exp).then_inc(s_pe, 1)
                if j >= 2 and j - 2 < len(PICKS) and PICKS[j - 2][0] == "gate":
                    tt = PICKS[j - 2][1]
                    act.wait_ge(s_pt, tt + 1)
                    nc.scalar.activation(HKT[:, :, tt * P:(tt + 1) * P],
                                         PS[:, 4 + tt, 0:3 * P].rearrange("p (a b) -> p a b", a=3), ACT.Copy)\
                        .then_inc(s_hk, 1)

            u_steps(act, u_high, gelu, beside)
            with act.Fori(0, S // 16) as i:
                for j in range(4):
                    b = take(UNITS["gates"] + j, i, 4)
                    act.wait_ge(s_gbuf, i * 4 + j + 1)
                    nc.scalar.activation(GE[:, j % 2].rearrange("p t n -> p (t n)"), PS[:, b, :], ACT.Copy)\
                        .then_inc(s_ge, 1)
                    act.wait_ge(s_ge, i * 4 + j + 1)
                    act.sem_inc(s_free[b], 1)

            act.wait_ge(s_gm, S // 4)

            def high(j, i=0):
                if j >= 2 or not isinstance(i, int):
                    act.wait_ge(s_ao, 4 * i + j - 1)
                nc.scalar.activation(AH[:, j % 2:j % 2 + 1, :], GT[:, bass.ds(4 * i + j, 1), :], ACT.Copy)\
                    .then_inc(s_ah, 1)
                act.wait_ge(s_vr[j % 4], (i + j // 4) * 16 + 16)
                for half in range(2):
                    at_ = slice(half * BANK, (half + 1) * BANK)
                    nc.scalar.activation(VH[:, j % 2, at_], VR[:, j % 4, at_], ACT.Copy).then_inc(s_vh, 1)

            v_steps(act, high, lambda *a: None)
            squares(X, s_x, 10)

        @block.vector
        def _(dve):
            chain = Chain(dve, s_dve)
            counts = {"rs": 0, "xhi": 0, "row": 0}

            def split_lo(s0, i=0, per=0, n=SLOT):
                r, use = slot(s0, i, per)
                for piece in range(PIECES):
                    at_ = slice(piece * n // PIECES, (piece + 1) * n // PIECES)
                    dve.wait_ge(s_whi[r], use * PIECES + piece + 1)
                    ins = nc.vector.tensor_tensor(wlo[:, r, at_], wraw[:, r, at_], whi[:, r, at_].bitcast(F32),
                                                  ALU.subtract)
                ins.then_inc(s_wlo[r], 1)

            def take(u0, i=0, per=0):
                b, use = unit(u0, i, per)
                dve.wait_ge(s_full[b], use + 1)
                return b

            def row():
                r = counts["row"]
                counts["row"] += 1
                dve.wait_ge(s_row[r % RB], 16 * (r // RB + 1))
                return rows[:, r % RB, :]

            def inverse_rms(tt):
                counts["rs"] += 1
                dve.wait_ge(s_rs, counts["rs"])
                chain.done(nc.vector.reciprocal(rs[:, tt:tt + 1], rs[:, tt:tt + 1]))

            def transposed_lo(u, hi, lo, tt, k0):
                b = unit(u)[0]
                counts["xhi"] += 1
                dve.wait_ge(s_xhi, counts["xhi"])
                at_ = (slice(None), slice(k0, k0 + 4), slice(tt * P, (tt + 1) * P))
                nc.vector.tensor_tensor(lo[at_], PS[:, b, :].rearrange("p (k t) -> p k t", k=4),
                                        hi[at_].bitcast(F32), ALU.subtract).then_inc(s_free[b], 1)

            def norm(n):
                gain = row()
                for tt in range(TT):
                    inverse_rms(tt)
                    nc.vector.scalar_tensor_tensor(XS[:, tt, :], X[:, tt, :], rs[:, tt:tt + 1], gain,
                                                   ALU.mult, ALU.mult).then_inc(s_xs, 1)
                dve.wait_ge(s_xs, 2 * n + 2)
                dve.sem_inc(s_rowused, 1)
                for u in range(4):
                    transposed_lo(UNITS[f"norm{n}"] + u, HH, HL, u // 2, 4 * (u % 2))

            def post_norm(n):
                gain = row()
                for tt in range(TT):
                    inverse_rms(tt)
                    nc.vector.scalar_tensor_tensor(XS[:, tt, :], PS[:, 4 + 2 * tt:6 + 2 * tt, :]
                                                   .rearrange("p h n -> p (h n)"), rs[:, tt:tt + 1], gain,
                                                   ALU.mult, ALU.mult).then_inc(s_accfree, 1)
                    dve.wait_ge(s_accfree, 2 * n + tt + 1)
                    if tt == TT - 1:
                        dve.sem_inc(s_rowused, 1)
                    nc.vector.tensor_tensor(X[:, tt, :], X[:, tt, :], XS[:, tt, :], ALU.add).then_inc(s_x, 1)

            def modulated(name, src, hi, lo):
                scale, gain = row(), row()
                chain.done(nc.vector.scalar_tensor_tensor(scale, scale, 1.0, gain, ALU.add, ALU.mult))
                shift = row()
                for tt in range(TT):
                    inverse_rms(tt)
                    chain.done(nc.vector.scalar_tensor_tensor(XS[:, tt, :], src[:, tt, :], rs[:, tt:tt + 1], scale,
                                                              ALU.mult, ALU.mult))
                    chain.done(nc.vector.tensor_tensor(XS[:, tt, :], XS[:, tt, :], shift, ALU.add))
                    dve.sem_inc(s_xs, 1)
                dve.sem_inc(s_rowused, 3)
                for u in range(4):
                    transposed_lo(UNITS[name] + u, hi, lo, u // 2, 4 * (u % 2))

            nc.vector.memset(eps_col, EPS).then_inc(s_eps, 1)
            b = take(UNITS["param"])
            nc.vector.tensor_copy(pcol[:, :], PS[:, b, 0:PROWS]).then_inc(s_pcol, 1)
            dve.wait_ge(s_pcol, 1)
            dve.sem_inc(s_free[b], 1)
            for g in range(2):
                dve.wait_ge(s_csilu, 1)
                half = (slice(None), slice(None), slice(64 * g, 64 * g + 64))
                src = csilu[:, 8 * g:8 * g + 8].unsqueeze(2).broadcast_to([P, KT, 64])
                chain.done(nc.vector.tensor_copy(ch[half], src))
                nc.vector.tensor_tensor(cl[half], src, ch[half].bitcast(F32), ALU.subtract).then_inc(s_cparts, 1)
            dve.wait_ge(s_alog, 2)
            nc.vector.tensor_scalar(at[1], at[0], 1.0, None, ALU.add).then_inc(s_acol, 1)
            dve.wait_ge(s_alog, 3)
            chain.done(nc.vector.tensor_scalar(at[1], at[1], -1.0, None, ALU.add))
            chain.done(nc.vector.tensor_scalar(at[3], at[1], 0.0, None, ALU.is_equal))
            chain.done(nc.vector.tensor_tensor(at[1], at[1], at[3], ALU.add))
            chain.done(nc.vector.reciprocal(at[1], at[1]))
            chain.done(nc.vector.tensor_tensor(at[2], at[2], at[1], ALU.mult))
            chain.done(nc.vector.tensor_tensor(at[2], at[2], at[3], ALU.add))
            chain.done(nc.vector.tensor_tensor(at[2], at[2], at[0], ALU.mult))
            chain.done(nc.vector.tensor_scalar(at[3], pcol[:, PAP:PAP + 12], -1.0, 0.0, ALU.mult, ALU.max))
            chain.done(nc.vector.tensor_tensor(at[2], at[2], at[3], ALU.add))
            chain.done(nc.vector.tensor_scalar(acol, at[2], -8.0, None, ALU.mult))
            nc.vector.tensor_scalar(ancol, at[2], 8.0, None, ALU.mult).then_inc(s_acol, 1)
            split_lo(0)

            def ada(i):
                for j in range(4):
                    split_lo(SLOTS["ada"] + j + 1, i, 4)
                    b = take(UNITS["ada"] + j, i, 4)
                    dve.wait_ge(s_abias[j], i * 16 + 16)
                    dve.wait_ge(s_ast[j], i * 32)
                    nc.vector.tensor_tensor(astage[:, j, :], PS[:, b, :], abias[:, j, :], ALU.add)\
                        .then_inc(s_free[b], 1)

            rounds(dve, 3, ada)
            norm(0)
            dve.wait_ge(s_rconst, 16 * (2 + RH))

            def rotate(i):
                for j in range(2):
                    split_lo(SLOTS["ret_in"] + j + 1, i, 2)
                    for half in range(2):
                        n = 2 * j + half
                        b = take(UNITS["ret_in"] + n, i, 4)
                        dve.wait_ge(s_rot, i * 4 + max(n - 1, 0) if n else i * 4)
                        src = PS[:, b, :].rearrange("p (x t) -> p x t", x=2)
                        for table in range(2):
                            ins = nc.vector.tensor_tensor(
                                RT[:, n % 2, 512 * table:512 * (table + 1)].rearrange("p (x t) -> p x t", x=2),
                                src, rot[:, table:table + 1, :].broadcast_to([P, 2, S]), ALU.mult)
                        ins.then_inc(s_free[b], 1)

            rounds(dve, 2, rotate)
            for part in range(2):
                with dve.Fori(0, 2) as i:
                    for j in range(2):
                        split_lo(SLOTS["ret_in"] + 4 + 4 * part + j + 1, i, 2)
            u = UNITS["ret_heads"]
            for kind, h in RET_STEPS:
                if kind == "s":
                    b = take(u)
                    nc.vector.tensor_tensor(SC[:, h % 2, :], PS[:, b, 0:384], decay[:, h, :], ALU.mult)\
                        .then_inc(s_free[b], 1)
                elif kind == "o":
                    for tt in range(TT):
                        b = take(u + tt)
                        chain.done(nc.vector.bn_stats(bst[:, tt, :], PS[:, b, :]))
                        nc.vector.bn_aggr(bmv[:, tt, :], bst[:, tt, :]).then_inc(s_bn, 1)
                    dve.wait_ge(s_bnr, h + 1)
                    chain.done(nc.vector.reciprocal(bmv[:, :, 1:2], bmv[:, :, 1:2]))
                    for tt in range(TT):
                        b = unit(u + tt)[0]
                        if h:
                            dve.wait_ge(s_og, 2 * h - 1 + tt)
                        nc.vector.tensor_scalar(ON[:, tt, :], PS[:, b, :], bmv[:, tt, 0:1], bmv[:, tt, 1:2],
                                                ALU.subtract, ALU.mult).then_inc(s_free[b], 1)
                else:
                    for tt in range(TT):
                        transposed_lo(u + tt, OH, OL, tt, 4 * h)
                u += RET_UNITS[kind]
            for j in range(4):
                split_lo(SLOTS["ret_out"] + j + 1)
            post_norm(0)

            def ffn(name, last):
                base, sbase = FFN_BASE[name], SLOTS[name]

                def step(kind, n, s0, i=0):
                    split_lo(s0 + 1, i, 4, after(sbase, s0, last))
                    if kind == "in":
                        g, use = unit(ffn_unit(name, n), i, 4)
                        b = take(ffn_unit(name, n) + 1, i, 4)
                        n, par = n + base, (n + base) % 2
                        dve.wait_ge(s_free[g], use + 1)
                        if n >= 2 or not isinstance(i, int):
                            dve.wait_ge(s_fp, i * 2 + n - 1)
                        nc.vector.tensor_tensor(fh[:, par, :], PS[:, b, :], fg[:, par, :], ALU.mult)\
                            .then_inc(s_fh, 1)
                        dve.wait_ge(s_fh, i * 2 + n + 1)
                        dve.sem_inc(s_free[b], 1)

                ffn_steps(dve, sbase, step, early=(lambda: modulated("norm_c", XC, CH, CL)) if name == "ffn1" else None)

            norm(1)
            ffn("ffn0", SLOT)
            post_norm(1)
            norm(2)
            chain.done(nc.vector.memset(UP[:, :, 0:3], 0.0))
            with dve.Fori(0, 3) as i:
                chain.enter(i, 2 * 9)
                for j in range(2):
                    split_lo(SLOTS["lru_in"] + j + 1, i, 2)
                    if j == 0:
                        continue
                    for half in range(2):
                        b = take(UNITS["lru_in"] + 2 + half, i, 4)
                        chain.done(nc.vector.tensor_copy(UP[:, 2 * half:2 * half + 2, 3:3 + S],
                                                         PS[:, b, :].rearrange("p (b t) -> p b t", b=2)))
                        dve.sem_inc(s_free[b], 1)
                        for q in range(2):
                            o = UC[:, bass.ds(i * 4 + (2 * half + q), 1), :]
                            col = lambda c: pcol[:, bass.ds(i * 4 + (c + 2 * half + q), 1)]
                            src = lambda tap: UP[:, 2 * half + q:2 * half + q + 1, tap:tap + S]
                            chain.done(nc.vector.tensor_scalar(o, src(0), col(PCW), col(PCB), ALU.mult, ALU.add))
                            for tap in range(1, 4):
                                ins = nc.vector.scalar_tensor_tensor(o, src(tap), col(PCW + 12 * tap), o,
                                                                     ALU.mult, ALU.add)
                                chain.done(ins)
                        dve.sem_inc(s_uc, 1)
            chain.leave(3)
            split_lo(SLOTS["lru_gate"] + 1, n=3072)
            for group in range(LB // 4):
                pairs = (2 * group, 2 * group + 1)
                if group >= 1:
                    split_lo(SLOTS["lru_out"] + group - 1)
                for n in pairs:
                    par, q = n % 2, LQ[:, n % 2, :]
                    dve.wait_ge(s_la, 4 * n + 4)
                    chain.done(nc.vector.tensor_tensor(q, LA[:, par, :], LA[:, par, :], ALU.mult))
                    chain.done(nc.vector.scalar_tensor_tensor(q, q, 1.0, LR[:, par, :], ALU.add, ALU.mult))
                    nc.vector.tensor_scalar(q, q, 2.0 ** -100, None, ALU.max).then_inc(s_lq, 1)
                for n in pairs:
                    par, pair, q = n % 2, slice(2 * n, 2 * n + 2), LQ[:, n % 2, :]
                    dve.wait_ge(s_liu, n + 1)
                    dve.wait_ge(s_lmult, n + 1)
                    chain.done(nc.vector.tensor_tensor(LI[:, par, :], LI[:, par, :], q, ALU.mult))
                    for j in range(2):
                        at_ = slice(j * S, (j + 1) * S)
                        ins = nc.vector.tensor_tensor_scan(q[:, at_], LA[:, par, at_], LI[:, par, at_], 0.0,
                                                           ALU.mult, ALU.add)
                    chain.done(ins)
                    nc.vector.tensor_tensor(UC[:, pair, :], q.rearrange("p (b t) -> p b t", b=2), Y[:, pair, :],
                                            ALU.mult).then_inc(s_lh, 1)
                    dve.wait_ge(s_lh, n + 1)
            for j in range(1, 3):
                split_lo(SLOTS["lru_out"] + j + 1)
            post_norm(2)
            norm(3)
            ffn("ffn1", SLOT)
            post_norm(3)
            def evacuated(u0, i=0, per=0):
                b, use = unit(u0, i, per)
                dve.wait_ge(s_free[b], use + 1)

            chain.done(nc.vector.memset(eps2_col, 1e-12))
            chain.done(nc.vector.memset(eps3_col, 64e-5))
            modulated("norm_l", X, HH, HL)
            for j in range(1, len(MIX_SLOTS)):
                split_lo(SLOTS["mix_in"] + j, n=KT * MIX_SLOTS[j][1])
            U = lambda k, d, what, n=0: UNITS["rwkv"] + RW_UNIT[k, d, what, n]
            vec = lambda n: RWR[:, n * 256:(n + 1) * 256]
            dve.wait_ge(s_mix, 16 * 13)
            evacuated(UNITS["mix_in"] + len(MIX_UNITS) - 1)
            for u in range(8):
                t, d = divmod(u, 2)
                b = take(UNITS["decay"] + u)
                nc.vector.tensor_tensor(WA[:, t, d].rearrange("p a c -> p (a c)"), PS[:, b, :],
                                        RWR[:, 512 * d:512 * d + 512], ALU.add).then_inc(s_free[b], 1)
            chain.done(nc.vector.tensor_tensor(KK[:, :, :], ZK[:, :, :], vec(4).unsqueeze(1).broadcast_to([P, 4, 256]),
                                               ALU.mult))
            square = TR[0][:, :, :, :].rearrange("p a b c -> p a (b c)")
            chain.done(nc.vector.tensor_tensor(square, KK[:, :, :], KK[:, :, :], ALU.mult))
            nc.vector.tensor_reduce(kn, TR[0][:, :, :, :].rearrange("p a b (e j) -> p (a b e) j", j=64), AX_X, ALU.add)\
                .then_inc(s_kk, 1)
            for d in range(2):
                chain.done(nc.vector.memset(SB[d][:, :, :], 0.0))
                dve.sem_inc(s_st[d], 1)
            dve.wait_ge(s_sig, 8)
            dve.wait_ge(s_mask, 16)
            for d in range(2):
                kd = KD[:, :, d * 256:(d + 1) * 256]
                chain.done(nc.vector.scalar_tensor_tensor(kd, WA[:, :, d, 1, :], -1.0,
                                                          vec(5).unsqueeze(1).broadcast_to([P, 4, 256]),
                                                          ALU.add, ALU.mult))
                chain.done(nc.vector.scalar_tensor_tensor(kd, kd, 1.0, ZK[:, :, :], ALU.add, ALU.mult))
            dve.wait_ge(s_kks, 1)
            chain.done(nc.vector.reciprocal(kn, kn))
            kk16 = KK[:, :, :].rearrange("p t (h j) -> p (t h) j", j=64)
            chain.done(nc.vector.tensor_tensor(kk16, kk16, kn.unsqueeze(2).broadcast_to([P, 16, 64]), ALU.mult))
            for d in range(2):
                chain.done(nc.vector.tensor_tensor(WA[:, :, d, 1, :], WA[:, :, d, 1, :], KK[:, :, :], ALU.mult))
            four = lambda m: m.unsqueeze(1).broadcast_to([P, 4, P])
            flat = lambda x: x[:, :, :, :].rearrange("p a b c -> p (a b) c")
            for k, d, t, what, n in RW_PLAN:
                mask = lambda m: MASK[:, 8 * d + m, :]
                level = None
                u = UNITS["rwkv"] + RW_UNIT[k, d, what, n] if what != "st" else None
                if what == "cum":
                    evacuated(u)
                    ep = EP[d][:, :, :, :].rearrange("p a b c -> p (a b c)")
                    en = EN[d][:, :, :, :].rearrange("p a b c -> p (a b c)")[:, 0:256]
                    nc.vector.tensor_tensor(BK[d][:, 1, :, :], KK[:, t, :].rearrange("p (h j) -> p h j", j=64),
                                            ep[:, 256:512].rearrange("p (h j) -> p h j", j=64), ALU.mult)
                    nc.vector.tensor_tensor(BE[d][:, :], WA[:, t, d, 1, :], en, ALU.mult)
                    ins = nc.vector.tensor_tensor(KR[d][:, :], KD[:, t, d * 256:(d + 1) * 256], en, ALU.mult)
                    if k >= 2:
                        ins = nc.vector.tensor_tensor(RH_[d][:, :], ZR[:, t - SEQ, :], ep[:, 0:256], ALU.mult)
                    ins.then_inc(s_rel, 1)
                elif what == "ab":
                    dve.wait_ge(s_aa, 4 * k + 2 * n + d + 1)
                    b = unit(u)[0]
                    nc.vector.tensor_tensor(BT[d][:, n, :, :], PS[:, b, 256:512].rearrange("p (a c) -> p a c", a=2),
                                            mask(6).unsqueeze(1).broadcast_to([P, 2, P]), ALU.mult)\
                        .then_inc(s_free[b], 1)
                elif what == "l":
                    b = take(u)
                    nc.vector.tensor_tensor(LL[d][:, n].rearrange("p a b c -> p (a b) c"),
                                            PS[:, b, :].rearrange("p (a c) -> p a c", a=4), four(mask(7)), ALU.mult)\
                        .then_inc(s_free[b], 1)
                elif what == "lev":
                    dve.wait_ge(s_rel, 2 * k + d + 1)
                    nc.vector.tensor_tensor(flat(AM[d]), flat(AA[d]), four(mask(0)), ALU.mult).then_inc(s_am, 1)
                    b = take(u)
                    nc.vector.tensor_tensor(flat(XX[d]), four(ident[:, :]), PS[:, b, :].rearrange("p (a c) -> p a c", a=4),
                                            ALU.subtract).then_inc(s_free[b], 1)
                elif what == "t":
                    nc.vector.tensor_tensor(flat(AM[d]), flat(AA[d]), four(mask(n)), ALU.mult).then_inc(s_am, 1)
                elif what == "xy":
                    b = take(u)
                    evacuated(U(k, d, "xy", n - 1) if n > 1 else U(k, d, "lev"))
                    nc.vector.tensor_tensor(flat(XX[d]), flat(XX[d]), PS[:, b, :].rearrange("p (a c) -> p a c", a=4),
                                            ALU.subtract).then_inc(s_free[b], 1)
                elif what == "mn":
                    b = take(u)
                    if k and n == 0:
                        dve.wait_ge(s_stp[d], 2 * k)
                    nc.vector.tensor_tensor(MN[d][:, n, :, :], PS[:, b, :].rearrange("p (a c) -> p a c", a=4),
                                            four(prow[:, :]), ALU.mult).then_inc(s_free[b], 1)
                elif what == "rt":
                    b = take(u)
                    nc.vector.tensor_tensor(RTt[d][:, :, :], PS[:, b, 0:256].rearrange("p (a c) -> p a c", a=2),
                                            TR[d][:, 3, :, :], ALU.add).then_inc(s_free[b], 1)
                elif what == "st" and (k, n) != (3, 1):
                    dve.wait_ge(s_stp[d], 2 * k + n + 1)
                    c = n ^ d
                    for hp in range(2):
                        ins = nc.vector.tensor_scalar(SB[d][:, hp, :], PS[:, 5 + d, hp * P:(hp + 1) * P],
                                                      PCD[:, t, d, hp, c:c + 1], None, ALU.mult)
                    ins.then_inc(s_st[d], 1)
            dve.wait_ge(s_y, 1)
            y = PS[:, 4, :].rearrange("p (g j) -> p g j", j=64)
            over = lambda c: c.unsqueeze(2).broadcast_to([P, 8, 64])
            groups = lambda x: x[:, :, :].rearrange("p t (h j) -> p (t h) j", j=64)
            both = lambda v: v.unsqueeze(1).broadcast_to([P, TT, 256])
            chain.done(nc.vector.tensor_reduce(gmu, y, AX_X, ALU.add))
            chain.done(nc.vector.tensor_scalar(gmu, gmu, 1.0 / 64, None, ALU.mult))
            chain.done(nc.vector.tensor_tensor(groups(RY), y, over(gmu), ALU.subtract))
            chain.done(nc.vector.tensor_tensor(RW2[:, :, :], RY[:, :, :], RY[:, :, :], ALU.mult))
            nc.vector.tensor_reduce(gvar, groups(RW2), AX_X, ALU.add).then_inc(s_gn, 1)
            dve.wait_ge(s_gn, 1)
            chain.done(nc.vector.tensor_tensor(RW2[:, :, :], ZR[:, :, :], ZK[:, SEQ:SEQ + 2, :], ALU.mult))
            chain.done(nc.vector.tensor_tensor(RW2[:, :, :], RW2[:, :, :], both(vec(6)), ALU.mult))
            chain.done(nc.vector.tensor_reduce(gsum, groups(RW2), AX_X, ALU.add))
            chain.done(nc.vector.tensor_tensor(groups(RW2), ZV[:, SEQ:SEQ + 2, :].rearrange("p t (h j) -> p (t h) j", j=64),
                                               over(gsum), ALU.mult))
            dve.wait_ge(s_gns, 1)
            chain.done(nc.vector.reciprocal(gvar, gvar))
            chain.done(nc.vector.tensor_tensor(groups(RY), groups(RY), over(gvar), ALU.mult))
            chain.done(nc.vector.tensor_tensor(RY[:, :, :], RY[:, :, :], both(vec(7)), ALU.mult))
            chain.done(nc.vector.tensor_tensor(RY[:, :, :], RY[:, :, :], RW2[:, :, :], ALU.add))
            b = take(UNITS["rw_gate"])
            chain.done(nc.vector.tensor_tensor(RY[:, :, :], RY[:, :, :], PS[:, b, :].rearrange("p (t c) -> p t c", t=TT),
                                               ALU.mult))
            dve.sem_inc(s_free[b], 1)
            dve.sem_inc(s_ry, 1)
            counts["xhi"] += 1
            dve.wait_ge(s_xhi, counts["xhi"])
            b = unit(UNITS["rw_out"])[0]
            nc.vector.tensor_tensor(HL[:, 0:2, :], PS[:, b, :].rearrange("p (k t) -> p k t", k=2),
                                    HH[:, 0:2, :].bitcast(F32), ALU.subtract).then_inc(s_free[b], 1)
            chain.done(nc.vector.memset(SP[:, :, 0:1], 0.0))
            chain.done(nc.vector.memset(SP[:, :, S + 1:S + 2], 0.0))
            chain.done(nc.vector.tensor_tensor(SP[:, :, 1:S + 1], SCZ[:, 2:4, :], SCZ[:, 4:6, :], ALU.mult))
            for blk in range(2):
                tap = lambda k: pcol[:, PSC + 2 * k + blk:PSC + 2 * k + blk + 1]
                o = SCZ[:, 4 + blk, :]
                chain.done(nc.vector.tensor_scalar(o, SP[:, blk, 0:S], tap(0), None, ALU.mult))
                for k in (1, 2):
                    chain.done(nc.vector.scalar_tensor_tensor(o, SP[:, blk, k:k + S], tap(k), o, ALU.mult, ALU.add))
            nc.vector.tensor_tensor(SCZ[:, 4:6, :], SCZ[:, 4:6, :], SCZ[:, 0:2, :], ALU.mult).then_inc(s_sc, 1)
            dve.wait_ge(s_sch, 1)
            nc.vector.tensor_tensor(HL[:, 6:8, :], SCZ[:, 4:6, :], HH[:, 6:8, :].bitcast(F32), ALU.subtract)\
                .then_inc(s_yt, 1)
            for i in range(NA_STEPS):
                b = take(UNITS["na"] + na_scores(i))
                if i >= 4:
                    dve.wait_ge(s_nx, i - 3)
                chain.done(nc.vector.tensor_reduce(nmax[i % 4], PS[:, b, :], AX_X, ALU.max))
                nc.vector.tensor_scalar(nmax[i % 4], nmax[i % 4], -(64 ** -0.5), None, ALU.mult).then_inc(s_ns, 1)
            dve.wait_ge(s_nx, NA_STEPS)
            chain.done(nc.vector.reciprocal(nsum, nsum))
            dve.wait_ge(s_no, 1)
            for tt in range(TT):
                nc.vector.tensor_tensor(NY[:, tt, :].rearrange("p (h j) -> p h j", j=64),
                                        PS[:, 5 + tt, :].rearrange("p (h j) -> p h j", j=64),
                                        nsum[:, 8 * tt:8 * tt + 8].unsqueeze(2).broadcast_to([P, 8, 64]), ALU.mult)\
                    .then_inc(s_ny, 1)
            for tt in range(TT):
                transposed_lo(UNITS["na_out"] + tt, HH, HL, tt, 2)
            for j in range(2):
                split_lo(SLOTS["mix_out"] + j)

            def gated_add(number):
                gate = row()
                for tt in range(TT):
                    dve.wait_ge(s_acc, 2 * number - 1 + tt)
                    nc.vector.tensor_tensor(XS[:, tt, :], PS[:, 4 + 2 * tt:6 + 2 * tt, :].rearrange("p h n -> p (h n)"),
                                            gate, ALU.mult).then_inc(s_accfree, 1)
                    dve.wait_ge(s_accfree, 2 * number - 1 + tt)
                    if tt == TT - 1:
                        dve.sem_inc(s_rowused, 1)
                    nc.vector.tensor_tensor(X[:, tt, :], X[:, tt, :], XS[:, tt, :], ALU.add).then_inc(s_x, 1)

            gated_add(5)
            split_lo(SLOTS["peer_q"])
            dve.wait_ge(s_x, 10)
            modulated("norm_p", X, HH, HL)
            for j in range(3):
                split_lo(SLOTS["peer_q"] + j + 1)

            def top16(count, values, at_, src):
                for r in range(2):
                    half = slice(8 * r, 8 * r + 8)
                    for g in range(count):
                        ins = nc.vector.max(values[:, g, half], src(g))
                    chain.done(ins)
                    for g in range(count):
                        ins = nc.vector.max_index(at_[:, g, half], values[:, g, half], src(g))
                    chain.done(ins)
                    if r == 0:
                        for g in range(count):
                            ins = nc.vector.match_replace(src(g), values[:, g, half], src(g), -3e38)
                        chain.done(ins)

            def picks_step(j):
                if j >= len(PICKS):
                    return
                what, tt, n = PICKS[j]
                tv = TV[:, :, :].rearrange("p (h s) k -> p h s k", s=2)
                tf = TF[:, :, :].rearrange("p (h s) k -> p h s k", s=2)
                over = lambda x: x.unsqueeze(2).broadcast_to([P, 8, 16])
                all_ = [P, 8, 16, 16]
                if what == "keys":
                    pair = slice(n, n + 2)
                    top16(2, TV[:, pair, :], TX[:, pair, :], lambda g: PSC_[tt][:, n + g, :])
                elif what == "sums":
                    chain.done(nc.vector.tensor_copy(TF[:, :, :], TX[:, :, :]))
                    chain.done(nc.vector.tensor_tensor(CAND[:, :, :, :], tv[:, :, 0, :].unsqueeze(3).broadcast_to(all_),
                                                       tv[:, :, 1, :].unsqueeze(2).broadcast_to(all_), ALU.add))
                elif what == "picks":
                    top16(1, CV[:, n:n + 1, :], CX[:, n:n + 1, :], lambda h: CAND[:, n].rearrange("p a b -> p (a b)"))
                elif what == "places":
                    chain.done(nc.vector.tensor_scalar(CXH[:, 0], CX[:, :, :], 4, None, ALU.logical_shift_right))
                    chain.done(nc.vector.tensor_scalar(CXH[:, 1], CX[:, :, :], 15, None, ALU.bitwise_and))
                    chain.done(nc.vector.tensor_copy(CF[:, :, :, :], CXH[:, :, :, :]))
                    chain.done(nc.vector.tensor_copy(CS[:, :], CV[:, :, 0]))
                    nc.vector.tensor_tensor(CV[:, :, :], CV[:, :, :], over(CS[:, :]), ALU.subtract).then_inc(s_pm, 1)
                elif what == "match":
                    if tt:
                        dve.wait_ge(s_pt, tt)
                    iota = IOTA[:, 0:16].unsqueeze(1).unsqueeze(1).broadcast_to(all_)
                    chain.done(nc.vector.tensor_tensor(EQ[:, :, :, :], CF[:, n].unsqueeze(3).broadcast_to(all_), iota,
                                                       ALU.is_equal))
                    chain.done(nc.vector.tensor_tensor(EQ[:, :, :, :], EQ[:, :, :, :],
                                                       tf[:, :, n, :].unsqueeze(2).broadcast_to(all_), ALU.mult))
                    chain.done(nc.vector.tensor_reduce(PK[:, n], EQ[:, :, :, :], AX_X, ALU.add))
                else:
                    dve.wait_ge(s_pe, tt + 1)
                    chain.done(nc.vector.tensor_reduce(CS[:, :], CV[:, :, :], AX_X, ALU.add))
                    chain.done(nc.vector.reciprocal(CS[:, :], CS[:, :]))
                    nc.vector.tensor_tensor(PK[:, 2], CV[:, :, :], over(CS[:, :]), ALU.mult).then_inc(s_pk, 1)
                    dve.wait_ge(s_pk, tt + 1)

            dve.wait_ge(s_iota, 16)
            evacuated(UNITS["peer_s"] + 7)
            def u_low(j, i=0):
                b, use = j % 2, i + j // 2
                for h in range(2):
                    dve.wait_ge(s_uh[b], 2 * use + h + 1)
                    nc.vector.tensor_tensor(UTL[:, b, 4 * h:4 * h + 4, :], PS[:, h, :].rearrange("p (k e) -> p k e", k=4),
                                            UTH[:, b, 4 * h:4 * h + 4, :].bitcast(F32), ALU.subtract)\
                        .then_inc(s_ul[b], 1)

            u_steps(dve, u_low, lambda *a: None, picks_step)
            dve.wait_ge(s_hk, TT)
            with dve.Fori(0, S // 16) as i:
                for j in range(4):
                    half = slice(4 * (j % 2), 4 * (j % 2) + 4)
                    b, use = unit(UNITS["gates"] + j - 2, i, 4)
                    dve.wait_ge(s_full[b], use + 1)
                    token = lambda n, x: HKT[:, n, bass.ds(i * 16 + 4 * j + x, 1)]
                    nc.vector.tensor_tensor(ONE2[:, half, :], IOTA[:, :].unsqueeze(1).broadcast_to([P, 4, P]),
                                            HKT[:, 1, bass.ds(i * 16 + 4 * j, 4)].unsqueeze(2).broadcast_to([P, 4, P]),
                                            ALU.is_equal)
                    for x in range(4):
                        ins = nc.vector.tensor_scalar(ONE1[:, 4 * (j % 2) + x, :], IOTA[:, :], token(0, x), token(2, x),
                                                      ALU.is_equal, ALU.mult)
                    ins.then_inc(s_oh, 1)

            def low_(j, i=0):
                b = j % 2
                dve.wait_ge(s_ah, 4 * i + j + 1)
                nc.vector.tensor_tensor(AL[:, b:b + 1, :], GT[:, bass.ds(4 * i + j, 1), :],
                                        AH[:, b:b + 1, :].bitcast(F32), ALU.subtract).then_inc(s_as, 1)
                for half in range(2):
                    at_ = slice(half * BANK, (half + 1) * BANK)
                    dve.wait_ge(s_vh, 8 * i + 2 * j + half + 1)
                    ins = nc.vector.tensor_tensor(VL[:, b, at_], VR[:, j % 4, at_], VH[:, b, at_].bitcast(F32),
                                                  ALU.subtract)
                ins.then_inc(s_vl, 1)

            v_steps(dve, low_, lambda *a: None)
            gated_add(6)
            gain = row()
            for tt in range(TT):
                inverse_rms(tt)
                nc.vector.scalar_tensor_tensor(XS[:, tt, :], X[:, tt, :], rs[:, tt:tt + 1], gain, ALU.mult, ALU.mult)\
                    .then_inc(s_x, 1)

        @block.tensor
        def _(pe):
            def mm3(o, ah, al, bh, bl, start, stop):
                nc.tensor.matmul(o, ah, bh, start=start, stop=False)
                nc.tensor.matmul(o, ah, bl, start=False, stop=False)
                return nc.tensor.matmul(o, al, bh, start=False, stop=stop)

            def free_bank(u0, i=0, per=0):
                b, use = unit(u0, i, per)
                pe.wait_ge(s_free[b], use)
                return b

            def evacuated(u0, i=0, per=0):
                b, use = unit(u0, i, per)
                pe.wait_ge(s_free[b], use + 1)

            def weights(s0, i=0, per=0):
                r, use = slot(s0, i, per)
                pe.wait_ge(s_wlo[r], use + 1)
                return r

            def wview(r, k=KT, n=None):
                n = n or SLOT
                return [w[:, r, 0:n].rearrange("p (k n) -> p k n", k=k) for w in (whi, wlo)]

            def t_unit(u0, i, per, wv, n0, blocks=2, hi=HH, lo=HL):
                b = free_bank(u0, i, per)
                for blk in range(blocks):
                    at_ = slice(n0 + blk * P, n0 + (blk + 1) * P)
                    for k in range(KT):
                        ins = mm3(PS[:, b, blk * S:(blk + 1) * S], wv[0][:, k, at_], wv[1][:, k, at_],
                                  hi[:, k, :], lo[:, k, :], k == 0, k == KT - 1)
                ins.then_inc(s_full[b], 1)
                return ins

            def n_unit(u0, i, per, wv, tt, n0=0, n=BANK, hi=HH, lo=HL):
                b = free_bank(u0, i, per)
                tok = slice(tt * P, (tt + 1) * P)
                for k in range(KT):
                    ins = mm3(PS[:, b, 0:n], hi[:, k, tok], lo[:, k, tok], wv[0][:, k, n0:n0 + n],
                              wv[1][:, k, n0:n0 + n], k == 0, k == KT - 1)
                ins.then_inc(s_full[b], 1)

            def used(r):
                pe.drain().then_inc(s_wused[r], 1)

            def transposes(n):
                normed_transposes(f"norm{n}", n)
                for u in range(4):
                    evacuated(UNITS[f"norm{n}"] + u)

            def normed_transposes(name, n):
                for u in range(4):
                    tt = u // 2
                    if u % 2 == 0:
                        pe.wait_ge(s_xs, 2 * n + tt + 1)
                    b = free_bank(UNITS[name] + u)
                    for j in range(4):
                        at_ = slice((4 * (u % 2) + j) * P, (4 * (u % 2) + j + 1) * P)
                        ins = nc.tensor.transpose(PS[:, b, j * P:(j + 1) * P], XS[:, tt, at_], ident[:, :])
                    ins.then_inc(s_full[b], 1)

            def into_acc(r, hi, lo, kts, first, last, w):
                for tt in range(TT):
                    for kk, kt in enumerate(kts):
                        tok = slice(tt * P, (tt + 1) * P)
                        for half in range(2):
                            at_ = slice(half * BANK, (half + 1) * BANK)
                            ins = mm3(acc(tt, half), hi[:, kt, tok], lo[:, kt, tok], w[0][:, kk, at_], w[1][:, kk, at_],
                                      first and kk == 0, last and kk == len(kts) - 1)
                    if last and tt == 0:
                        ins.then_inc(s_acc, 1)
                return ins

            def project_acc(name, n_slots, hi, lo, number, parts_ready=None, per_slot=0):
                for j in range(n_slots):
                    r = weights(SLOTS[name] + j)
                    if parts_ready is not None:
                        pe.wait_ge(parts_ready, (j + 1) * per_slot)
                    if j == 0 and number:
                        pe.wait_ge(s_accfree, 2 * number)
                    ins = into_acc(r, hi, lo, range(4 * j, 4 * j + 4), j == 0, j == n_slots - 1, wview(r, 4))
                    ins.then_inc(s_wused[r], 1)
                pe.drain().then_inc(s_acc, 1)

            pe.wait_ge(s_const, 16 * 8)
            b = free_bank(UNITS["param"])
            nc.tensor.transpose(PS[:, b, 0:PROWS], prow[0:PROWS, :], ident[0:PROWS, 0:PROWS]).then_inc(s_full[b], 1)
            pe.wait_ge(s_cparts, 2)

            def ada(i):
                for j in range(4):
                    r = weights(SLOTS["ada"] + j, i, 4)
                    wv = wview(r)
                    b = free_bank(UNITS["ada"] + j, i, 4)
                    for k in range(KT):
                        ins = mm3(PS[:, b, :], ch[:, k, :], cl[:, k, :], wv[0][:, k, :], wv[1][:, k, :],
                                  k == 0, k == KT - 1)
                    ins.then_inc(s_full[b], 1)
                    used(r)

            rounds(pe, 3, ada)
            transposes(0)
            with pe.Fori(0, 2) as i:
                for j in range(2):
                    r = weights(SLOTS["ret_in"] + j, i, 2)
                    for half in range(2):
                        t_unit(UNITS["ret_in"] + 2 * j + half, i, 4, wview(r), half * 2 * P)
                    used(r)
            with pe.Fori(0, 4) as i:
                for j in range(2):
                    r = weights(SLOTS["ret_in"] + 4 + j, i, 2)
                    for tt in range(TT):
                        n_unit(UNITS["ret_in"] + 8 + 2 * j + tt, i, 4, wview(r), tt)
                    used(r)
            u = UNITS["ret_heads"]
            for kind, h in RET_STEPS:
                hd = slice(h * RDV, (h + 1) * RDV)
                if kind == "s":
                    if h == 0:
                        pe.wait_ge(s_rot, 8)
                    b = free_bank(u)
                    for at_, keys, queries in ((slice(0, S), slice(0, P), slice(0, S)),
                                               (slice(S, S + P), slice(P, S), slice(P, S))):
                        for x in range(2):
                            ins = nc.tensor.matmul(PS[:, b, at_], QK[:, 8 + 2 * h + x, keys],
                                                   QK[:, 2 * h + x, queries], start=x == 0, stop=x == 1)
                    ins.then_inc(s_full[b], 1)
                    scores_unit = {**(scores_unit if h else {}), h: u}
                elif kind == "o":
                    if h == 0:
                        for v in range(16):
                            evacuated(UNITS["ret_in"] + 8 + v)
                    evacuated(scores_unit[h])
                    b = free_bank(u)
                    nc.tensor.matmul(PS[:, b, :], SC[:, h % 2, 0:P], V[:, 0, hd], start=True, stop=True)\
                        .then_inc(s_full[b], 1)
                    b = free_bank(u + 1)
                    nc.tensor.matmul(PS[:, b, :], SC[:, h % 2, P:2 * P], V[:, 0, hd], start=True, stop=False)
                    nc.tensor.matmul(PS[:, b, :], SC[:, h % 2, 2 * P:3 * P], V[:, 1, hd], start=False, stop=True)\
                        .then_inc(s_full[b], 1)
                else:
                    for tt in range(TT):
                        pe.wait_ge(s_og, 2 * h + tt + 1)
                        b = free_bank(u + tt)
                        for j in range(4):
                            ins = nc.tensor.transpose(PS[:, b, j * P:(j + 1) * P],
                                                      SG[:, tt, h * RDV + j * P:h * RDV + (j + 1) * P], ident[:, :])
                        ins.then_inc(s_full[b], 1)
                u += RET_UNITS[kind]
            for v in range(8):
                evacuated(u - 8 + v)
            project_acc("ret_out", 4, OH, OL, 0)

            def ffn(name, number):
                base, sbase = FFN_BASE[name], SLOTS[name]

                def step(kind, n, s0, i=0):
                    r = weights(s0, i, 4)
                    if kind == "in":
                        for half in range(2):
                            t_unit(ffn_unit(name, n) + half, i, 4, wview(r), half * 256)
                        used(r)
                        return
                    if n == 0:
                        pe.wait_ge(s_accfree, 2 * number)
                    first, last = n == 0, n == FI - 1
                    n, par = n + base, (n + base) % 2
                    pe.wait_ge(s_fp, i * 2 + n + 1)
                    into_acc(r, FH[:, par], FL[:, par], range(2), first, last, wview(r, 2, 2 * D))\
                        .then_inc(s_wused[r], 1)
                    pe.wait_ge(s_wused[r], slot(s0, i, 4)[1] + 1)
                    pe.sem_inc(s_fu, 1)

                ffn_steps(pe, sbase, step, early=(lambda: normed_transposes("norm_c", 4)) if name == "ffn1" else None)
                pe.drain().then_inc(s_acc, 1)

            transposes(1)
            ffn("ffn0", 1)
            transposes(2)
            with pe.Fori(0, 3) as i:
                for j in range(2):
                    r = weights(SLOTS["lru_in"] + j, i, 2)
                    for half in range(2):
                        t_unit(UNITS["lru_in"] + 2 * j + half, i, 4, wview(r), half * 2 * P)
                    used(r)
            for n in range(LB // 2):
                if n % 3 == 0:
                    r = weights(SLOTS["lru_gate"] + n // 3)
                pe.wait_ge(s_up, n + 1)
                for g in range(2):
                    b = free_bank(UNITS["lru_gate"] + 2 * n + g)
                    for blk in range(2):
                        for k in range(2):
                            o = g * 1536 + (n % 3) * 512 + k * 256 + blk * P
                            ins = mm3(PS[:, b, blk * S:(blk + 1) * S], whi[:, r, o:o + P], wlo[:, r, o:o + P],
                                      UH[:, 2 * n + k, :], UL[:, 2 * n + k, :], k == 0, k == 1)
                    ins.then_inc(s_full[b], 1)
                if n % 3 == 2:
                    used(r)
            project_acc("lru_out", 3, UH, UL, 2, s_lp, 2)
            transposes(3)
            ffn("ffn1", 3)
            normed_transposes("norm_l", 5)
            for u in range(4):
                evacuated(UNITS["norm_l"] + u)
            tokens = ((CH, CL), (HH, HL))
            at_unit = UNITS["mix_in"]
            for j, (_, n_cols) in enumerate(MIX_SLOTS):
                r = weights(SLOTS["mix_in"] + j)
                wv = wview(r, n=KT * n_cols)
                for s, parts_, _ in MIX_UNITS:
                    if s != j:
                        continue
                    b, o = free_bank(at_unit), 0
                    for part in parts_:
                        if part[0] == "n":
                            _, t, c, n = part
                            hi, lo = tokens[t // 2]
                            tok = slice((t % 2) * P, (t % 2 + 1) * P)
                            for k in range(KT):
                                ins = mm3(PS[:, b, o:o + n], hi[:, k, tok], lo[:, k, tok], wv[0][:, k, c:c + n],
                                          wv[1][:, k, c:c + n], k == 0, k == KT - 1)
                            o += n
                        else:
                            _, c, t = part
                            hi, lo = tokens[t // 2]
                            for k in range(KT):
                                ins = mm3(PS[:, b, o:o + S], wv[0][:, k, c:c + P], wv[1][:, k, c:c + P], hi[:, k, :],
                                          lo[:, k, :], k == 0, k == KT - 1)
                            o += S
                    ins.then_inc(s_full[b], 1)
                    at_unit += 1
                used(r)
            pe.wait_ge(s_mix, 16 * 13)
            for v in range(4):
                evacuated(at_unit - 1 - v)
            for u in range(8):
                t, d = divmod(u, 2)
                b = free_bank(UNITS["decay"] + u)
                rows_, tok = slice(64 * d, 64 * d + 64), slice(t * P, (t + 1) * P)
                for j, x in enumerate((LWT, LAT)):
                    ins = nc.tensor.matmul(PS[:, b, j * 256:(j + 1) * 256], x[rows_, tok], LORA[rows_, j, :],
                                           start=True, stop=True)
                ins.then_inc(s_full[b], 1)
            b = free_bank(UNITS["chunk"])
            for u in range(8):
                t, d = divmod(u, 2)
                if u == 0:
                    pe.wait_ge(s_sig, 8)
                for hp in range(2):
                    ins = nc.tensor.matmul(PS[:, b, 4 * u + 2 * hp:4 * u + 2 * hp + 2], WA[:, t, d, 0, hp * P:(hp + 1) * P],
                                           chk, start=True, stop=True)
            ins.then_inc(s_full[b], 1)
            first_y = True
            pe.wait_ge(s_mask, 16)
            for k, d, t, what, n in RW_PLAN:
                U = lambda what, n=0: UNITS["rwkv"] + RW_UNIT[k, d, what, n]
                quarter = lambda q: PS[:, b, q * P:(q + 1) * P]
                pairs = lambda x, kind, hp: x[d][:, kind, hp, :]
                if what == "st":
                    c = n ^ d
                    ch_ = slice(64 * c, 64 * c + 64)
                    if n == 0:
                        evacuated(U("mn", 0))
                        evacuated(U("mn", 1))
                        if k >= 2:
                            evacuated(U("rt"))
                    if k == 0 and n == 0:
                        evacuated(UNITS["chunk"])
                    pe.wait_ge(s_st[d], 2 * k + n + 1)
                    if k >= 2:
                        for hp in range(2):
                            o = (t - SEQ) * 256 + hp * P
                            nc.tensor.matmul(PS[ch_, 4, o:o + P], RTt[d][:, hp, ch_], SB[d][:, hp, :], start=False,
                                             stop=False, skip_group_check=True)
                    if (k, n) != (3, 1):
                        for hp in range(2):
                            o = PS[:, 5 + d, hp * P:(hp + 1) * P]
                            nc.tensor.matmul(o, ident[:, :], SB[d][:, hp, :], start=hp == 0, stop=False,
                                             skip_group_check=True)
                            nc.tensor.matmul(o, ident[:, :], MN[d][:, c, 2 + hp, :], start=False, stop=False,
                                             skip_group_check=True)
                            ins = nc.tensor.matmul(o, MN[d][:, c, hp, :], SB[d][:, hp, :], start=False, stop=hp == 1,
                                                   skip_group_check=True)
                        ins.then_inc(s_stp[d], 1)
                    continue
                b = free_bank(U(what, n))
                if what == "cum":
                    for j, m in enumerate((7, 6)):
                        ins = nc.tensor.matmul(PS[:, b, j * 256:(j + 1) * 256], MASK[:, 8 * d + m, :], WA[:, t, d, 0, :],
                                               start=True, stop=True)
                elif what == "tr":
                    if n == 0:
                        pe.wait_ge(s_rel, 2 * k + d + 1)
                    for j in range(2 if n and k < 2 else 4):
                        kind, hp = j // 2, j % 2
                        if (n, kind) == (0, 0):
                            src = BK[d][:, 1, 2 * hp:2 * hp + 2, :].rearrange("p h j -> p (h j)")
                        else:
                            src = ((None, BE[d]) if n == 0 else (KR[d], RH_[d]))[kind][:, hp * P:(hp + 1) * P]
                        ins = nc.tensor.transpose(quarter(j), src, ident[:, :])
                elif what in ("ab", "l"):
                    if (what, n) == ("ab", 0):
                        evacuated(U("tr", 0))
                        evacuated(U("tr", 1))
                    half = slice(64 * n, 64 * n + 64)
                    for j in range(4):
                        kind, hp = j // 2, j % 2
                        if what == "ab":
                            left, right = ((0, 1), (2, 0))[kind]
                        else:
                            left, right = ((1, 3), (2, 3))[kind]
                        ins = nc.tensor.matmul(quarter(j), TR[d][half, left, hp, :], TR[d][half, right, hp, :],
                                               start=True, stop=True)
                elif what == "bv":
                    evacuated(U("ab", 0))
                    evacuated(U("ab", 1))
                    for h in range(4):
                        ins = nc.tensor.matmul(PS[:, b, h * 64:(h + 1) * 64], BT[d][:, h % 2, h // 2, :],
                                               ZV[:, t, h * 64:(h + 1) * 64], start=True, stop=True)
                elif what == "lev":
                    pe.wait_ge(s_am, 12 * k + d + 1)
                    for j in range(4):
                        ins = nc.tensor.transpose(quarter(j), AM[d][:, j // 2, j % 2, :], ident[:, :])
                elif what == "t":
                    evacuated(U("xy", n - 1) if n > 1 else U("lev"))
                    for j in range(4):
                        ins = nc.tensor.transpose(quarter(j), XX[d][:, j // 2, j % 2, :], ident[:, :])
                elif what == "y":
                    pe.wait_ge(s_am, 12 * k + 2 * n + d + 1)
                    for j in range(4):
                        ins = nc.tensor.matmul(quarter(j), AM[d][:, j // 2, j % 2, :], XX[d][:, j // 2, j % 2, :],
                                               start=True, stop=True)
                elif what == "xy":
                    evacuated(U("t", n))
                    evacuated(U("y", n))
                    for j in range(4):
                        ins = nc.tensor.matmul(quarter(j), TI[d][:, j // 2, j % 2, :], YY[d][:, j // 2, j % 2, :],
                                               start=True, stop=True)
                elif what == "ug":
                    evacuated(U("xy", 5))
                    evacuated(U("bv"))
                    for h in range(4):
                        ins = nc.tensor.matmul(quarter(h), XX[d][:, h % 2, h // 2, :],
                                               BK[d][:, :, h, :], start=True, stop=True)
                elif what == "mn":
                    if n == 0:
                        evacuated(U("ug"))
                    half = slice(64 * n, 64 * n + 64)
                    for hp in range(2):
                        cols_ = slice(hp * P, (hp + 1) * P)
                        nc.tensor.matmul(quarter(hp), NUG[d][half, 1, 2 * hp:2 * hp + 2, :].rearrange("p h j -> p (h j)"), BE[d][half, cols_],
                                         start=True, stop=True)
                        nc.tensor.matmul(quarter(2 + hp), BE[d][half, cols_], NUG[d][half, 0, 2 * hp:2 * hp + 2, :].rearrange("p h j -> p (h j)"),
                                         start=True, stop=False)
                        ins = nc.tensor.matmul(quarter(2 + hp), KR[d][half, cols_], ZV[half, t, cols_],
                                               start=False, stop=True)
                elif what == "rt":
                    if k >= 2:
                        evacuated(U("l", 0))
                        evacuated(U("l", 1))
                    for h in range(4):
                        par, hp = h % 2, h // 2
                        o = PS[:, 4, (t - SEQ) * 256 + h * 64:(t - SEQ) * 256 + h * 64 + 64]
                        if first_y:
                            pe.wait_ge(s_accfree, 8)
                        nc.tensor.matmul(o, LL[d][:, par, 1, hp, :], ZV[:, t, h * 64:(h + 1) * 64], start=first_y,
                                         stop=False, skip_group_check=True)
                        first_y = False
                        nc.tensor.matmul(o, LL[d][:, par, 0, hp, :], NUG[d][:, 0, h, :], start=False, stop=False,
                                         skip_group_check=True)
                    for h in range(4):
                        par, hp = h % 2, h // 2
                        ins = nc.tensor.matmul(PS[64 * par:64 * par + 64, b, hp * P:(hp + 1) * P], NUG[d][:, 1, h, :],
                                               LL[d][:, par, 0, hp, :], start=True, stop=True, skip_group_check=True)
                ins.then_inc(s_full[b], 1)
            pe.drain().then_inc(s_y, 1)
            b = free_bank(UNITS["rw_gate"])
            for tt in range(TT):
                ins = nc.tensor.matmul(PS[:, b, tt * 256:(tt + 1) * 256], SGT[:, tt * P:(tt + 1) * P], LORA[:, 2, :],
                                       start=True, stop=True)
            ins.then_inc(s_full[b], 1)
            pe.wait_ge(s_ry, 1)
            b = free_bank(UNITS["rw_out"])
            for blk in range(2):
                for tt in range(TT):
                    o = (2 * blk + tt) * P
                    ins = nc.tensor.transpose(PS[:, b, o:o + P], RY[:, tt, blk * P:(blk + 1) * P], ident[:, :])
            ins.then_inc(s_full[b], 1)
            def na_score(i):
                qt, h = divmod(i, 8)
                half = slice(64 * (h % 2), 64 * (h % 2) + 64)
                b = free_bank(UNITS["na"] + na_scores(i))
                if h == 0:
                    pe.wait_ge(s_biasm, qt + 1)
                nc.tensor.matmul(PS[:, b, :], NQ[half, h // 2, qt * P:(qt + 1) * P], NK[half, h // 2, :],
                                 start=True, stop=False, skip_group_check=True)
                nc.tensor.matmul(PS[:, b, S:2 * S], FLIP[:, :], BIAS[:, qt, h, :], start=False, stop=True,
                                 skip_group_check=True).then_inc(s_full[b], 1)

            def na_turn(i):
                b = free_bank(UNITS["na"] + na_turned(i))
                pe.wait_ge(s_nx, i + 1)
                for j in range(4):
                    ins = nc.tensor.transpose(PS[:, b, j * P:(j + 1) * P], NS[:, i % 4, j * P:(j + 1) * P], ident[:, :])
                ins.then_inc(s_full[b], 1)

            def na_output(i):
                qt, h = divmod(i, 8)
                evacuated(UNITS["na"] + na_turned(i))
                for j in range(4):
                    nc.tensor.matmul(PS[:, 5 + qt, h * 64:(h + 1) * 64], NPT[:, i % 2, j * P:(j + 1) * P],
                                     NV[:, j, h * 64:(h + 1) * 64], start=(h, j) == (0, 0), stop=(h, j) == (7, 3),
                                     skip_group_check=True)

            na_score(0)
            for i in range(NA_STEPS):
                if i + 1 < NA_STEPS:
                    na_score(i + 1)
                na_turn(i)
                if i:
                    na_output(i - 1)
            na_output(NA_STEPS - 1)
            pe.drain().then_inc(s_no, 1)
            for tt in range(TT):
                pe.wait_ge(s_ny, tt + 1)
                b = free_bank(UNITS["na_out"] + tt)
                for j in range(4):
                    ins = nc.tensor.transpose(PS[:, b, j * P:(j + 1) * P], NY[:, tt, j * P:(j + 1) * P], ident[:, :])
                ins.then_inc(s_full[b], 1)
            evacuated(UNITS["rw_out"])
            for tt in range(TT):
                evacuated(UNITS["na_out"] + tt)
            pe.wait_ge(s_yt, 1)
            project_acc("mix_out", 2, HH, HL, 4)
            normed_transposes("norm_p", 6)
            for u in range(4):
                evacuated(UNITS["norm_p"] + u)
            for j in range(4):
                r = weights(SLOTS["peer_q"] + j)
                for half in range(2):
                    t_unit(UNITS["peer_q"] + 2 * j + half, 0, 0, wview(r), half * 2 * P)
                used(r)
            pe.wait_ge(s_keys, 16)
            for q in range(4):
                b = free_bank(UNITS["keys"] + q)
                for j in range(4):
                    ins = nc.tensor.transpose(PS[:, b, j * P:(j + 1) * P], KN[:, 4 * q + j, :], ident[:, :])
                ins.then_inc(s_full[b], 1)
            for q in range(4):
                evacuated(UNITS["keys"] + q)
            for tt in range(TT):
                for q in range(4):
                    b = free_bank(UNITS["peer_s"] + 4 * tt + q)
                    for j in range(4):
                        ins = nc.tensor.matmul(PS[:, b, j * P:(j + 1) * P], QT[:, 4 * q + j, tt * P:(tt + 1) * P],
                                               KTt[:, 4 * q + j, :], start=True, stop=True)
                    ins.then_inc(s_full[b], 1)
            def turn_u(j, i=0):
                b, use = j % 2, i + j // 2
                pe.wait_ge(s_ur[b], use * 16 + 16)
                for h in range(2):
                    if j or not isinstance(i, int):
                        pe.wait_ge(s_ul[1 - b], 2 * (i + (j - 1) // 2) + h + 1)
                    for q in range(4):
                        at_ = (4 * h + q) * P
                        ins = nc.tensor.transpose(PS[:, h, q * P:(q + 1) * P], UR[:, b, at_:at_ + P], ident[:, :])
                    ins.then_inc(s_ut[b], 1)

            def activations(j, i=0):
                b, use = j % 2, i + j // 2
                pe.wait_ge(s_ul[b], 2 * use + 2)
                if j >= 2 or not isinstance(i, int):
                    pe.wait_ge(s_ag, 2 * i + j - 1)
                for k in range(KT):
                    ins = mm3(PS[:, 2 + b, 0:S], UTH[:, b, k, :], UTL[:, b, k, :], HH[:, k, :], HL[:, k, :],
                              k == 0, k == KT - 1)
                ins.then_inc(s_ap, 1)

            def add_v(j, i=0):
                b = j % 2
                pe.wait_ge(s_as, 4 * i + j + 1)
                pe.wait_ge(s_vl, 4 * i + j + 1)
                for tt in range(TT):
                    tok = slice(tt * P, (tt + 1) * P)
                    for half in range(2):
                        at_ = slice(half * BANK, (half + 1) * BANK)
                        ins = mm3(acc(tt, half), AH[:, b, tok], AL[:, b, tok], VH[:, b, at_], VL[:, b, at_],
                                  isinstance(i, int) and j == 0, isinstance(i, int) and j == P - 1)
                    if isinstance(i, int) and j == P - 1 and tt == 0:
                        ins.then_inc(s_acc, 1)
                ins.then_inc(s_ao, 1)

            def beside(j):
                if j and j - 1 < len(PICKS) and PICKS[j - 1][0] == "gate":
                    tt = PICKS[j - 1][1]
                    pe.wait_ge(s_pk, tt + 1)
                    for q in range(3):
                        ins = nc.tensor.transpose(PS[:, 4 + tt, q * P:(q + 1) * P],
                                                  PK[:, q].rearrange("p h k -> p (h k)"), ident[:, :])
                    ins.then_inc(s_pt, 1)

            for q in range(8):
                evacuated(UNITS["peer_s"] + q)
            pe.wait_ge(s_accfree, 10)
            u_steps(pe, turn_u, activations, beside)
            pe.wait_ge(s_ag, P)
            with pe.Fori(0, S // 16) as i:
                for j in range(4):
                    b = free_bank(UNITS["gates"] + j, i, 4)
                    pe.wait_ge(s_oh, i * 4 + j + 1)
                    for x in range(4):
                        s = 4 * (j % 2) + x
                        ins = nc.tensor.matmul(PS[:, b, x * P:(x + 1) * P], ONE2[:, s, :], ONE1[:, s, :],
                                               start=True, stop=True)
                    ins.then_inc(s_full[b], 1)
            for q in range(4):
                evacuated(UNITS["gates"] + S // 4 - 4 + q)
            pe.wait_ge(s_hk, TT)
            v_steps(pe, lambda *a: None, add_v)
            pe.drain().then_inc(s_acc, 1)


_INS = ['x', 'ret_w_in', 'ret_w_out', 'lru_w_in', 'lru_conv_w', 'lru_conv_b', 'lru_gate_w', 'lru_gate_b',
        'lru_a_param', 'lru_w_out', 'norm_g', 'ffn_w_in', 'ffn_w_out', 'c_2', 'ctx_2', 'c_ctx_2', 'ada_w_2',
        'ada_b_2', 'norm1_g_2', 'norm2_g_2', 'w_in_2', 'rw_w0_2', 'rw_w_up_2', 'rw_a0_2', 'rw_a_up_2',
        'rw_g_up_2', 'rw_k_k_2', 'rw_k_a_2', 'rw_r_k_2', 'rw_lnx_g_2', 'na_rpb_2', 'sc_conv_w_2', 'w_out_2',
        'peer_q_w_2', 'peer_sub_keys_2', 'peer_u_2', 'peer_v_2', 'final_g_2']


def kernel(**inputs):
    import numpy as _np
    import concourse.bacc as _bacc
    from concourse import mybir as _mybir
    from concourse.bass_utils import run_bass_kernel_spmd as _run

    nc = _bacc.Bacc("TRN2", target_bir_lowering=False, num_devices=1,
                    dynamic_dma_scratch_size=8192)
    arrays, args = {}, {}
    for name in _INS:
        a = _np.ascontiguousarray(inputs[name])
        arrays[f"in_{name}_dram"] = a
        args[name] = nc.dram_tensor(f"in_{name}_dram", a.shape, _mybir.dt.from_np(a.dtype), kind="ExternalInput").ap()
    tables = _np.concatenate([_np.broadcast_to(CONST[n], (P, CONST[n].shape[1])) for n in CONST], axis=1)
    arrays["tables_dram"] = _np.ascontiguousarray(tables)
    consts = nc.dram_tensor("tables_dram", tables.shape, F32, kind="ExternalInput").ap()
    out = nc.dram_tensor("out_dram", (1, S, D), F32, kind="ExternalOutput").ap()
    mods = nc.dram_tensor("mods_dram", (2, 6 * D), F32, kind="Internal").ap()
    first_and_second_block(nc, args, consts, out, mods)
    r = _run(nc, [arrays], core_ids=[0])
    return r.results[0]["out_dram"]
```
